# Optimizing a Trainium2 kernel written in Bass

```python
import math
import jax, jax.numpy as jnp
from jax import lax
import numpy as np

D_MODEL = 1024
BATCH = 1
SEQ = 512
DEPTH = 1

N_META = 16
CHUNK = 64
PAD_FRONT = (-N_META) % CHUNK
CONV_W = 4
RMS_EPS = 1e-6
L2_EPS = 1e-6
LB_FLOOR = 1e-30

A_HEADS = 4
A_DK = 128
A_DV = 128
B_HEADS = 4
B_DK = 128
B_DV = 128
C_HEADS = 4
C_DK = 64
C_DV = 128
C_GK_RANK = 16
C_GK_NORM = 16.0

BRANCH_W = 512
N_BRANCH = 3

N_GROUPS = 4
EXP_PER_GROUP = 8
EXPERT_HIDDEN = 256
TOP_K = 2

IN_SPLITS = (
    A_HEADS * A_DK,
    A_HEADS * A_DK,
    A_HEADS * A_DV,
    A_HEADS * A_DV,
    B_HEADS * (2 * B_DK + B_DV),
    B_HEADS,
    B_HEADS,
    B_HEADS * B_DV,
    C_HEADS * C_DK,
    C_HEADS * C_DK,
    C_HEADS * C_DV,
    C_GK_RANK,
    C_HEADS * C_DV,
    N_BRANCH * D_MODEL,
)
IN_COLS = sum(IN_SPLITS)

kernel_name = "hybrid_hgrn2_gdn_gla_hmoe"

def _rmsnorm(x, w):
    xf = x.astype(jnp.float32)
    y = xf * lax.rsqrt(jnp.mean(xf * xf, axis=-1, keepdims=True) + RMS_EPS)
    return (y * w.astype(jnp.float32)).astype(x.dtype)

def _l2norm(x):
    return x * lax.rsqrt(jnp.sum(x * x, axis=-1, keepdims=True) + L2_EPS)

def _split_heads(x, n):
    b, l, c = x.shape
    return jnp.transpose(x.reshape(b, l, n, c // n), (0, 2, 1, 3))

def _to_chunks(x):
    b, h, l, d = x.shape
    return jnp.moveaxis(x.reshape(b, h, l // CHUNK, CHUNK, d), 2, 0)

def _from_chunks(x):
    n, b, h, c, d = x.shape
    return jnp.moveaxis(x, 0, 2).reshape(b, h, n * c, d)

def _masked_exp(diff, mask):
    return jnp.where(mask, jnp.exp(jnp.where(mask, diff, 0.0)), 0.0)

def _gated_head_norm(o, gate, w):
    b, h, l, dv = o.shape
    o = jnp.transpose(o, (0, 2, 1, 3))
    o = _rmsnorm(o, w) * jax.nn.silu(gate.reshape(b, l, h, dv))
    return o.reshape(b, l, h * dv)

def _causal_conv(x, w):
    return lax.conv_general_dilated(
        x, w[:, None, :].astype(x.dtype), window_strides=(1,), padding=((CONV_W - 1, 0),),
        dimension_numbers=("NWC", "WIO", "NWC"), feature_group_count=x.shape[-1])

def _chunk_gla(q, k, v, log_f):
    b_, h_, _, dk = q.shape
    dv = v.shape[-1]
    causal = jnp.tril(jnp.ones((CHUNK, CHUNK), dtype=bool))[:, :, None]

    def step(S, xs):
        qc, kc, vc, gc = xs
        bcum = jnp.cumsum(gc, axis=-2)
        b_last = bcum[..., -1:, :]
        pair = _masked_exp(bcum[..., :, None, :] - bcum[..., None, :, :], causal)
        scores = jnp.einsum('bhtsd,bhsd->bhts', qc[..., :, None, :] * pair, kc)
        o = (jnp.einsum('bhts,bhse->bhte', scores, vc)
             + jnp.einsum('bhtd,bhde->bhte', qc * jnp.exp(bcum), S))
        S = (jnp.exp(b_last[..., 0, :])[..., None] * S
             + jnp.einsum('bhsd,bhse->bhde', kc * jnp.exp(b_last - bcum), vc))
        return S, o

    S0 = jnp.zeros((b_, h_, dk, dv), q.dtype)
    _, o = lax.scan(step, S0, (_to_chunks(q), _to_chunks(k), _to_chunks(v), _to_chunks(log_f)))
    return _from_chunks(o)

def _chunk_gated_delta(q, k, v, log_a, beta):
    dvv = v.shape[-1]
    qc, kc, vc = _to_chunks(q), _to_chunks(k), _to_chunks(v)
    g = jnp.cumsum(_to_chunks(log_a[..., None])[..., 0], axis=-1)
    bc = _to_chunks(beta[..., None])[..., 0]
    causal = jnp.tril(jnp.ones((CHUNK, CHUNK), dtype=bool))
    strict = jnp.tril(jnp.ones((CHUNK, CHUNK), dtype=bool), -1)
    decay = _masked_exp(g[..., :, None] - g[..., None, :], causal)
    a_mat = jnp.where(strict, bc[..., :, None] * jnp.einsum('nbhtd,nbhsd->nbhts', kc, kc) * decay, 0.0)
    eye = jnp.eye(CHUNK, dtype=q.dtype)
    rhs = jnp.concatenate([vc * bc[..., None], kc * (bc * jnp.exp(g))[..., None]], axis=-1)
    sol = lax.linalg.triangular_solve(a_mat + eye, rhs, left_side=True, lower=True, unit_diagonal=True)
    u, w = sol[..., :dvv], sol[..., dvv:]
    qk = jnp.einsum('nbhtd,nbhsd->nbhts', qc, kc) * decay

    def step(S, xs):
        q_, k_, u_, w_, g_, qk_ = xs
        v_new = u_ - jnp.einsum('bhcd,bhde->bhce', w_, S)
        o = (jnp.einsum('bhcd,bhde->bhce', q_ * jnp.exp(g_)[..., None], S)
             + jnp.einsum('bhts,bhse->bhte', qk_, v_new))
        g_last = g_[..., -1:]
        S = (jnp.exp(g_last)[..., None] * S
             + jnp.einsum('bhsd,bhse->bhde', k_ * jnp.exp(g_last - g_)[..., None], v_new))
        return S, o

    S0 = jnp.zeros((q.shape[0], q.shape[1], q.shape[-1], dvv), q.dtype)
    _, o = lax.scan(step, S0, (qc, kc, u, w, g, qk))
    return _from_chunks(o)

def _hgrn2(q_in, f_in, i_in, g_in, lb, norm_w, valid):
    q = jax.nn.silu(q_in) * (A_DK ** -0.5)
    log_f = jnp.logaddexp(jnp.log(jnp.maximum(lb, LB_FLOOR)), jnp.log1p(-lb) + jax.nn.log_sigmoid(f_in))
    k = (1.0 - lb) * jax.nn.sigmoid(-f_in) * valid
    o = _chunk_gla(_split_heads(q, A_HEADS), _split_heads(k, A_HEADS),
                   _split_heads(i_in, A_HEADS), _split_heads(log_f, A_HEADS))
    return _gated_head_norm(o, g_in, norm_w)

def _gated_deltanet(qkv_in, beta_in, decay_in, g_in, conv_w, a_log, dt_bias, norm_w, valid):
    qkv = jax.nn.silu(_causal_conv(qkv_in, conv_w))
    q, k, v = jnp.split(qkv, [B_HEADS * B_DK, 2 * B_HEADS * B_DK], axis=-1)
    q = _l2norm(_split_heads(q, B_HEADS)) * (B_DK ** -0.5)
    k = _l2norm(_split_heads(k * valid, B_HEADS))
    v = _split_heads(v, B_HEADS)
    beta = jnp.transpose(jax.nn.sigmoid(beta_in) * valid, (0, 2, 1))
    log_a = jnp.transpose(-jnp.exp(a_log) * jax.nn.softplus(decay_in + dt_bias), (0, 2, 1))
    o = _chunk_gated_delta(q, k, v, log_a, beta)
    return _gated_head_norm(o, g_in, norm_w)

def _gla(q_in, k_in, v_in, gk_low, g_in, gk_w2, gk_b, norm_w, valid):
    q = _split_heads(q_in, C_HEADS) * (C_DK ** -0.5)
    k = _split_heads(k_in * valid, C_HEADS)
    v = _split_heads(v_in, C_HEADS)
    log_f = _split_heads(jax.nn.log_sigmoid(gk_low @ gk_w2 + gk_b) / C_GK_NORM, C_HEADS)
    o = _chunk_gla(q, k, v, log_f)
    return _gated_head_norm(o, g_in, norm_w)

def _hier_moe(x, wg, bg, we, be, w_gate, w_up, w_down):
    xf = x.astype(jnp.float32)
    b, l, _ = xf.shape
    p_group = jax.nn.softmax(xf @ wg + bg, axis=-1)
    g_val, g_idx = lax.top_k(p_group, 1)
    e_logits = (xf @ we + be).reshape(b, l, N_GROUPS, EXP_PER_GROUP)
    e_logits = jnp.take_along_axis(e_logits, g_idx[..., None], axis=2)[:, :, 0, :]
    p_exp = jax.nn.softmax(e_logits, axis=-1)
    e_val, e_idx = lax.top_k(p_exp, TOP_K)
    e_w = e_val / jnp.sum(e_val, axis=-1, keepdims=True)
    within = jnp.einsum('blk,blke->ble', e_w, jax.nn.one_hot(e_idx, EXP_PER_GROUP, dtype=jnp.float32))
    combine = (jax.nn.one_hot(g_idx[..., 0], N_GROUPS, dtype=jnp.float32)[..., None]
               * (g_val * within)[:, :, None, :])
    y = jnp.zeros_like(xf)
    for grp in range(N_GROUPS):
        hid = (jax.nn.silu(jnp.einsum('bld,edh->bleh', xf, w_gate[grp]))
               * jnp.einsum('bld,edh->bleh', xf, w_up[grp]))
        y = y + jnp.einsum('bleh,ble,ehd->bld', hid, combine[:, :, grp], w_down[grp])
    return y

def setup_inputs(seed: int = 0) -> dict:
    key = jax.random.key(seed)
    ks = jax.random.split(key, 24)
    f32 = jnp.float32

    def nrm(k, shape, scale):
        return jax.random.normal(k, shape, f32) * scale

    dt = jnp.exp(jax.random.uniform(ks[8], (DEPTH, B_HEADS), f32, math.log(1e-3), math.log(1e-1)))
    return {
        "x": nrm(ks[0], (BATCH, SEQ, D_MODEL), 1.0),
        "meta_tokens": nrm(ks[1], (N_META, D_MODEL), 1.0),
        "norm_mix": 1.0 + nrm(ks[2], (DEPTH, D_MODEL), 0.02),
        "w_in": nrm(ks[3], (DEPTH, D_MODEL, IN_COLS), D_MODEL ** -0.5),
        "hgrn_lb_logits": nrm(ks[4], (DEPTH, A_HEADS * A_DK), 0.5),
        "hgrn_norm": 1.0 + nrm(ks[5], (DEPTH, A_DV), 0.02),
        "gdn_conv": nrm(ks[6], (DEPTH, CONV_W, B_HEADS * (2 * B_DK + B_DV)), CONV_W ** -0.5),
        "gdn_a_log": jnp.log(jax.random.uniform(ks[7], (DEPTH, B_HEADS), f32, 1.0, 16.0)),
        "gdn_dt_bias": dt + jnp.log(-jnp.expm1(-dt)),
        "gdn_norm": 1.0 + nrm(ks[9], (DEPTH, B_DV), 0.02),
        "gla_gk_w2": nrm(ks[10], (DEPTH, C_GK_RANK, C_HEADS * C_DK), C_GK_RANK ** -0.5),
        "gla_gk_b": nrm(ks[11], (DEPTH, C_HEADS * C_DK), 0.1),
        "gla_norm": 1.0 + nrm(ks[12], (DEPTH, C_DV), 0.02),
        "w_branch": nrm(ks[13], (DEPTH, N_BRANCH, BRANCH_W, D_MODEL), BRANCH_W ** -0.5),
        "w_out": nrm(ks[14], (DEPTH, D_MODEL, D_MODEL), D_MODEL ** -0.5),
        "norm_ffn": 1.0 + nrm(ks[15], (DEPTH, D_MODEL), 0.02),
        "router_group_w": nrm(ks[16], (DEPTH, D_MODEL, N_GROUPS), D_MODEL ** -0.5),
        "router_group_b": nrm(ks[17], (DEPTH, N_GROUPS), 0.01),
        "router_expert_w": nrm(ks[18], (DEPTH, D_MODEL, N_GROUPS * EXP_PER_GROUP), D_MODEL ** -0.5),
        "router_expert_b": nrm(ks[19], (DEPTH, N_GROUPS * EXP_PER_GROUP), 0.01),
        "expert_w_gate": nrm(ks[20], (DEPTH, N_GROUPS, EXP_PER_GROUP, D_MODEL, EXPERT_HIDDEN), D_MODEL ** -0.5),
        "expert_w_up": nrm(ks[21], (DEPTH, N_GROUPS, EXP_PER_GROUP, D_MODEL, EXPERT_HIDDEN), D_MODEL ** -0.5),
        "expert_w_down": nrm(ks[22], (DEPTH, N_GROUPS, EXP_PER_GROUP, EXPERT_HIDDEN, D_MODEL), EXPERT_HIDDEN ** -0.5),
        "norm_final": 1.0 + nrm(ks[23], (D_MODEL,), 0.02),
    }

def reference(x, meta_tokens, norm_mix, w_in, hgrn_lb_logits, hgrn_norm, gdn_conv, gdn_a_log,
              gdn_dt_bias, gdn_norm, gla_gk_w2, gla_gk_b, gla_norm, w_branch, w_out, norm_ffn,
              router_group_w, router_group_b, router_expert_w, router_expert_b,
              expert_w_gate, expert_w_up, expert_w_down, norm_final):
    b, s, d = x.shape
    dtype = x.dtype
    total = PAD_FRONT + N_META + s
    pad = jnp.zeros((b, PAD_FRONT, d), dtype)
    meta = jnp.broadcast_to(meta_tokens.astype(dtype)[None], (b, N_META, d))
    h = jnp.concatenate([pad, meta, x], axis=1)
    valid = (jnp.arange(total) >= PAD_FRONT).astype(jnp.float32)[None, :, None]

    lb_p = jax.nn.softmax(hgrn_lb_logits.astype(jnp.float32), axis=0)
    lb_all = jnp.maximum(jnp.cumsum(lb_p, axis=0) - lb_p[0:1], 0.0)

    split_points = np.cumsum(IN_SPLITS)[:-1].tolist()
    for layer in range(DEPTH):
        u = _rmsnorm(h, norm_mix[layer]).astype(jnp.float32) * valid
        (a_q, a_f, a_i, a_g, b_qkv, b_beta, b_decay, b_g,
         c_q, c_k, c_v, c_gk, c_g, gate_logits) = jnp.split(u @ w_in[layer], split_points, axis=-1)
        y_a = _hgrn2(a_q, a_f, a_i, a_g, lb_all[layer], hgrn_norm[layer], valid)
        y_b = _gated_deltanet(b_qkv, b_beta, b_decay, b_g, gdn_conv[layer], gdn_a_log[layer],
                              gdn_dt_bias[layer], gdn_norm[layer], valid)
        y_c = _gla(c_q, c_k, c_v, c_gk, c_g, gla_gk_w2[layer], gla_gk_b[layer], gla_norm[layer], valid)
        ys = jnp.stack([y_a, y_b, y_c], axis=2)
        gates = jax.nn.sigmoid(gate_logits.reshape(b, total, N_BRANCH, d))
        proj = jnp.einsum('blne,ned->blnd', ys, w_branch[layer])
        merged = jnp.sum(gates * proj, axis=2)
        h = h + (merged @ w_out[layer]).astype(dtype)
        u2 = _rmsnorm(h, norm_ffn[layer])
        h = h + _hier_moe(u2, router_group_w[layer], router_group_b[layer], router_expert_w[layer],
                          router_expert_b[layer], expert_w_gate[layer], expert_w_up[layer],
                          expert_w_down[layer]).astype(dtype)

    out = _rmsnorm(h, norm_final)
    return out[:, PAD_FRONT + N_META:, :]


_drawn_inputs = setup_inputs


def setup_inputs(seed=0):
    import zlib

    import numpy as np

    out = dict(_drawn_inputs(seed))
    spreads = {}
    factors = {'hgrn_norm': 9.957,
     'gdn_norm': 12.31,
     'gla_norm': 12.33,
     'router_group_b': 19.59,
     'router_expert_b': 12.822,
     'norm_final': 8.455,
     'norm_ffn': 3.891}
    for name, (base, spread) in spreads.items():
        noise = np.random.default_rng([zlib.crc32(name.encode()), seed]).standard_normal(out[name].shape)
        drawn = base * np.exp(spread * noise) if base else spread * noise
        out[name] = __import__('jax').numpy.asarray(drawn.astype(out[name].dtype))
    for name, factor in factors.items():
        out[name] = (out[name] * factor).astype(out[name].dtype)
    return out
```

```python
import numpy as np
import concourse.bass as bass
from concourse import mybir
from contextlib import ExitStack

F32 = mybir.dt.float32
I32 = mybir.dt.int32
ALU = mybir.AluOpType
ACT = mybir.ActivationFunctionType
AX = mybir.AxisListType

P = 128
D = 1024
KD = D // P
SEQ, META = 512, 16
TOK = META + SEQ
NT = SEQ // P
LEVELS = 7
PADTOK = P + SEQ
NTP = NT + 1
NB, BW = 3, 512
NG, NE, HID = 4, 8, 256
NX = NG * NE
SLOTS = 64
EXTRA = 2 * SEQ // SLOTS
ROWS = (NX + EXTRA) * SLOTS
EPS = 1e-6
LN2 = float(np.log(2.0))

A_Q, A_F, A_I, A_G = 0, 512, 1024, 1536
B_QKV, B_BETA, B_DECAY, B_G = 2048, 3584, 3588, 3592
C_Q, C_K, C_V, C_GK, C_G = 4104, 4360, 4616, 5128, 5144
GATES = 5656

R_NORM, R_LB, R_AN, R_BN, R_CN, R_CONV, R_GKB = 0, 8, 12, 13, 14, 15, 63
NROWS = 65

K_ID, K_INC, K_STR, K_UP, K_LOW = 0, P, 2 * P, 3 * P, (3 + LEVELS) * P
K_RESET = (3 + 2 * LEVELS) * P
K_E64 = K_RESET + TOK
K_DESC = K_E64 + NX
K_J = K_DESC + NE
KCOLS = K_J + 16


def constants():
    c = np.zeros((P, KCOLS), np.float32)
    s, t = np.arange(P)[:, None], np.arange(P)[None, :]
    c[:, K_ID:K_ID + P] = s == t
    c[:, K_INC:K_INC + P] = s <= t
    c[:, K_STR:K_STR + P] = s < t
    for l in range(LEVELS):
        up = ((s ^ t) >> l == 1) & (s < t)
        c[:, K_UP + l * P:K_UP + (l + 1) * P] = up
        c[:, K_LOW + l * P:K_LOW + (l + 1) * P] = up.T
    n = np.arange(TOK)
    c[:, K_RESET:K_RESET + TOK] = ~((n == 0) | ((n >= META) & ((n - META) % P == 0)))
    c[:, K_E64:K_E64 + NX] = np.arange(NX) * SLOTS
    c[:, K_DESC:K_DESC + NE] = NE - np.arange(NE)
    c[:, K_J:K_J + 16] = np.arange(16)
    return c


class Steps:

    def __init__(self, sem, names, base=0):
        self.sem, self.names, self.at, self.base = sem, names, 0, base
        self.index = {n: k + 1 for k, n in enumerate(names)}
        assert len(self.index) == len(names)

    def after(self, name, i=0):
        return self.sem, i * len(self.names) + (self.base + self.index[name])

    def rounds(self, i):
        return self.sem, i * len(self.names) + self.base

    def begin(self, engine):
        engine.nop().then_inc(self.sem, self.base)

    def did(self, name):
        assert self.names[self.at % len(self.names)] == name, (name, self.names[self.at % len(self.names)])
        self.at += 1
        return self.sem, 1


def gla_names(kind):
    nh = 1 if kind == "a" else 2
    sub = range(nh)
    lv = range(LEVELS)
    if kind == "a":
        pe = ["f", "q", "g0", "v"]
        act = ["sgk", "sgq", "sgg0", "v0", "vm", "ab", "e", "l", "ad", "e2", "l2"]
        dve = ["f", "k", "q", "g0", "ls", "dif", "mx", "lf", "b"]
    else:
        pe = ["k", "f", "q", "g0", "g1", "v"]
        act = ["sgg0", "sgg1", "v0", "v1", "vm", "ab", "e", "l"]
        dve = ["k", "f", "q", "g0", "g1", "ls", "lf", "b"]
    ngate = 2 * nh
    pe += [f"gd{s}" for s in sub]
    gate_at = {}
    for l in lv:
        pe += [f"gr{l}_{s}" for s in sub]
        if l == 0:
            pe += ["keT"]
        if l == 1:
            pe += ["kv"]
    pe += [f"o{s}" for s in sub] + [f"ss{s}" for s in sub]
    act += ["eb", "dec", "eke", "keTm", "keTr"]
    for l in lv:
        act += [f"xa{l}", f"xb{l}"]
    act += [f"sq{s}" for s in sub] + [x for s in sub for x in (f"ln{s}", f"ri{s}")]
    dve += ["dbm", "dbr", "d0", "qe", "ke"] + [f"Pd{s}" for s in sub]
    for l in lv:
        if l + 1 < LEVELS:
            dve += [f"d{l + 1}"]
        dve += [f"za{l}", f"zb{l}"]
        if l == 2:
            dve += ["S0", "S1", "S2", "S3"]
        if l:
            dve += [f"P{l - 1}_{s}" for s in sub]
    dve += [f"P{LEVELS - 1}_{s}" for s in sub]
    dve += [x for s in sub for x in (f"y1{s}", f"y{s}")]
    return nh, pe, act, dve


def hybrid_trunk(nc, x, meta_tokens, norm_mix, w_in, hgrn_lb_logits, hgrn_norm, gdn_conv, gdn_a_log,
                 gdn_dt_bias, gdn_norm, gla_gk_w2, gla_gk_b, gla_norm, w_branch, w_out, norm_ffn,
                 router_group_w, router_group_b, router_expert_w, router_expert_b,
                 expert_w_gate, expert_w_up, expert_w_down, norm_final, consts, out, dbg=None, stop=None):
    ctx = ExitStack()
    with ctx:
        def sb(name, shape, dt=F32):
            return ctx.enter_context(nc.sbuf_tensor(name, shape, dt))

        sems = {}

        def sem(name):
            if name not in sems:
                sems[name] = ctx.enter_context(nc.semaphore(name))
            return sems[name]

        C = sb("C", [P, KCOLS])
        ident, inc, strict = C[:, K_ID:K_ID + P], C[:, K_INC:K_INC + P], C[:, K_STR:K_STR + P]
        reset = C[:, K_RESET:K_RESET + TOK]

        def up(l):
            return C[:, K_UP + l * P:K_UP + (l + 1) * P]

        def low(l):
            return C[:, K_LOW + l * P:K_LOW + (l + 1) * P]

        ones = sb("ones", [P, P])
        spare = sb("spare", [P, 24])
        spare_at = [0]

        def next_spare():
            spare_at[0] = (spare_at[0] + 1) % 24
            return spare[:, spare_at[0]:spare_at[0] + 1]
        col = sb("col", [P, 16])
        one_c, eps_c, zero_c = col[:, 0:1], col[:, 1:2], col[:, 2:3]
        rowsT = sb("rowsT", [P, NROWS])
        gates = sb("gates", [P, NB * KD, SEQ])
        yT = sb("yT", [P, NB * BW // P, SEQ])
        ARENA = 29500
        arena = sb("arena", [P, ARENA])
        uT = arena[:, 0:KD * TOK].rearrange("p (k t) -> p k t", k=KD)
        o = KD * TOK
        wseg = arena[:, o:o + 6 * KD * P].rearrange("p (s k c) -> p s k c", s=6, k=KD)
        o += 6 * KD * P
        wgt = arena[:, o:o + 4 * KD * P].rearrange("p (s k c) -> p s k c", s=4, k=KD)
        o += 4 * KD * P
        WORK = o

        class Area:

            def __init__(self, at, end=ARENA):
                self.at, self.end = at, end

            def take(self, n):
                self.at += n
                assert self.at <= self.end, (self.at, self.end)
                return arena[:, self.at - n:self.at]

        ps = ctx.enter_context(nc.psum_tensor("ps", [P, 8 * 512], F32))

        def bank(n, w=512):
            return ps[:, n * 512:n * 512 + w]

        def slot(n):
            return ps[:, n * 1024 + 496:n * 1024 + 1024]

        def over(ap, n):
            return ap.unsqueeze(1).broadcast_to([ap.shape[0], n, ap.shape[1]])

        def tiles(ap, n=NT):
            return ap.rearrange("p (n t) -> p n t", n=n)

        xs_dram = nc.dram_tensor("sorted_tokens", [ROWS, D], F32).ap()
        ys_dram = nc.dram_tensor("sorted_results", [ROWS, D], F32).ap()

        block = ctx.enter_context(nc.Block())
        programs = {e: [] for e in ("sync", "scalar", "vector", "tensor", "gpsimd")}

        w0 = Area(WORK)
        xt = gates[:, 0:2 * NT, :].rearrange("p (i a) t -> p i (a t)", a=2)
        xm = gates[0:META, 8:10, :].rearrange("p a t -> p (a t)")
        rowsb = gates[0:NROWS, 10, 0:P]
        scr = gates[:, 12:14, :].rearrange("p a t -> p (a t)")
        zeros = gates[:, 14:22, :].rearrange("p a t -> p (a t)")
        ssq = col[:, 3:8]
        small_w = w0.take(KD * 24).rearrange("p (k c) -> p k c", k=KD)
        gkw2 = sb("gkw2", [16, 2 * P])
        lbc = sb("lbc", [P, 16])
        bcol = sb("bcol", [P, 10 * 4 * NTP])
        gkT = sb("gkT", [16, TOK])

        pe0 = Steps(sem("setup_pe"), ["rows", "alb"] + [f"u{k}" for k in range(KD)] + ["small", "gkT", "gcol"])
        act0 = Steps(sem("setup_act"), ["ln", "rs", "lb1", "lb2", "am", "sgm", "ab", "e", "l", "ea", "gk", "eg", "egl", "ekd"])
        dve0 = Steps(sem("setup_dve"), ["ones", "c1", "c2", "c3", "zero", "rows"] +
                     [f"sq{i}" for i in range(5)] + ["ms"] + [f"ut{i}" for i in range(5)] +
                     [f"u{k}" for k in range(KD)] +
                     ["lbm", "lbs", "lb", "om", "lbf", "lnf", "pad", "sm", "smm", "dt", "beta", "sp", "nea", "la0", "gkm", "g", "gl", "bg", "dk"])

        def setup_sync(sp):
            sp.dma_start(xt, x[0].rearrange("(i p) d -> p i d", p=P)).then_inc(sem("x_loaded"), 16)
            sp.dma_start(xm, meta_tokens).then_inc(sem("x_loaded"), 16)
            sp.dma_start(C[:, :], consts).then_inc(sem("consts_loaded"), 16)
            for at, src in ((R_NORM, norm_mix[0].rearrange("(a b) -> a b", b=P)),
                            (R_LB, hgrn_lb_logits[0].rearrange("(a b) -> a b", b=P)),
                            (R_AN, hgrn_norm), (R_BN, gdn_norm), (R_CN, gla_norm),
                            (R_CONV, gdn_conv[0].rearrange("j (c b) -> (j c) b", b=P)),
                            (R_GKB, gla_gk_b[0].rearrange("(a b) -> a b", b=P))):
                sp.dma_start(rowsb[at:at + src.shape[0], :], src).then_inc(sem("rows_loaded"), 16)
            wv = w_in[0].rearrange("(k p) c -> p k c", p=P)
            sp.dma_start(small_w[:, :, 0:8], wv[:, :, B_BETA:B_BETA + 8]).then_inc(sem("small_loaded"), 16)
            sp.dma_start(small_w[:, :, 8:24], wv[:, :, C_GK:C_GK + 16]).then_inc(sem("small_loaded"), 16)
            sp.dma_start(gkw2[:, :], gla_gk_w2[0]).then_inc(sem("small_loaded"), 16)
            sp.dma_start(bcol[:, 0:4], gdn_a_log.partition_broadcast(P) if False else gdn_a_log[0:1, :].broadcast_to([P, 4])).then_inc(sem("small_loaded"), 16)
            sp.dma_start(bcol[:, 4:8], gdn_dt_bias[0:1, :].broadcast_to([P, 4])).then_inc(sem("small_loaded"), 16)

        def bq(n):
            return bcol[:, 8 + n * 20:8 + (n + 1) * 20]
        q_dec, q_beta, q_la, q_g, q_gl, q_eg, q_bg, q_egl = (bq(n) for n in range(8))
        q_kd = bq(8)

        def setup_vector(v):
            v.memset(ones[:, :], 1.0).then_inc(*dve0.did("ones"))
            v.memset(one_c, 1.0).then_inc(*dve0.did("c1"))
            v.memset(eps_c, EPS).then_inc(*dve0.did("c2"))
            v.memset(ssq, 1.0).then_inc(*dve0.did("c3"))
            v.memset(zeros, 0.0).then_inc(*dve0.did("zero"))
            v.wait_ge(*pe0.after("rows"))
            v.tensor_copy(rowsT[:, :], bank(0, NROWS)).then_inc(*dve0.did("rows"))
            v.wait_ge(sem("x_loaded"), 32)
            v.wait_ge(*dve0.after("zero"))
            for i in range(5):
                src = xt[:, i, :] if i < NT else xm
                r = src.shape[0]
                if i:
                    v.wait_ge(*dve0.after(f"sq{i - 1}"))
                v.tensor_tensor_reduce(scr[0:r], src, src, 1.0, 0.0, ALU.mult, ALU.add,
                                       accum_out=ssq[0:r, i:i + 1]).then_inc(*dve0.did(f"sq{i}"))
            v.wait_ge(*dve0.after("sq4"))
            v.tensor_scalar(ssq, ssq, 1.0 / D, EPS, ALU.mult, ALU.add).then_inc(*dve0.did("ms"))
            v.wait_ge(*act0.after("rs"))
            for i in range(5):
                src = xt[:, i, :] if i < NT else xm
                r = src.shape[0]
                v.tensor_scalar(src, src, ssq[0:r, i:i + 1], None, ALU.mult).then_inc(*dve0.did(f"ut{i}"))
            v.wait_ge(*dve0.after("rows"))
            for k in range(KD):
                v.wait_ge(*pe0.after(f"u{k}"))
                v.tensor_scalar(uT[:, k, :], slot(k % 2), rowsT[:, R_NORM + k:R_NORM + k + 1], None,
                                ALU.mult).then_inc(*dve0.did(f"u{k}"))
            lg = rowsT[:, R_LB:R_LB + 4]
            v.tensor_tensor(lbc[:, 0:4], lg, lg, ALU.subtract).then_inc(*dve0.did("lbm"))
            v.wait_ge(*act0.after("lb1"))
            v.reciprocal(lbc[:, 8:12], lbc[:, 4:8]).then_inc(*dve0.did("lbs"))
            v.wait_ge(*dve0.after("lbs"))
            v.tensor_tensor(lbc[:, 4:8], lbc[:, 4:8], lbc[:, 8:12], ALU.mult).then_inc(*dve0.did("lb"))
            v.wait_ge(*dve0.after("lb"))
            v.tensor_tensor(lbc[:, 8:12], lbc[:, 4:8], lbc[:, 4:8], ALU.subtract).then_inc(*dve0.did("om"))
            v.wait_ge(*dve0.after("om"))
            v.tensor_scalar(lbc[:, 0:4], lbc[:, 8:12], -1.0, 1.0, ALU.mult, ALU.add).then_inc(*dve0.did("lbf"))
            v.tensor_scalar(lbc[:, 8:12], lbc[:, 8:12], 1e-30, 2.0 ** 50, ALU.max, ALU.mult).then_inc(*dve0.did("lnf"))
            v.memset(bcol[:, 8:], 0.0).then_inc(*dve0.did("pad"))
            v.wait_ge(*pe0.after("small"))
            v.wait_ge(*dve0.after("pad"))
            v.wait_ge(sem("valid_set"), 4)
            bt = bank(4, NT * 24).rearrange("p (t c) -> p t c", t=NT)
            bm = bank(5, 24)[0:META]
            v.tensor_copy(small_t[:, 1:, :], bt).then_inc(*dve0.did("sm"))
            v.tensor_copy(small_t[0:META, 0, :], bm).then_inc(*dve0.did("smm"))
            v.wait_ge(sem("small_loaded"), 80)
            v.wait_ge(*dve0.after("smm"))
            dec5 = q_dec.rearrange("p (t h) -> p t h", t=NTP)
            v.tensor_tensor(dec5, small_t[:, :, 4:8], over(bcol[:, 4:8], NTP), ALU.add).then_inc(*dve0.did("dt"))
            v.wait_ge(*act0.after("sgm"))
            v.wait_ge(*dve0.after("pad"))
            b5 = q_beta.rearrange("p (t h) -> p t h", t=NTP)
            sg5 = q_eg.rearrange("p (t h) -> p t h", t=NTP)
            v.tensor_copy(b5, sg5).then_inc(*dve0.did("beta"))
            v.wait_ge(*act0.after("l"))
            v.scalar_tensor_tensor(q_dec, q_dec, 0.0, q_la, ALU.max, ALU.add).then_inc(*dve0.did("sp"))
            v.wait_ge(*act0.after("ea"))
            v.wait_ge(*dve0.after("sp"))
            v.scalar_tensor_tensor(dec5, dec5, -1.0, over(bcol[:, 0:4], NTP), ALU.mult, ALU.mult).then_inc(*dve0.did("nea"))
            v.wait_ge(*dve0.after("nea"))
            v.tensor_tensor(q_la, q_dec, valid[:, :], ALU.mult).then_inc(*dve0.did("la0"))
            v.wait_ge(*dve0.after("beta"))
            v.tensor_tensor(q_beta, q_beta, valid[:, :], ALU.mult).then_inc(*dve0.did("gkm"))
            v.wait_ge(*pe0.after("gcol"))
            v.tensor_copy(q_g, bank(6, 20)).then_inc(*dve0.did("g"))
            v.tensor_copy(q_gl, bank(7, 20)).then_inc(*dve0.did("gl"))
            v.wait_ge(*act0.after("egl"))
            v.wait_ge(*dve0.after("gl"))
            v.tensor_tensor(q_bg, q_beta, q_eg, ALU.mult).then_inc(*dve0.did("bg"))
            v.tensor_tensor(q_kd, q_gl, q_g, ALU.subtract).then_inc(*dve0.did("dk"))

        small_t = sb("small_t", [P, NTP, 24])
        valid = sb("valid", [P, 20])

        def setup_gpsimd(g):
            g.memset(valid[:, :], 1.0).then_inc(sem("valid_set"), 1)
            g.memset(small_t[:, 0, :], 0.0).then_inc(sem("valid_set"), 1)
            g.wait_ge(sem("valid_set"), 1)
            g.memset(valid[:, 0:4], 0.0).then_inc(sem("valid_set"), 1)
            g.wait_ge(sem("valid_set"), 3)
            g.memset(valid[0:META, 0:4], 1.0).then_inc(sem("valid_set"), 1)
            g.wait_ge(*dve0.after("zero"))
            n = ROWS * D // P // 4096
            xz = xs_dram.rearrange("(p r) d -> p (r d)", p=P)
            for c in range(0, ROWS * D // P, 4096):
                w = min(4096, ROWS * D // P - c)
                g.dma_start(xz[:, c:c + w], zeros[:, 0:w]).then_inc(sem("rows_zeroed"), 16)
            yz = ys_dram[NX * SLOTS:, :].rearrange("(p r) d -> p (r d)", p=P)
            for c in range(0, EXTRA * SLOTS * D // P, 4096):
                g.dma_start(yz[:, c:c + 4096], zeros[:, 0:4096]).then_inc(sem("rows_zeroed"), 16)
        n_zero = -(-(ROWS * D // P) // 4096) + EXTRA * SLOTS * D // P // 4096

        def setup_scalar(a):
            a.wait_ge(*dve0.after("ms"))
            a.activation(ssq, ssq, ACT.Ln).then_inc(*act0.did("ln"))
            a.wait_ge(*act0.after("ln"))
            a.activation(ssq, ssq, ACT.Exp, scale=-0.5).then_inc(*act0.did("rs"))
            a.wait_ge(*dve0.after("lbm"))
            a.activation(lbc[:, 4:8], lbc[:, 0:4], ACT.Exp).then_inc(*act0.did("lb1"))
            a.wait_ge(*dve0.after("lnf"))
            a.activation(lbc[:, 4:12], lbc_src, ACT.Ln).then_inc(*act0.did("lb2")) if False else \
                a.activation(lbc[:, 8:12], lbc[:, 8:12], ACT.Ln).then_inc(*act0.did("lb2"))
            a.activation(lbc[:, 4:8], lbc[:, 0:4], ACT.Ln).then_inc(*act0.did("am"))
            a.wait_ge(*dve0.after("smm"))
            a.wait_ge(sem("valid_set"), 4)
            a.activation(q_eg.rearrange("p (t h) -> p t h", t=NTP), small_t[:, :, 0:4], ACT.Sigmoid).then_inc(*act0.did("sgm"))
            a.wait_ge(*dve0.after("dt"))
            a.activation(q_la, q_dec, ACT.Abs).then_inc(*act0.did("ab"))
            a.wait_ge(*act0.after("ab"))
            a.activation(q_la, q_la, ACT.Exp, scale=-1.0).then_inc(*act0.did("e"))
            a.wait_ge(*act0.after("e"))
            a.activation(q_la, q_la, ACT.Ln, bias=one_c).then_inc(*act0.did("l"))
            a.activation(bcol[:, 0:4], bcol[:, 0:4], ACT.Exp).then_inc(*act0.did("ea"))
            a.wait_ge(*pe0.after("gkT"))
            a.activation(gkT[:, :], slot(1)[0:16], ACT.Copy).then_inc(*act0.did("gk"))
            a.wait_ge(*dve0.after("gl"))
            a.activation(q_eg, q_g, ACT.Exp).then_inc(*act0.did("eg"))
            a.activation(q_egl, q_gl, ACT.Exp).then_inc(*act0.did("egl"))
            a.wait_ge(*dve0.after("dk"))
            a.activation(q_kd, q_kd, ACT.Exp).then_inc(*act0.did("ekd"))

        def setup_tensor(t):
            t.wait_ge(sem("consts_loaded"), 16)
            t.wait_ge(sem("rows_loaded"), 16 * 7)
            t.transpose(bank(0, NROWS), rowsb, ident[0:NROWS, 0:NROWS]).then_inc(*pe0.did("rows"))
            t.wait_ge(*dve0.after("ut4"))
            t.wait_ge(*dve0.after("rows"))
            t.nop().then_inc(*pe0.did("alb"))
            for k in range(KD):
                if k >= 2:
                    t.wait_ge(*dve0.after(f"u{k - 2}"))
                s = slot(k % 2)
                t.transpose(s[:, 0:META], xm[:, k * P:(k + 1) * P], ident[0:META, 0:META])
                for i in range(NT):
                    mm = t.transpose(s[:, META + i * P:META + (i + 1) * P], xt[:, i, k * P:(k + 1) * P], ident)
                mm.then_inc(*pe0.did(f"u{k}"))
            t.wait_ge(*dve0.after(f"u{KD - 1}"))
            t.wait_ge(sem("small_loaded"), 80)
            for i in range(NTP):
                dst = bank(5, 24)[0:META] if i == 0 else ps[:, 4 * 512 + (i - 1) * 24:4 * 512 + i * 24]
                lo = 0 if i == 0 else META + (i - 1) * P
                w = META if i == 0 else P
                for k in range(KD):
                    mm = t.matmul(dst, uT[:, k, lo:lo + w], small_w[:, k, :], start=(k == 0), stop=(k == KD - 1))
            mm.then_inc(*pe0.did("small"))
            t.wait_ge(*dve0.after("smm"))
            s = slot(1)
            t.transpose(s[0:16, 0:META], small_t[0:META, 0, 8:24], ident[0:META, 0:META])
            for i in range(NT):
                mm = t.transpose(s[0:16, META + i * P:META + (i + 1) * P], small_t[:, i + 1, 8:24], ident)
            mm.then_inc(*pe0.did("gkT"))
            t.wait_ge(*dve0.after("gkm"))
            t.wait_ge(*dve0.after("ones"))
            t.matmul(bank(6, 20), inc, q_la, start=True, stop=True)
            t.matmul(bank(7, 20), ones[:, :], q_la, start=True, stop=True).then_inc(*pe0.did("gcol"))
            t.wait_ge(*act0.after("gk"))
            t.wait_ge(*dve0.after("gl"))

        for e, f in (("sync", setup_sync), ("scalar", setup_scalar), ("vector", setup_vector),
                     ("tensor", setup_tensor), ("gpsimd", setup_gpsimd)):
            programs[e].append(f)

        wv = w_in[0].rearrange("(k p) c -> p k c", p=P)

        def gla(kind, rounds, first_y, first_gate, earlier):
            nh, pe_n, act_n, dve_n = gla_names(kind)
            pe, act, dve = (Steps(sem(f"{kind}_{e}"), n, 1) for e, n in (("pe", pe_n), ("act", act_n), ("dve", dve_n)))
            segs = ["f", "q", "g0", "v"] if kind == "a" else ["k", "q", "g0", "g1", "v"]
            ngate = 2 * nh
            gate_pe = Steps(sem(f"{kind}_gate_pe"), [f"t{n}" for n in range(ngate)], 1)
            gate_ev = Steps(sem(f"{kind}_gate_evac"), [f"t{n}" for n in range(ngate)], 1)
            w = Area(WORK)
            fb, k_, b_, lf, tmp, eke = (w.take(TOK) for _ in range(6))
            q_, eb, qe = (w.take(SEQ) for _ in range(3))
            g_ = [w.take(SEQ) for _ in range(nh)]
            db = w.take(TOK)
            sg = w.take(SEQ)
            dd = [w.take(SEQ) for _ in range(2)]
            ee = [w.take(SEQ) for _ in range(2)]
            zz = [w.take(SEQ) for _ in range(2)]
            pm = [w.take(SEQ) for _ in range(nh)]
            vt = [w.take(SEQ) for _ in range(nh)]
            vm = w.take(nh * P)[0:META]
            kt = tiles(w.take(NT * P))
            st = tiles(w.take(NT * P))
            dec = w.take(NT)
            sq, ri = eb, sg
            offs = {"a": {"f": (A_F, P), "q": (A_Q, P), "g0": (A_G, P), "v": (A_I, P)},
                    "c": {"k": (C_K, P), "q": (C_Q, P), "g0": (C_G, 2 * P), "g1": (C_G + P, 2 * P),
                          "v": (C_V, 2 * P)}}[kind]
            wi = {s: n for n, s in enumerate(segs)}
            KH = P // nh

            def sync(sp):
                def load(seg, i):
                    at, step = offs[seg]
                    n = nh if seg == "v" else 1
                    for c in range(n):
                        sp.dma_start(wseg[:, wi[seg] + c, :, :], wv[:, :, bass.ds(i * step + at + c * P, P)]
                                     if not isinstance(i, int) else wv[:, :, i * step + at + c * P:i * step + at + (c + 1) * P]
                                     ).then_inc(sem(f"{kind}_w_{seg}"), 16)

                def load_gate(n, i):
                    at = i * (ngate * P) + GATES + (first_gate + n) * P
                    src = wv[:, :, at:at + P] if isinstance(at, int) else wv[:, :, bass.ds(at, P)]
                    sp.dma_start(wgt[:, n, :, :], src).then_inc(sem(f"{kind}_wgate{n}"), 16)
                for q in earlier:
                    sp.wait_ge(*q)
                for s in segs:
                    load(s, 0)
                for n in range(ngate):
                    load_gate(n, 0)
                with sp.Fori(1, rounds, 1) as i:
                    for s in (["q", "f", "g0", "v"] if kind == "a" else segs):
                        sp.wait_ge(*pe.after(s, i - 1))
                        load(s, i)
                    for n in range(ngate):
                        sp.wait_ge(*gate_pe.after(f"t{n}", i - 1))
                        load_gate(n, i)

            def tensor(t):
                pe.begin(t)
                gate_pe.begin(t)
                gates_left = []

                def project(seg, i, n):
                    t.wait_ge(sem(f"{kind}_w_{seg}"), i * 16 + 16)
                    s = slot(n)
                    for k in range(KD):
                        t.matmul(s[:, META:], wseg[:, wi[seg], k, :], uT[:, k, META:], start=(k == 0), stop=(k == KD - 1))
                        mm = t.matmul(s[:, 0:META], wseg[:, wi[seg], k, :], uT[:, k, 0:META], start=(k == 0), stop=(k == KD - 1))
                    mm.then_inc(*pe.did(seg))

                def gate_part(i, steps):
                    for _ in range(steps):
                        if not gates_left:
                            return
                        n, k = gates_left.pop(0)
                        if k == 0:
                            t.wait_ge(sem(f"{kind}_wgate{n}"), i * 16 + 16)
                            if n >= 2:
                                t.wait_ge(*gate_ev.after(f"t{n - 2}", i))
                            elif n == 0:
                                t.wait_ge(*dve.after(f"g{nh - 1}", i))
                        mm = t.matmul(bank(1 + 2 * (n % 2)), wgt[:, n, k, :], uT[:, k, META:],
                                      start=(k == 0), stop=(k == KD - 1))
                        if k == KD - 1:
                            mm.then_inc(*gate_pe.did(f"t{n}"))

                for q in earlier:
                    t.wait_ge(*q)
                with t.Fori(0, rounds, 1) as i:
                    gates_left.extend((n, k) for n in range(ngate) for k in range(KD))
                    if kind == "a":
                        t.wait_ge(*gate_ev.rounds(i))
                        project("f", i, 0)
                        project("q", i, 1)
                        t.wait_ge(*dve.after("f", i))
                        project("g0", i, 0)
                    else:
                        t.wait_ge(*gate_ev.rounds(i))
                        project("k", i, 0)
                        t.wait_ge(sem("c_w2"), i + 1)
                        s = slot(1)
                        for lo, n in ((META, SEQ), (0, META)):
                            mm = t.matmul(s[:, lo:lo + n], w2pad(i), gkT[:, lo:lo + n], start=True, stop=True)
                        mm.then_inc(*pe.did("f"))
                        t.wait_ge(*dve.after("k", i))
                        project("q", i, 0)
                        t.wait_ge(*dve.after("f", i))
                        project("g0", i, 1)
                        t.wait_ge(*dve.after("q", i))
                        project("g1", i, 0)
                    t.wait_ge(sem(f"{kind}_w_v"), i * 16 * nh + 16 * nh)
                    t.wait_ge(*dve.rounds(i))
                    for s in range(nh):
                        for c in range(NTP):
                            lo, n = (0, META) if c == 0 else (META + (c - 1) * P, P)
                            dst = bank(6)[0:META, s * P:(s + 1) * P] if c == 0 else bank(4 + s)[:, (c - 1) * P:c * P]
                            for k in range(KD):
                                mm = t.matmul(dst, uT[:, k, lo:lo + n], wseg[:, wi["v"] + s, k, :],
                                              start=(k == 0), stop=(k == KD - 1))
                    mm.then_inc(*pe.did("v"))
                    gate_part(i, 4 * nh)
                    gb = 0

                    def gram(name, lhs, rhs, free):
                        nonlocal gb
                        t.wait_ge(*free)
                        for c in range(NT):
                            mm = t.matmul(bank(4 + gb % 2)[:, c * P:(c + 1) * P], lhs[:, c * P:(c + 1) * P],
                                          rhs[:, c * P:(c + 1) * P], start=True, stop=True)
                        mm.then_inc(*pe.did(name))
                        gb += 1
                    order = [f"Pd{s}" for s in range(nh)] + [f"P{l}_{s}" for l in range(LEVELS) for s in range(nh)]

                    def free():
                        return act.after("vm", i) if gb < 2 else dve.after(order[gb - 2], i)
                    t.wait_ge(*dve.after("k" if kind == "a" else "f", i))
                    t.wait_ge(*dve.after("q", i))
                    for s in range(nh):
                        gram(f"gd{s}", k_[s * KH:(s + 1) * KH, META:], q_[s * KH:(s + 1) * KH], free())
                    for l in range(LEVELS):
                        gate_part(i, 2 * nh)
                        t.wait_ge(*dve.after(f"zb{l}", i))
                        for s in range(nh):
                            z = zz[l % 2][s * KH:(s + 1) * KH]
                            gram(f"gr{l}_{s}", z, z, free())
                        if l == 0:
                            t.wait_ge(*dve.after("ke", i))
                            t.transpose(bank(6)[0:META, 0:P], eke[:, 0:META], ident)
                            for c in range(1, NT):
                                lo = META + (c - 1) * P
                                mm = t.transpose(bank(6)[:, c * P:(c + 1) * P], eke[:, lo:lo + P], ident)
                            mm.then_inc(*pe.did("keT"))
                        if l == 1:
                            t.wait_ge(*act.after("keTr", i))
                            for c in range(NT):
                                for s in range(nh):
                                    lhs = kt[0:META, 0, s * KH:(s + 1) * KH] if c == 0 else kt[:, c, s * KH:(s + 1) * KH]
                                    rhs = vm[:, s * P:(s + 1) * P] if c == 0 else vt[s][:, (c - 1) * P:c * P]
                                    mm = t.matmul(bank(7)[s * KH:(s + 1) * KH, c * P:(c + 1) * P], lhs, rhs,
                                                  start=True, stop=True)
                            mm.then_inc(*pe.did("kv"))
                    gate_part(i, 100)
                    t.wait_ge(*dve.after(f"P{LEVELS - 1}_{nh - 1}", i))
                    for s in range(nh):
                        for c in range(NT):
                            cs = slice(c * P, (c + 1) * P)
                            ks = slice(s * KH, (s + 1) * KH)
                            t.matmul(bank(6 + s)[:, cs], st[ks, c, :], qe[ks, cs], start=True, stop=False)
                            mm = t.matmul(bank(6 + s)[:, cs], vt[s][:, cs], pm[s][:, cs], start=False, stop=True)
                        mm.then_inc(*pe.did(f"o{s}"))
                    for s in range(nh):
                        t.wait_ge(*act.after(f"sq{s}", i))
                        t.matmul(bank(4 + s), ones[:, :], sqs[s], start=True, stop=True).then_inc(*pe.did(f"ss{s}"))

            def w2pad(i):
                return gkw2s[:, :]

            def scalar(a):
                act.begin(a)
                gate_ev.begin(a)
                for q in earlier:
                    a.wait_ge(*q)
                with a.Fori(0, rounds, 1) as i:
                    a.wait_ge(*dve.rounds(i))
                    if kind == "a":
                        a.wait_ge(*dve.after("f", i))
                        a.activation(tmp, fb, ACT.Sigmoid, scale=-1.0).then_inc(*act.did("sgk"))
                        a.wait_ge(*pe.after("q", i))
                        a.activation(sg, slot(1)[:, META:], ACT.Sigmoid).then_inc(*act.did("sgq"))
                        a.wait_ge(*pe.after("g0", i))
                        a.activation(eb, slot(0)[:, META:], ACT.Sigmoid).then_inc(*act.did("sgg0"))
                    else:
                        a.wait_ge(*pe.after("g0", i))
                        a.activation(sg, slot(1)[:, META:], ACT.Sigmoid).then_inc(*act.did("sgg0"))
                        a.wait_ge(*pe.after("g1", i))
                        a.activation(eb, slot(0)[:, META:], ACT.Sigmoid).then_inc(*act.did("sgg1"))
                    a.wait_ge(*pe.after("v", i))
                    for s in range(nh):
                        a.activation(vt[s], bank(4 + s), ACT.Copy).then_inc(*act.did(f"v{s}"))
                    a.activation(vm, bank(6, nh * P)[0:META], ACT.Copy).then_inc(*act.did("vm"))
                    if kind == "a":
                        a.wait_ge(*dve.after("k", i))
                    else:
                        a.wait_ge(*dve.after("f", i))
                    a.activation(tmp, fb, ACT.Abs).then_inc(*act.did("ab"))
                    a.wait_ge(*act.after("ab", i))
                    a.activation(tmp, tmp, ACT.Exp, scale=-1.0).then_inc(*act.did("e"))
                    a.wait_ge(*act.after("e", i))
                    a.activation(tmp, tmp, ACT.Ln, bias=one_c).then_inc(*act.did("l"))
                    if kind == "a":
                        a.wait_ge(*dve.after("dif", i))
                        a.activation(tmp, lf, ACT.Abs).then_inc(*act.did("ad"))
                        a.wait_ge(*act.after("ad", i))
                        a.activation(tmp, tmp, ACT.Exp, scale=-1.0).then_inc(*act.did("e2"))
                        a.wait_ge(*act.after("e2", i))
                        a.activation(tmp, tmp, ACT.Ln, bias=one_c).then_inc(*act.did("l2"))
                    a.wait_ge(*dve.after("b", i))
                    a.activation(eb, b_[:, META:], ACT.Exp).then_inc(*act.did("eb"))
                    a.activation(dec, b_[:, META + P - 1::P], ACT.Exp).then_inc(*act.did("dec"))
                    a.wait_ge(*dve.after("dbr", i))
                    a.activation(eke[:, 0:TOK - P], db[:, 0:TOK - P], ACT.Exp, scale=-1.0).then_inc(*act.did("eke"))

                    def level(l):
                        h = 1 << l
                        d5 = dd[l % 2].rearrange("p (n a h) -> p n a h", a=2, h=h)
                        e5 = ee[l % 2].rearrange("p (n a h) -> p n a h", a=2, h=h)
                        a.wait_ge(*dve.after(f"d{l}", i))
                        if l >= 2:
                            a.wait_ge(*dve.after(f"zb{l - 2}", i))
                        a.activation(e5[:, :, 0, :], d5[:, :, 0, :], ACT.Exp, scale=-1.0).then_inc(*act.did(f"xa{l}"))
                        a.activation(e5[:, :, 1, :], d5[:, :, 1, :], ACT.Exp).then_inc(*act.did(f"xb{l}"))
                    for l in range(LEVELS):
                        if l == ACT_KET:
                            a.wait_ge(*pe.after("keT", i))
                            a.activation(kt[0:META, 0, :], bank(6)[0:META, 0:P], ACT.Copy).then_inc(*act.did("keTm"))
                            a.activation(kt[:, 1:, :], tiles(bank(6))[:, 1:, :], ACT.Copy).then_inc(*act.did("keTr"))
                        level(l)
                        if l >= 3:
                            for n in range((l - 3) * ngate // 4, (l - 2) * ngate // 4):
                                a.wait_ge(*gate_pe.after(f"t{n}", i))
                                a.activation(gates[:, i * ngate + (first_gate + n), :], bank(1 + 2 * (n % 2)),
                                             ACT.Copy).then_inc(*gate_ev.did(f"t{n}"))
                    for s in range(nh):
                        a.wait_ge(*pe.after(f"o{s}", i))
                        a.activation(sqs[s], bank(6 + s), ACT.Square).then_inc(*act.did(f"sq{s}"))
                    for s in range(nh):
                        a.wait_ge(*pe.after(f"ss{s}", i))
                        a.activation(ris[s], bank(4 + s), ACT.Ln, bias=eps_c, scale=1.0 / P).then_inc(*act.did(f"ln{s}"))
                        a.wait_ge(*act.after(f"ln{s}", i))
                        a.activation(ris[s], ris[s], ACT.Exp, scale=-0.5).then_inc(*act.did(f"ri{s}"))

            sqs = [dd[0], dd[1]]
            ris = [ee[0], ee[1]]
            ACT_KET = 2
            fixed = [n for n in act_n if n not in ("keTm", "keTr")]
            at = fixed.index(f"xa{ACT_KET}")
            act.names = fixed[:at] + ["keTm", "keTr"] + fixed[at:]
            act.index = {n: k + 1 for k, n in enumerate(act.names)}
            gkw2s = sb("gkw2s", [16, P]) if kind == "c" else None

            def vector(v):
                dve.begin(v)
                def tt(name, out_, a_, b2, op):
                    v.tensor_tensor(out_, a_, b2, op).then_inc(*dve.did(name))

                with v.Fori(0, rounds, 1) as i:
                    if kind == "a":
                        v.wait_ge(*pe.after("f", i))
                        v.tensor_copy(fb, slot(0)).then_inc(*dve.did("f"))
                        v.wait_ge(*act.after("sgk", i))
                        v.tensor_scalar(k_, tmp, lbc[:, bass.ds(i, 1)], None, ALU.mult).then_inc(*dve.did("k"))
                        v.wait_ge(*act.after("sgq", i))
                        v.scalar_tensor_tensor(q_, slot(1)[:, META:], P ** -0.5, sg, ALU.mult, ALU.mult).then_inc(*dve.did("q"))
                        v.wait_ge(*act.after("sgg0", i))
                        v.tensor_tensor(g_[0], slot(0)[:, META:], eb, ALU.mult).then_inc(*dve.did("g0"))
                        v.wait_ge(*act.after("l", i))
                        v.scalar_tensor_tensor(fb, fb, 0.0, tmp, ALU.min, ALU.subtract).then_inc(*dve.did("ls"))
                        v.wait_ge(*dve.after("ls", i))
                        v.tensor_scalar(lf, fb, lbc[:, bass.ds(i + 4, 1)], lbc[:, bass.ds(i + 8, 1)],
                                        ALU.add, ALU.subtract).then_inc(*dve.did("dif"))
                        v.tensor_scalar(fb, fb, lbc[:, bass.ds(i + 4, 1)], lbc[:, bass.ds(i + 8, 1)],
                                        ALU.add, ALU.max).then_inc(*dve.did("mx"))
                        v.wait_ge(*act.after("l2", i))
                        v.wait_ge(*dve.after("mx", i))
                        tt("lf", lf, fb, tmp, ALU.add)
                    else:
                        v.wait_ge(*pe.after("k", i))
                        v.tensor_copy(k_, slot(0)).then_inc(*dve.did("k"))
                        v.wait_ge(*pe.after("f", i))
                        v.tensor_scalar(fb, slot(1), rowsT[:, bass.ds(i + R_GKB, 1)], None, ALU.add).then_inc(*dve.did("f"))
                        v.wait_ge(*pe.after("q", i))
                        v.tensor_scalar(q_, slot(0)[:, META:], KH ** -0.5, None, ALU.mult).then_inc(*dve.did("q"))
                        v.wait_ge(*act.after("sgg0", i))
                        tt("g0", g_[0], slot(1)[:, META:], sg, ALU.mult)
                        v.wait_ge(*act.after("sgg1", i))
                        tt("g1", g_[1], slot(0)[:, META:], eb, ALU.mult)
                        v.wait_ge(*act.after("l", i))
                        v.scalar_tensor_tensor(fb, fb, 0.0, tmp, ALU.min, ALU.subtract).then_inc(*dve.did("ls"))
                        v.wait_ge(*dve.after("ls", i))
                        v.tensor_scalar(lf, fb, 1.0 / 16.0, None, ALU.mult).then_inc(*dve.did("lf"))
                    v.wait_ge(*dve.after("lf", i))
                    v.tensor_tensor_scan(b_, reset, lf, 0.0, ALU.mult, ALU.add).then_inc(*dve.did("b"))
                    v.wait_ge(*dve.after("b", i))
                    tt("dbm", db[:, 0:META], b_[:, 0:META], b_[:, META - 1:META].broadcast_to([P, META]), ALU.subtract)
                    br = tiles(b_[:, META:])
                    tt("dbr", tiles(db[:, META:])[:, 0:NT - 1], br[:, 0:NT - 1],
                       br[:, 0:NT - 1, P - 1:P].broadcast_to([P, NT - 1, P]), ALU.subtract)

                    def diff(l):
                        h = 1 << l
                        n = SEQ // (2 * h)
                        bb = b_[:, META:].rearrange("p (n t) -> p n t", t=2 * h)
                        if l >= 2:
                            v.wait_ge(*act.after(f"xb{l - 2}", i))
                        tt(f"d{l}", dd[l % 2].rearrange("p (n t) -> p n t", t=2 * h), bb,
                           bb[:, :, h - 1:h].broadcast_to([P, n, 2 * h]), ALU.subtract)
                    diff(0)
                    v.wait_ge(*act.after("eb", i))
                    tt("qe", qe, q_, eb, ALU.mult)
                    v.wait_ge(*act.after("eke", i))
                    tt("ke", eke[:, 0:TOK - P], eke[:, 0:TOK - P], k_[:, 0:TOK - P], ALU.mult)
                    for s in range(nh):
                        v.wait_ge(*pe.after(f"gd{s}", i))
                        tt(f"Pd{s}", tiles(pm[s]), tiles(bank(4 + s % 2)), over(ident, NT), ALU.mult)
                    gb = nh

                    def pick(l):
                        nonlocal gb
                        for s in range(nh):
                            v.wait_ge(*pe.after(f"gr{l}_{s}", i))
                            v.wait_ge(*dve.after(f"Pd{s}" if l == 0 else f"P{l - 1}_{s}", i))
                            v.tensor_copy(next_spare(), one_c)
                            v.copy_predicated(tiles(pm[s]), over(up(l).bitcast(I32), NT), tiles(bank(4 + gb % 2))
                                              ).then_inc(*dve.did(f"P{l}_{s}"))
                            gb += 1
                    for l in range(LEVELS):
                        if l + 1 < LEVELS:
                            diff(l + 1)
                        h = 1 << l
                        view = "p (n a h) -> p n a h"
                        e5, z5 = (m[l % 2].rearrange(view, a=2, h=h) for m in (ee, zz))
                        k5, q5 = (m.rearrange(view, a=2, h=h) for m in (k_[:, META:], q_))
                        v.wait_ge(*act.after(f"xb{l}", i))
                        if l >= 2:
                            v.wait_ge(*pe.after(f"gr{l - 2}_{nh - 1}", i))
                        tt(f"za{l}", z5[:, :, 0, :], k5[:, :, 0, :], e5[:, :, 0, :], ALU.mult)
                        tt(f"zb{l}", z5[:, :, 1, :], q5[:, :, 1, :], e5[:, :, 1, :], ALU.mult)
                        if l == 2:
                            v.wait_ge(*pe.after("kv", i))
                            v.tensor_copy(st[:, 0, :], bank(7)[:, 0:P]).then_inc(*dve.did("S0"))
                            for c in range(1, NT):
                                v.wait_ge(*dve.after(f"S{c - 1}", i))
                                v.scalar_tensor_tensor(st[:, c, :], st[:, c - 1, :], dec[:, c - 1:c],
                                                       bank(7)[:, c * P:(c + 1) * P], ALU.mult, ALU.add
                                                       ).then_inc(*dve.did(f"S{c}"))
                        if l:
                            pick(l - 1)
                    pick(LEVELS - 1)
                    nw = {"a": R_AN, "c": R_CN}[kind]
                    for s in range(nh):
                        v.wait_ge(*act.after(f"ri{s}", i))
                        v.scalar_tensor_tensor(zz[s], bank(6 + s), rowsT[:, nw:nw + 1], ris[s], ALU.mult, ALU.mult
                                               ).then_inc(*dve.did(f"y1{s}"))
                        v.wait_ge(*dve.after(f"y1{s}", i))
                        tt(f"y{s}", yT[:, i * nh + (first_y + s), :], zz[s], g_[s], ALU.mult)

            def gpsimd(g):
                if kind == "c":
                    with g.Fori(0, rounds, 1) as i:
                        g.wait_ge(*pe.rounds(i))
                        g.wait_ge(sem("small_loaded"), 80)
                        g.tensor_copy(gkw2s[:, :], gkw2[:, bass.ds(i * P, P)]).then_inc(sem("c_w2"), 1)

            if kind == "c":
                plain = tensor

                def w2pad(i):
                    return gkw2s[:, :]
            for e, f in (("sync", sync), ("scalar", scalar), ("vector", vector), ("tensor", tensor), ("gpsimd", gpsimd)):
                programs[e].append(f)
            return pe, act, dve, gate_pe, gate_ev

        def delta(rounds, first_y, first_gate, earlier):
            LV = range(1, LEVELS)
            pe = Steps(sem("b_pe"), ["q", "k", "v", "g", "ssq", "ssk", "G", "B", "KK", "QK", "N", "kT", "vT"] +
                       [x for l in LV for x in ((f"Z{l}", f"EZ{l}", f"ZD{l}") if l < LEVELS - 1 else (f"Z{l}", f"EZ{l}"))] +
                       ["nw"] + [x for c in range(NTP) for x in ([f"V{c}"] + ([f"S{c}"] if c < NT else []))] + ["o", "ss"], 1)
            act = Steps(sem("b_act"), ["sq", "sk", "sv", "sg", "qq", "kk", "lq", "rq", "lk", "rk", "eg", "E", "N"] +
                        [f"Z{l}" for l in LV] + ["nw", "oo", "ln", "ri"], 1)
            dve = Steps(sem("b_dve"), [f"{s}{j}" for s in "qkv" for j in range(4)] +
                        [x for s in "qkv" for x in (f"{s}m", f"{s}r")] + ["g", "pad"] +
                        ["qn", "kn", "dif", "min", "kb", "Ei", "qg", "Es", "U", "QK", "Ua", "Ub", "kbg", "kd", "vb", "Da", "Db"] +
                        [x for l in LV for x in ((f"E{l}", f"D{l}") if l < LEVELS - 1 else (f"E{l}",))] +
                        [x for c in range(NTP) for x in ([f"V{c}"] + ([f"S{c}"] if c < NT else []))] + ["y1", "y"], 1)
            pool = Steps(sem("b_pool"), ["la", "be"], 1)
            gate_pe = Steps(sem("b_gate_pe"), ["t0", "t1"], 1)
            gate_ev = Steps(sem("b_gate_evac"), ["t0", "t1"], 1)
            w = Area(WORK)
            z_, kbg, kd, vb, vn, nwT, s_, n_, qf, kf, vf, kb, em, es, u_, d_, e_ = (w.take(PADTOK) for _ in range(17))
            g_, eg, qg, qk = (w.take(SEQ) for _ in range(4))
            conv = {"q": z_[:, 0:TOK], "k": kbg[:, 0:TOK], "v": kd[:, 0:TOK]}
            sig = vb[:, 0:TOK]
            feat = {"q": qf, "k": kf, "v": vf}
            sqb, rr, labc, bebc = vn, nwT, s_, n_
            segs = ["q", "k", "v", "g"]
            offs = {"q": B_QKV, "k": B_QKV + BW, "v": B_QKV + 2 * BW, "g": B_G}
            slots = {"q": 0, "k": 1, "v": 0, "g": 1}

            def t5(ap):
                return tiles(ap, NTP)

            def pair(n):
                return ps[:, n * 512:n * 512 + PADTOK]

            def head_col(q, i):
                return q.rearrange("p (t h) -> p t h", t=NTP)[:, :, bass.ds(i, 1)].broadcast_to([P, NTP, P])

            def sync(sp):
                def load(s, i):
                    at = i * P + offs[s]
                    src = wv[:, :, at:at + P] if isinstance(at, int) else wv[:, :, bass.ds(at, P)]
                    sp.dma_start(wseg[:, segs.index(s), :, :], src).then_inc(sem(f"b_w_{s}"), 16)

                def load_gate(n, i):
                    at = i * (2 * P) + GATES + (first_gate + n) * P
                    src = wv[:, :, at:at + P] if isinstance(at, int) else wv[:, :, bass.ds(at, P)]
                    sp.dma_start(wgt[:, n, :, :], src).then_inc(sem(f"b_wgate{n}"), 16)
                for q in earlier:
                    sp.wait_ge(*q)
                for s in segs:
                    load(s, 0)
                for n in range(2):
                    load_gate(n, 0)
                with sp.Fori(1, rounds, 1) as i:
                    for s in segs:
                        sp.wait_ge(*pe.after(s, i - 1))
                        load(s, i)
                    for n in range(2):
                        sp.wait_ge(*gate_pe.after(f"t{n}", i - 1))
                        load_gate(n, i)

            def gpsimd(g):
                pool.begin(g)
                for q in earlier:
                    g.wait_ge(*q)
                with g.Fori(0, rounds, 1) as i:
                    g.wait_ge(*dve.rounds(i))
                    g.wait_ge(*dve0.after("dk"))
                    g.tensor_copy(t5(labc), head_col(q_la, i)).then_inc(*pool.did("la"))
                    g.tensor_copy(t5(bebc), head_col(q_beta, i)).then_inc(*pool.did("be"))

            def tensor(t):
                pe.begin(t)
                gate_pe.begin(t)
                left = []

                def gate_part(i, steps):
                    for _ in range(steps):
                        if not left:
                            return
                        n, k = left.pop(0)
                        if k == 0:
                            t.wait_ge(sem(f"b_wgate{n}"), i * 16 + 16)
                            t.wait_ge(*dve.after("g", i))
                        mm = t.matmul(bank(1 + 2 * n), wgt[:, n, k, :], uT[:, k, META:], start=(k == 0), stop=(k == KD - 1))
                        if k == KD - 1:
                            mm.then_inc(*gate_pe.did(f"t{n}"))

                def each(name, dst, lhs, rhs, n=NTP, transpose=False):
                    for c in range(n):
                        cs = slice(c * P, (c + 1) * P)
                        if transpose:
                            mm = t.transpose(dst[:, cs], lhs[:, cs], ident)
                        else:
                            mm = t.matmul(dst[:, cs], lhs[:, cs], rhs[:, cs], start=True, stop=True)
                    mm.then_inc(*pe.did(name))

                for q in earlier:
                    t.wait_ge(*q)
                with t.Fori(0, rounds, 1) as i:
                    left.extend((n, k) for n in range(2) for k in range(KD))
                    t.wait_ge(*gate_ev.rounds(i))
                    for seg, free in (("q", None), ("k", dve.rounds(i)), ("v", dve.after("q3", i)), ("g", dve.after("k3", i))):
                        t.wait_ge(sem(f"b_w_{seg}"), i * 16 + 16)
                        if free:
                            t.wait_ge(*free)
                        s = slot(slots[seg])
                        for k in range(KD):
                            wt = wseg[:, segs.index(seg), k, :]
                            t.matmul(s[:, META:], wt, uT[:, k, META:], start=(k == 0), stop=(k == KD - 1))
                            if seg != "g":
                                mm = t.matmul(s[:, 0:META], wt, uT[:, k, 0:META], start=(k == 0), stop=(k == KD - 1))
                            else:
                                mm = t.matmul(s[:, 0:META], wt, uT[:, k, 0:META], start=(k == 0), stop=(k == KD - 1))
                        mm.then_inc(*pe.did(seg))
                    for s, b in (("q", 4), ("k", 6)):
                        t.wait_ge(*act.after(s * 2, i))
                        src = sqb if s == "q" else kb
                        t.matmul(pair(b)[:, 0:512], ones[:, :], src[:, 0:512], start=True, stop=True)
                        t.matmul(pair(b)[:, 512:], ones[:, :], src[:, 512:], start=True, stop=True).then_inc(*pe.did("ss" + s))
                    t.wait_ge(*pool.after("la", i))
                    t.wait_ge(*act.after("lq", i))
                    for c in range(NTP):
                        mm = t.matmul(pair(4)[:, c * P:(c + 1) * P], labc[:, c * P:(c + 1) * P], inc, start=True, stop=True)
                    mm.then_inc(*pe.did("G"))
                    t.wait_ge(*pool.after("be", i))
                    t.wait_ge(*act.after("lk", i))
                    for c in range(NTP):
                        mm = t.matmul(pair(6)[:, c * P:(c + 1) * P], bebc[:, c * P:(c + 1) * P], ident, start=True, stop=True)
                    mm.then_inc(*pe.did("B"))
                    gate_part(i, 4)
                    t.wait_ge(*dve.after("kb", i))
                    t.wait_ge(*act.after("eg", i))
                    each("KK", pair(4), kf, kb)
                    each("QK", bank(6), kf[:, P:], qf[:, P:], NT)
                    gate_part(i, 1)
                    t.wait_ge(*dve.after("U", i))
                    each("N", pair(4), u_, None, transpose=True)
                    t.wait_ge(*dve.after("QK", i))
                    each("kT", pair(6), kf, None, transpose=True)
                    t.wait_ge(*dve.after("kd", i))
                    each("vT", pair(6), vf, None, transpose=True)
                    gate_part(i, 1)
                    for l in LV:
                        t.wait_ge(*dve.after("Db" if l == 1 else f"D{l - 1}", i))
                        each(f"Z{l}", pair(4), n_, e_)
                        gate_part(i, 1)
                        t.wait_ge(*act.after(f"Z{l}", i))
                        t.wait_ge(*dve.after("vb" if l == 1 else f"E{l - 1}", i))
                        each(f"EZ{l}", pair(6), d_, z_)
                        if l < LEVELS - 1:
                            each(f"ZD{l}", pair(4), z_, d_)
                        gate_part(i, 1)
                    gate_part(i, 100)
                    t.wait_ge(*dve.after(f"E{LEVELS - 1}", i))
                    each("nw", pair(4), kbg, e_)
                    t.wait_ge(*act.after("nw", i))
                    for c in range(NTP):
                        cs = slice(c * P, (c + 1) * P)
                        if c:
                            t.wait_ge(*dve.after(f"S{c - 1}", i))
                        vd = bank(4 + c % 2, P)
                        mm = t.matmul(vd, e_[:, cs], vb[:, cs], start=True, stop=(c == 0))
                        if c:
                            mm = t.matmul(vd, nwT[:, cs], s_[:, (c - 1) * P:c * P], start=False, stop=True)
                        mm.then_inc(*pe.did(f"V{c}"))
                        t.wait_ge(*dve.after(f"V{c}", i))
                        if c < NT:
                            t.matmul(bank(6 + c % 2, P), kd[:, cs], vn[:, cs], start=True, stop=True).then_inc(*pe.did(f"S{c}"))
                        if c:
                            os = slice((c - 1) * P, c * P)
                            t.matmul(bank(2)[:, os], s_[:, os], qg[:, os], start=True, stop=False)
                            mm = t.matmul(bank(2)[:, os], vn[:, cs], qk[:, os], start=False, stop=True)
                    mm.then_inc(*pe.did("o"))
                    t.wait_ge(*act.after("oo", i))
                    t.matmul(bank(4), ones[:, :], d_[:, 0:SEQ], start=True, stop=True).then_inc(*pe.did("ss"))

            def scalar(a):
                act.begin(a)
                gate_ev.begin(a)
                a.wait_ge(sem("rows_zeroed"), 16 * n_zero)
                a.wait_ge(*act0.after("ekd"))
                with a.Fori(0, rounds, 1) as i:
                    a.wait_ge(*dve.rounds(i))
                    for s in "qkv":
                        a.wait_ge(*dve.after(f"{s}3", i))
                        if s != "q":
                            a.wait_ge(*dve.after({"k": "qr", "v": "kr"}[s], i))
                        a.activation(sig, conv[s], ACT.Sigmoid).then_inc(*act.did(f"s{s}"))
                    a.wait_ge(*pe.after("g", i))
                    a.activation(eg, slot(1)[:, META:], ACT.Sigmoid).then_inc(*act.did("sg"))
                    a.wait_ge(*dve.after("pad", i))
                    a.activation(sqb, qf, ACT.Square).then_inc(*act.did("qq"))
                    a.activation(kb, kf, ACT.Square).then_inc(*act.did("kk"))
                    for s, b, dst in (("q", 4, rr), ("k", 6, em)):
                        a.wait_ge(*pe.after("ss" + s, i))
                        a.activation(dst, pair(b), ACT.Ln, bias=eps_c).then_inc(*act.did("l" + s))
                        a.wait_ge(*act.after("l" + s, i))
                        a.activation(dst, dst, ACT.Exp, scale=-0.5).then_inc(*act.did("r" + s))
                    a.wait_ge(*dve.after("min", i))
                    a.activation(eg, pair(4)[:, P:], ACT.Exp).then_inc(*act.did("eg"))
                    a.activation(es, es, ACT.Exp).then_inc(*act.did("E"))
                    a.wait_ge(*pe.after("N", i))
                    a.activation(n_, pair(4), ACT.Copy).then_inc(*act.did("N"))
                    for l in LV:
                        a.wait_ge(*pe.after(f"Z{l}", i))
                        a.activation(z_, pair(4), ACT.Copy).then_inc(*act.did(f"Z{l}"))
                        if l >= 4 and l < 6:
                            n = l - 4
                            a.wait_ge(*gate_pe.after(f"t{n}", i))
                            a.activation(gates[:, i * 2 + (first_gate + n), :], bank(1 + 2 * n), ACT.Copy).then_inc(*gate_ev.did(f"t{n}"))
                    a.wait_ge(*pe.after("nw", i))
                    a.activation(nwT, pair(4), ACT.Copy, scale=-1.0).then_inc(*act.did("nw"))
                    a.wait_ge(*pe.after("o", i))
                    a.activation(d_[:, 0:SEQ], bank(2), ACT.Square).then_inc(*act.did("oo"))
                    a.wait_ge(*pe.after("ss", i))
                    a.activation(u_[:, 0:SEQ], bank(4), ACT.Ln, bias=eps_c, scale=1.0 / P).then_inc(*act.did("ln"))
                    a.wait_ge(*act.after("ln", i))
                    a.activation(u_[:, 0:SEQ], u_[:, 0:SEQ], ACT.Exp, scale=-0.5).then_inc(*act.did("ri"))

            def vector(v):
                dve.begin(v)
                def tt(name, out_, a_, b2, op=ALU.mult):
                    v.tensor_tensor(out_, a_, b2, op).then_inc(*dve.did(name))
                v.wait_ge(*act0.after("ekd"))
                with v.Fori(0, rounds, 1) as i:
                    for n, s in enumerate("qkv"):
                        v.wait_ge(*pe.after(s, i))
                        src, c = slot(slots[s]), conv[s]
                        for j in range(4):
                            wc = rowsT[:, bass.ds(i + (R_CONV + (3 - j) * 12 + n * 4), 1)]
                            if j == 0:
                                v.tensor_scalar(c, src, wc, None, ALU.mult).then_inc(*dve.did(f"{s}0"))
                            else:
                                v.wait_ge(*dve.after(f"{s}{j - 1}", i))
                                v.scalar_tensor_tensor(c[:, j:], src[:, 0:TOK - j], wc, c[:, j:], ALU.mult, ALU.add
                                                       ).then_inc(*dve.did(f"{s}{j}"))
                    for s in "qkv":
                        v.wait_ge(*act.after(f"s{s}", i))
                        tt(f"{s}m", feat[s][:, 0:META], conv[s][:, 0:META], sig[:, 0:META])
                        tt(f"{s}r", feat[s][:, P:], conv[s][:, META:], sig[:, META:])
                    v.wait_ge(*act.after("sg", i))
                    tt("g", g_, slot(1)[:, META:], eg)
                    v.memset(arena3(qf, META, P), 0.0).then_inc(*dve.did("pad"))
                    v.wait_ge(*act.after("rq", i))
                    v.scalar_tensor_tensor(qf, qf, P ** -0.5, rr, ALU.mult, ALU.mult).then_inc(*dve.did("qn"))
                    v.wait_ge(*act.after("rk", i))
                    tt("kn", kf, kf, em)
                    v.wait_ge(*pe.after("G", i))
                    tt("dif", t5(es), t5(pair(4)), head_col(q_g, i), ALU.subtract)
                    v.wait_ge(*dve.after("dif", i))
                    v.tensor_scalar(es, es, 0.0, None, ALU.min).then_inc(*dve.did("min"))
                    v.wait_ge(*pe.after("B", i))
                    v.wait_ge(*dve.after("kn", i))
                    v.scalar_tensor_tensor(kb, pair(6), -1.0, kf, ALU.mult, ALU.mult).then_inc(*dve.did("kb"))
                    v.wait_ge(*act.after("E", i))
                    tt("Ei", t5(em), t5(es), over(inc, NTP))
                    tt("qg", qg, qf[:, P:], eg)
                    v.wait_ge(*dve.after("Ei", i))
                    tt("Es", t5(es), t5(es), over(strict, NTP))
                    v.wait_ge(*dve.after("Es", i))
                    v.wait_ge(*pe.after("KK", i))
                    tt("U", u_, pair(4), es)
                    v.wait_ge(*pe.after("QK", i))
                    tt("QK", qk, bank(6), em[:, P:])
                    v.wait_ge(*dve.after("U", i))
                    tt("Ua", t5(e_), t5(u_), over(up(0), NTP))
                    v.wait_ge(*dve.after("Ua", i))
                    tt("Ub", t5(e_), t5(e_), over(ident, NTP), ALU.add)
                    v.wait_ge(*pe.after("kT", i))
                    tt("kbg", t5(kbg), t5(pair(6)), head_col(q_bg, i))
                    tt("kd", t5(kd), t5(pair(6)), head_col(q_kd, i))
                    v.wait_ge(*pe.after("vT", i))
                    tt("vb", t5(vb), t5(pair(6)), head_col(q_beta, i))
                    v.wait_ge(*act.after("N", i))
                    tt("Da", t5(d_), t5(n_), over(low(0), NTP))
                    v.wait_ge(*dve.after("Da", i))
                    tt("Db", t5(d_), t5(d_), over(ident, NTP), ALU.add)
                    for l in LV:
                        v.wait_ge(*pe.after(f"EZ{l}", i))
                        v.tensor_copy(next_spare(), one_c)
                        v.copy_predicated(t5(e_), over(up(l).bitcast(I32), NTP), t5(pair(6))).then_inc(*dve.did(f"E{l}"))
                        if l < LEVELS - 1:
                            v.wait_ge(*pe.after(f"ZD{l}", i))
                            v.tensor_copy(next_spare(), one_c)
                            v.copy_predicated(t5(d_), over(low(l).bitcast(I32), NTP), t5(pair(4))).then_inc(*dve.did(f"D{l}"))
                    for c in range(NTP):
                        cs = slice(c * P, (c + 1) * P)
                        v.wait_ge(*pe.after(f"V{c}", i))
                        v.tensor_copy(vn[:, cs], bank(4 + c % 2, P)).then_inc(*dve.did(f"V{c}"))
                        if c < NT:
                            v.wait_ge(*pe.after(f"S{c}", i))
                            if c == 0:
                                v.tensor_copy(s_[:, cs], bank(6, P)).then_inc(*dve.did("S0"))
                            else:
                                v.wait_ge(*dve.after(f"S{c - 1}", i))
                                v.scalar_tensor_tensor(s_[:, cs], s_[:, (c - 1) * P:c * P],
                                                       q_egl[:, bass.ds(i + c * 4, 1)], bank(6 + c % 2, P),
                                                       ALU.mult, ALU.add).then_inc(*dve.did(f"S{c}"))
                    v.wait_ge(*act.after("ri", i))
                    v.scalar_tensor_tensor(es[:, 0:SEQ], bank(2), rowsT[:, R_BN:R_BN + 1], u_[:, 0:SEQ], ALU.mult, ALU.mult
                                           ).then_inc(*dve.did("y1"))
                    v.wait_ge(*dve.after("y1", i))
                    tt("y", yT[:, bass.ds(i + first_y, 1), :].rearrange("p a t -> p (a t)"), es[:, 0:SEQ], g_)

            def arena3(first, lo, hi):
                at = WORK + 8 * PADTOK
                return arena[:, at:at + 3 * PADTOK].rearrange("p (a t) -> p a t", a=3)[:, :, lo:hi]

            for e, f in (("sync", sync), ("scalar", scalar), ("vector", vector), ("tensor", tensor), ("gpsimd", gpsimd)):
                programs[e].append(f)
            return pe, act, dve, gate_pe, gate_ev

        def tail(a_steps, b_steps, c_steps):
            pe_c, act_c, dve_c, _, gate_c = c_steps
            mixers_done = [dve_c.rounds(2), gate_c.rounds(2), pe_c.rounds(2)]
            WBR = ARENA - KD * D - 2 * 12 * P
            wbr = [arena[:, WBR + n * 12 * P:WBR + (n + 1) * 12 * P].rearrange("p (k c) -> p k c", k=12) for n in range(2)]
            wo = arena[:, ARENA - KD * D:].rearrange("p (k c) -> p k c", k=KD)
            gb = gates[:, :, :].rearrange("p (b n) t -> p b n t", b=NB)
            h = yT[:, 0:2 * NT, :].rearrange("p (i a) t -> p i (a t)", a=2)
            u2 = gates[:, 8:16, :].rearrange("p (i a) t -> p i (a t)", a=2)
            u2T = gates[:, 0:KD, :]
            wr = gates[:, 16, 0:288].rearrange("p (k c) -> p k c", k=KD)
            rb = gates[:, 16, 288:324]
            scr2 = gates[:, 18:20, :].rearrange("p a t -> p (a t)")
            nf = gates[:, 20:22, :].rearrange("p a t -> p (a t)")
            nfin = gates[:, 22:24, :].rearrange("p a t -> p (a t)")
            pe = Steps(sem("merge_pe"), ["p0", "p1"], 1)
            act = Steps(sem("merge_act"), ["s0", "s1"], 1)
            dve = Steps(sem("merge_dve"), [f"{s}{n}" for n in range(2) for s in ("m", "a", "b")], 1)
            pe2 = Steps(sem("router_pe"), [f"o{n}" for n in range(8)] + [f"T{k}" for k in range(KD)] + ["lg", "rk"])
            rt = ["lb", "gm", "lt", "gs", "gv", "ge", "gd", "gx", "og", "el", "es", "m1", "e1", "q1", "x1", "o1",
                  "n2", "m2", "e2", "q2", "x2", "o2", "dm", "w1a", "w1", "w2", "c1", "c2", "O1", "O2", "M", "rank", "cnt",
                  "j64", "xa", "xb", "xc", "xd", "ci", "ob", "A1", "A2", "r1", "r2", "r3", "R1", "R1s", "R2", "R2s",
                  "idx", "ja", "jb", "jc", "jd", "ji", "ni"]
            dve2 = Steps(sem("router_dve"), [f"h{n}" for n in range(8)] + [f"s{i}" for i in range(NT)] + ["ms"] +
                         [f"u{i}" for i in range(NT)] + [f"T{k}" for k in range(KD)] + rt)
            act2 = Steps(sem("router_act"), ["ln", "rs", "eg", "e2"])
            R = arena3r = gates[:, 17, :]
            rw = sb("rw", [P, 900])
            idx = sb("idx", [P, 2 * NT], I32)
            tile_of = sb("tile_of", [1, EXTRA + 1], I32)
            at = [0]

            def small(*shape):
                n = int(np.prod(shape))
                at[0] += n
                assert at[0] <= 900
                ap = rw[:, at[0] - n:at[0]]
                if len(shape) == 2:
                    return ap.rearrange("p (a b) -> p a b", a=shape[0])
                return ap
            ss2 = small(NT)
            lg = small(NT, NG + NX)
            c_w = [small(NT), small(NT)]

            def sync(sp):
                for q in mixers_done:
                    sp.wait_ge(*q)
                bv = w_branch[0].rearrange("b (k p) d -> p (b k) d", p=P)
                sp.dma_start(wbr[0], bv[:, :, 0:P]).then_inc(sem("branch_w0"), 16)
                sp.dma_start(wbr[1], bv[:, :, P:2 * P]).then_inc(sem("branch_w1"), 16)
                sp.dma_start(wo, w_out[0].rearrange("(k p) d -> p k d", p=P)).then_inc(sem("out_w"), 16)
                with sp.Fori(1, KD // 2, 1) as i:
                    for n in range(2):
                        sp.wait_ge(*pe.after(f"p{n}", i - 1))
                        sp.dma_start(wbr[n], bv[:, :, bass.ds(i * (2 * P) + n * P, P)]).then_inc(sem(f"branch_w{n}"), 16)
                for q in (pe.rounds(KD // 2), dve.rounds(KD // 2)):
                    sp.wait_ge(*q)
                sp.dma_start(h, x[0].rearrange("(i p) d -> p i d", p=P)).then_inc(sem("x_again"), 16)
                sp.dma_start(nf, norm_ffn[0:1, :].broadcast_to([P, D])).then_inc(sem("tail_small"), 16)
                sp.dma_start(nfin, norm_final.unsqueeze(0).broadcast_to([P, D])).then_inc(sem("tail_small"), 16)
                sp.dma_start(wr[:, :, 0:NG], router_group_w[0].rearrange("(k p) c -> p k c", p=P)).then_inc(sem("tail_small"), 16)
                sp.dma_start(wr[:, :, NG:], router_expert_w[0].rearrange("(k p) c -> p k c", p=P)).then_inc(sem("tail_small"), 16)
                sp.dma_start(rb[:, 0:NG], router_group_b[0:1, :].broadcast_to([P, NG])).then_inc(sem("tail_small"), 16)
                sp.dma_start(rb[:, NG:], router_expert_b[0:1, :].broadcast_to([P, NX])).then_inc(sem("tail_small"), 16)

            def scalar(a):
                act.begin(a)
                a.wait_ge(*gate_c.rounds(2))
                with a.Fori(0, KD // 2, 1) as i:
                    for n in range(2):
                        g = gb[:, :, bass.ds(i * 2 + n, 1), :].rearrange("p b a t -> p b (a t)")
                        a.activation(g, g, ACT.Sigmoid).then_inc(*act.did(f"s{n}"))
                a.wait_ge(*dve2.after("ms"))
                a.activation(ss2, ss2, ACT.Ln).then_inc(*act2.did("ln"))
                a.wait_ge(*act2.after("ln"))
                a.activation(ss2, ss2, ACT.Exp, scale=-0.5).then_inc(*act2.did("rs"))
                a.wait_ge(*dve2.after("lt"))
                a.activation(gx, lt, ACT.Exp).then_inc(*act2.did("eg"))
                a.wait_ge(*dve2.after("dm"))
                a.activation(e2, dm, ACT.Exp).then_inc(*act2.did("e2"))

            def tensor(t):
                pe.begin(t)
                t.wait_ge(*dve_c.rounds(2))
                t.wait_ge(*gate_c.rounds(2))
                with t.Fori(0, KD // 2, 1) as i:
                    for n in range(2):
                        t.wait_ge(sem(f"branch_w{n}"), i * 16 + 16)
                        if n == 0:
                            t.wait_ge(*dve.rounds(i))
                        for b in range(NB):
                            for k in range(4):
                                mm = t.matmul(bank(4 * n + b), wbr[n][:, 4 * b + k, :], yT[:, 4 * b + k, :],
                                              start=(k == 0), stop=(k == 3))
                        mm.then_inc(*pe.did(f"p{n}"))
                t.wait_ge(*dve.rounds(KD // 2))
                t.wait_ge(sem("out_w"), 16)
                for n in range(8):
                    i, j = n // 2, n % 2
                    for k in range(KD):
                        mm = t.matmul(bank(n), gates[:, k, i * P:(i + 1) * P], wo[:, k, j * 512:(j + 1) * 512],
                                      start=(k == 0), stop=(k == KD - 1))
                    mm.then_inc(*pe2.did(f"o{n}"))
                t.wait_ge(*dve2.after(f"u{NT - 1}"))
                for k in range(KD):
                    if k >= 2:
                        t.wait_ge(*dve2.after(f"T{k - 2}"))
                    for i in range(NT):
                        mm = t.transpose(bank(k % 2)[:, i * P:(i + 1) * P], u2[:, i, k * P:(k + 1) * P], ident)
                    mm.then_inc(*pe2.did(f"T{k}"))
                t.wait_ge(*dve2.after(f"T{KD - 1}"))
                t.wait_ge(sem("tail_small"), 96)
                for i in range(NT):
                    for k in range(KD):
                        mm = t.matmul(bank(2)[:, i * 36:(i + 1) * 36], u2T[:, k, i * P:(i + 1) * P], wr[:, k, :],
                                      start=(k == 0), stop=(k == KD - 1))
                mm.then_inc(*pe2.did("lg"))
                t.wait_ge(*dve2.after("M"))
                for i in range(NT):
                    dst = bank(3)[:, i * NX:(i + 1) * NX]
                    t.matmul(dst, strict, mm_[:, i, :], start=True, stop=(i == 0))
                    for j in range(i):
                        t.matmul(dst, ones[:, :], mm_[:, j, :], start=False, stop=(j == i - 1))
                for j in range(NT):
                    mm = t.matmul(bank(3)[:, NT * NX:(NT + 1) * NX], ones[:, :], mm_[:, j, :], start=(j == 0), stop=(j == NT - 1))
                mm.then_inc(*pe2.did("rk"))

            lt, gx, og = small(NT, NG), small(NT, NG), small(NT, NG)
            t4 = small(NT, NG)
            gm, gv, m1, m2, dm, e2, mx = (small(NT) for _ in range(7))
            el, o1, o2, t8 = small(NT, NE), small(NT, NE), small(NT, NE), small(NT, NE)
            O1, O2, mm_, rk = (gates[:, 17, n * 128:(n + 1) * 128].rearrange("p (i e) -> p i e", i=NT) for n in range(4))
            sel = gates[:, 16, 324:324 + 128].rearrange("p (i g e) -> p i g e", i=NT, g=NG)
            cnt, ci, ex, ob, aa = (small(NX) for _ in range(5))
            j64 = small(16)
            rows2 = small(NT, 2)
            ej = small(17)
            big = gates[:, 18, :].rearrange("p (e j) -> p e j", j=16)
            u2out = u2
            J = C[:, K_J:K_J + 16]
            DESC = C[:, K_DESC:K_DESC + NE]
            E64 = C[:, K_E64:K_E64 + NX]

            def vector(v):
                dve.begin(v)
                with v.Fori(0, KD // 2, 1) as i:
                    for n in range(2):
                        g = gb[:, :, bass.ds(i * 2 + n, 1), :].rearrange("p b a t -> p b (a t)")
                        v.wait_ge(*pe.after(f"p{n}", i))
                        v.wait_ge(*act.after(f"s{n}", i))
                        v.tensor_tensor(g, ps[:, 4 * n * 512:(4 * n + 3) * 512].rearrange("p (b t) -> p b t", b=NB), g,
                                        ALU.mult).then_inc(*dve.did(f"m{n}"))
                        for b, s in ((1, "a"), (2, "b")):
                            v.wait_ge(*dve.after(f"m{n}" if s == "a" else f"a{n}", i))
                            v.tensor_tensor(g[:, 0, :], g[:, 0, :], g[:, b, :], ALU.add).then_inc(*dve.did(f"{s}{n}"))
                v.wait_ge(sem("x_again"), 16)
                for n in range(8):
                    i, j = n // 2, n % 2
                    hs = h[:, i, j * 512:(j + 1) * 512]
                    v.wait_ge(*pe2.after(f"o{n}"))
                    v.tensor_tensor(hs, bank(n), hs, ALU.add).then_inc(*dve2.did(f"h{n}"))
                for i in range(NT):
                    v.wait_ge(*dve2.after(f"h{2 * i + 1}" if i == 0 else f"s{i - 1}"))
                    if i == 0:
                        v.wait_ge(*dve2.after("h7"))
                    v.tensor_tensor_reduce(scr2, h[:, i, :], h[:, i, :], 1.0, 0.0, ALU.mult, ALU.add,
                                           accum_out=ss2[:, i:i + 1]).then_inc(*dve2.did(f"s{i}"))
                v.wait_ge(*dve2.after(f"s{NT - 1}"))
                v.tensor_scalar(ss2, ss2, 1.0 / D, EPS, ALU.mult, ALU.add).then_inc(*dve2.did("ms"))
                v.wait_ge(sem("tail_small"), 96)
                v.wait_ge(*act2.after("rs"))
                for i in range(NT):
                    v.scalar_tensor_tensor(u2[:, i, :], h[:, i, :], ss2[:, i:i + 1], nf, ALU.mult, ALU.mult).then_inc(*dve2.did(f"u{i}"))
                for k in range(KD):
                    v.wait_ge(*pe2.after(f"T{k}"))
                    v.tensor_copy(u2T[:, k, :], bank(k % 2)).then_inc(*dve2.did(f"T{k}"))
                last = [None]

                def step(name, ins):
                    ins.then_inc(*dve2.did(name))
                    v.wait_ge(*dve2.after(name))

                def tt(name, out_, a_, b_, op):
                    step(name, v.tensor_tensor(out_, a_, b_, op))

                def ts(name, out_, a_, s1, op0, s2=None, op1=None):
                    step(name, v.tensor_scalar(out_, a_, s1, s2, op0, op1) if op1 else v.tensor_scalar(out_, a_, s1, None, op0))

                def red(name, out_, a_, op):
                    step(name, v.tensor_reduce(out_, a_, axis=AX.X, op=op))

                def wide(ap, n):
                    return ap.unsqueeze(2).broadcast_to([P, NT, n])
                v.wait_ge(*pe2.after("lg"))
                tt("lb", lg, bank(2, NT * 36).rearrange("p (i c) -> p i c", i=NT), over(rb, NT), ALU.add)
                g4, g32 = lg[:, :, 0:NG], lg[:, :, NG:].rearrange("p i (g e) -> p i g e", g=NG)
                red("gm", gm, g4, ALU.max)
                tt("lt", lt, g4, wide(gm, NG), ALU.subtract)
                v.wait_ge(*act2.after("eg"))
                red("gs", gv, gx, ALU.add)
                step("gv", v.reciprocal(gv, gv))
                ts("ge", t4, lt, 0.0, ALU.is_ge)
                tt("gd", t4, t4, over(DESC[:, 0:NG], NT), ALU.mult)
                red("gx", mx, t4, ALU.max)
                tt("og", og, t4, wide(mx, NG), ALU.is_equal)
                tt("el", sel, g32, og.unsqueeze(3).broadcast_to([P, NT, NG, NE]), ALU.mult)
                red("es", el, sel.rearrange("p i g e -> p i e g"), ALU.add)
                for n, o_, m_ in (("1", o1, m1), ("2", o2, m2)):
                    if n == "2":
                        step("n2", v.scalar_tensor_tensor(el, o1, -1e30, el, ALU.mult, ALU.add))
                    red("m" + n, m_, el, ALU.max)
                    tt("e" + n, t8, el, wide(m_, NE), ALU.is_ge)
                    tt("q" + n, t8, t8, over(DESC, NT), ALU.mult)
                    red("x" + n, mx, t8, ALU.max)
                    tt("o" + n, o_, t8, wide(mx, NE), ALU.is_equal)
                tt("dm", dm, m2, m1, ALU.subtract)
                v.wait_ge(*act2.after("e2"))
                ts("w1a", m1, e2, 1.0, ALU.add)
                step("w1", v.reciprocal(m1, m1))
                tt("w2", m2, e2, m1, ALU.mult)
                tt("c1", c_w[0], m1, gv, ALU.mult)
                tt("c2", c_w[1], m2, gv, ALU.mult)
                for n, o_, O_ in (("1", o1, O1), ("2", o2, O2)):
                    tt("O" + n, O_.rearrange("p i (g e) -> p i g e", g=NG), og.unsqueeze(3).broadcast_to([P, NT, NG, NE]),
                       o_.unsqueeze(2).broadcast_to([P, NT, NG, NE]), ALU.mult)
                tt("M", mm_, O1, O2, ALU.add)
                v.wait_ge(*pe2.after("rk"))
                step("rank", v.tensor_copy(rk, bank(3, NT * NX).rearrange("p (i e) -> p i e", i=NT)))
                step("cnt", v.tensor_copy(cnt, bank(3)[:, NT * NX:(NT + 1) * NX]))
                ts("j64", j64, J, float(SLOTS), ALU.mult)
                tt("xa", big, cnt.unsqueeze(2).broadcast_to([P, NX, 16]), over(j64, NX), ALU.subtract)
                ts("xb", big, big, 0.0, ALU.is_gt)
                red("xc", ex, big, ALU.add)
                ts("xd", ex, ex, 1.0, ALU.max, -1.0, ALU.add)
                step("ci", v.tensor_tensor_scan(ci, ones[:, 0:NX], ex, 0.0, ALU.mult, ALU.add))
                tt("ob", ob, ci, ex, ALU.subtract)
                ts("A1", aa, ob, float(SLOTS), ALU.mult, float((NX - 1) * SLOTS), ALU.add)
                tt("A2", aa, aa, E64, ALU.subtract)
                ts("r1", sel.rearrange("p i g e -> p i (g e)"), rk, float(SLOTS), ALU.is_ge)
                selr = sel.rearrange("p i g e -> p i (g e)")
                tt("r2", selr, selr, over(aa, NT), ALU.mult)
                tt("r3", rk, rk, over(E64, NT), ALU.add)
                tt("R1", rk, rk, selr, ALU.add)
                tt("R1s", O1, O1, rk, ALU.mult)
                tt("R2", O2, O2, rk, ALU.mult)
                red("R2s", rows2[:, :, 0], O1, ALU.add)
                red("idx", rows2[:, :, 1], O2, ALU.add)
                step("ja", v.tensor_copy(idx[:, :], rows2.rearrange("p i k -> p (i k)")))
                tt("jb", big, J.unsqueeze(1).broadcast_to([P, NX, 16]), ci.unsqueeze(2).broadcast_to([P, NX, 16]), ALU.is_ge)
                red("jc", ej[:, 0:16], big.rearrange("p e j -> p j e"), ALU.add)
                ts("jd", ej[:, 0:16], ej[:, 0:16], float(NX - 1), ALU.min)
                step("ji", v.tensor_copy(tile_of[:, 0:16], ej[0:1, 0:16]))
                step("ni", v.tensor_copy(tile_of[:, 16:17], ci[0:1, NX - 1:NX]))

            def gpsimd(g):
                g.wait_ge(*dve2.after("ja"))
                g.wait_ge(sem("rows_zeroed"), 16 * n_zero)
                for i in range(NT):
                    for k in range(2):
                        g.indirect_dma_start(out=xs_dram, out_offset=bass.IndirectOffsetOnAxis(ap=idx[:, 2 * i + k:2 * i + k + 1], axis=0),
                                             in_=u2[:, i, :], in_offset=None).then_inc(sem("scattered"), 16)

            for e, f in (("sync", sync), ("scalar", scalar), ("vector", vector), ("tensor", tensor), ("gpsimd", gpsimd)):
                programs[e].append(f)

            NR = 3
            ring = [arena[:, n * 6144:(n + 1) * 6144] for n in range(3)]
            NX_R = NR
            xr = [gates[0:SLOTS, 2 * n:2 * n + 2, :].rearrange("p a t -> p (a t)") for n in range(4)]
            yr = [gates[0:SLOTS, 8 + 2 * n:10 + 2 * n, :].rearrange("p a t -> p (a t)") for n in range(2)]
            xT = [gates[:, 12 + n, :].rearrange("p (k t) -> p k t", k=KD) for n in range(2)]
            hd = [gates[:, 14 + n, 0:256] for n in range(2)]
            wgv = expert_w_gate[0].rearrange("g e (p k) h -> (g e) p (k h)", p=P)
            wuv = expert_w_up[0].rearrange("g e (p k) h -> (g e) p (k h)", p=P)
            wdv = expert_w_down[0].rearrange("g e (p k) h -> (g e) p (k h)", p=P)
            U = 4
            epe = Steps(sem("expert_pe"), [f"{s}{n}" for n in range(U) for s in ("T", "g", "u", "y")], 1)
            eact = Steps(sem("expert_act"), [f"{s}{n}" for n in range(U) for s in ("s", "y")], 1)
            edve = Steps(sem("expert_dve"), [f"{s}{n}" for n in range(U) for s in ("T", "a", "h", "y")], 1)
            ring4 = ring + [arena[:, 18432:18432 + 6144]]

            def parts(n):
                r = ring4[n]
                return (r[:, 0:2048].rearrange("p (k h) -> p k h", k=KD), r[:, 2048:4096].rearrange("p (k h) -> p k h", k=KD),
                        r[:, 4096:6144].rearrange("p (j d) -> p j d", j=2))

            def load_weights(sp, n, e):
                one = (lambda vw: vw[e]) if isinstance(e, int) else (lambda vw: vw[bass.ds(e, 1)].rearrange("a p m -> p (a m)"))
                for vw, lo in ((wgv, 0), (wuv, 2048), (wdv, 4096)):
                    sp.dma_start(ring4[n][:, lo:lo + 2048], one(vw)).then_inc(sem(f"expert_w{n}"), 16)

            def load_rows(sp, n, e):
                sp.dma_start(xr[n], xs_dram[e * SLOTS:(e + 1) * SLOTS, :] if isinstance(e, int)
                             else xs_dram[bass.ds(e * SLOTS, SLOTS), :]).then_inc(sem(f"expert_x{n}"), 16)

            def esync(sp):
                for n in range(3):
                    load_weights(sp, n, n)
                sp.wait_ge(*pe2.after("o7"))
                load_weights(sp, 3, 3)
                sp.wait_ge(sem("scattered"), 16 * 2 * NT)
                sp.wait_ge(*pe2.after("lg"))
                if dbg:
                    sp.dma_start(dbg["u2"], u2).then_inc(sem("dbg"), 16)
                    sp.dma_start(dbg["h"], h).then_inc(sem("dbg"), 16)
                    sp.wait_ge(*dve2.after("ni"))
                    sp.dma_start(dbg["rw"], rw[:, 0:148+8]).then_inc(sem("dbg"), 16)
                    sp.wait_ge(sem("dbg"), 48)
                for n in range(U):
                    load_rows(sp, n, n)
                with sp.Fori(0, NX // U - 1, 1) as i:
                    for n in range(U):
                        sp.wait_ge(*epe.after(f"T{n}", i))
                        load_rows(sp, n, i * U + (n + U))
                        sp.wait_ge(*epe.after(f"y{n}", i))
                        load_weights(sp, n, i * U + (n + U))

            def expert_tensor(t, st_, ev_a, ev_d, n, i, xw, ww, wv_):
                wg, wu, wd = parts(n)
                t.wait_ge(*xw)
                for k in range(KD):
                    dst, rows = bank(n % 2)[:, k * SLOTS:(k + 1) * SLOTS], xr[n][:, k::KD]
                    if k == 0:
                        t.matmul(dst, rows, ident[0:SLOTS, 0:SLOTS], start=True, stop=True)
                    else:
                        mm = t.transpose(dst, rows, ident[0:SLOTS, 0:SLOTS])
                mm.then_inc(*st_.did(f"T{n}"))
                t.wait_ge(*ww)
                t.wait_ge(*ev_d.after(f"T{n}", i))
                for s, wm, b in (("g", wg, 2), ("u", wu, 4)):
                    for j in range(2):
                        for k in range(KD):
                            mm = t.matmul(bank(b + n % 2)[:, j * SLOTS:(j + 1) * SLOTS], wm[:, k, j::2], xT[n % 2][:, k, :],
                                          start=(k == 0), stop=(k == KD - 1))
                    mm.then_inc(*st_.did(f"{s}{n}"))
                t.wait_ge(*ev_d.after(f"h{n}", i))
                for q in wv_:
                    t.wait_ge(*q)
                for half in range(2):
                    for j in range(2):
                        mm = t.matmul(bank(6 + half)[0:SLOTS, :], hd[n % 2][:, j * SLOTS:(j + 1) * SLOTS],
                                      wd[:, j, half * 512:(half + 1) * 512], start=(j == 0), stop=(j == 1))
                mm.then_inc(*st_.did(f"y{n}"))

            def etensor(t):
                epe.begin(t)
                with t.Fori(0, NX // U, 1) as i:
                    for n in range(U):
                        prev = [eact.rounds(i), edve.rounds(i)] if n == 0 else [eact.after(f"y{n - 1}", i), edve.after(f"y{n - 1}", i)]
                        expert_tensor(t, epe, eact, edve, n, i, (sem(f"expert_x{n}"), i * 16 + 16),
                                      (sem(f"expert_w{n}"), i * 48 + 48), prev)

            def expert_scalar(a, st_, pe_, n, i, sw):
                a.wait_ge(*pe_.after(f"g{n}", i))
                a.activation(hd[n % 2][:, 128:256], bank(2 + n % 2, 2 * SLOTS), ACT.Sigmoid).then_inc(*st_.did(f"s{n}"))
                a.wait_ge(*pe_.after(f"y{n}", i))
                if sw:
                    a.wait_ge(*sw)
                a.activation(yr[n % 2][:, 0:512], bank(6)[0:SLOTS, :], ACT.Copy).then_inc(*st_.did(f"y{n}"))

            def escalar(a):
                eact.begin(a)
                for n in range(2):
                    a.nop().then_inc(sem(f"expert_stored{n}"), 1)
                with a.Fori(0, NX // U, 1) as i:
                    for n in range(U):
                        if n < 2:
                            a.wait_ge(*edve.rounds(i))
                        sw = (sem(f"expert_stored{n % 2}"), i * 32 + 1) if n < 2 else (sem(f"expert_stored{n % 2}"), i * 32 + 17)
                        expert_scalar(a, eact, epe, n, i, sw)
                        a.wait_ge(*eact.after(f"y{n}", i))
                        a.wait_ge(*edve.after(f"y{n}", i))
                        a.dma_start(ys_dram[bass.ds(i * (U * SLOTS) + n * SLOTS, SLOTS), :], yr[n % 2]
                                    ).then_inc(sem(f"expert_stored{n % 2}"), 16)

            def expert_vector(v, st_, pe_, ac_, n, i, sw):
                v.wait_ge(*pe_.after(f"T{n}", i))
                v.tensor_copy(xT[n % 2], bank(n % 2).rearrange("p (k t) -> p k t", k=KD)).then_inc(*st_.did(f"T{n}"))
                v.wait_ge(*ac_.after(f"s{n}", i))
                v.tensor_tensor(hd[n % 2][:, 128:256], hd[n % 2][:, 128:256], bank(2 + n % 2, 2 * SLOTS), ALU.mult).then_inc(*st_.did(f"a{n}"))
                v.wait_ge(*st_.after(f"a{n}", i))
                v.wait_ge(*pe_.after(f"u{n}", i))
                v.tensor_tensor(hd[n % 2][:, 0:128], hd[n % 2][:, 128:256], bank(4 + n % 2, 2 * SLOTS), ALU.mult).then_inc(*st_.did(f"h{n}"))
                v.wait_ge(*pe_.after(f"y{n}", i))
                if sw:
                    v.wait_ge(*sw)
                v.tensor_copy(yr[n % 2][:, 512:], bank(7)[0:SLOTS, :]).then_inc(*st_.did(f"y{n}"))

            def evector(v):
                edve.begin(v)
                v.wait_ge(sem("scattered"), 16 * 2 * NT)
                with v.Fori(0, NX // U, 1) as i:
                    for n in range(U):
                        sw = (sem(f"expert_stored{n % 2}"), i * 32 + 1) if n < 2 else (sem(f"expert_stored{n % 2}"), i * 32 + 17)
                        expert_vector(v, edve, epe, eact, n, i, sw)

            for e, f in (("sync", esync), ("scalar", escalar), ("vector", evector), ("tensor", etensor)):
                programs[e].append(f)

            ope = Steps(sem("extra_pe"), ["T0", "g0", "u0", "y0"], 1)
            oact = Steps(sem("extra_act"), ["s0", "y0"], 1)
            odve = Steps(sem("extra_dve"), ["T0", "a0", "h0", "y0"], 1)

            def extra(eng, body):
                eng.wait_ge(*dve2.after("ni"))
                count = eng.value_load(tile_of[0:1, EXTRA:EXTRA + 1], min_val=0, max_val=EXTRA)
                with eng.If(count > 0):
                    with eng.Fori(0, EXTRA, 1) as j:
                        with eng.If(count > j):
                            body(j)
                return count

            def osync(sp):
                sp.wait_ge(*epe.rounds(NX // U))
                sp.wait_ge(sem("expert_stored0"), 16 * NX // 2 + 1)
                sp.wait_ge(sem("expert_stored1"), 16 * NX // 2 + 1)

                def body(j):
                    sp.wait_ge(sem("extra_stored"), j * 16 + 1)
                    e = sp.value_load(tile_of[0:1, bass.ds(j, 1)], min_val=0, max_val=NX - 1)
                    sp.dma_start(xr[0], xs_dram[bass.ds(j * SLOTS + NX * SLOTS, SLOTS), :]).then_inc(sem("extra_x"), 16)
                    for vw, lo in ((wgv, 0), (wuv, 2048), (wdv, 4096)):
                        sp.dma_start(ring4[0][:, lo:lo + 2048], vw[bass.ds(e, 1)].rearrange("a p m -> p (a m)")).then_inc(sem("extra_w"), 16)
                count = extra(sp, body)
                sp.wait_ge(sem("extra_stored"), count * 16 + 1)
                sp.nop().then_inc(sem("results_stored"), 1)

            def otensor(t):
                ope.begin(t)
                def body(j):
                    t.wait_ge(*oact.rounds(j))
                    t.wait_ge(*odve.rounds(j))
                    t.wait_ge(*eact.rounds(NX // U))
                    t.wait_ge(*edve.rounds(NX // U))
                    expert_tensor(t, ope, oact, odve, 0, j, (sem("extra_x"), j * 16 + 16), (sem("extra_w"), j * 48 + 48), [])
                extra(t, body)

            def oscalar(a):
                oact.begin(a)
                a.nop().then_inc(sem("extra_stored"), 1)
                def body(j):
                    a.wait_ge(sem("extra_x"), j * 16 + 16)
                    expert_scalar(a, oact, ope, 0, j, None)
                    a.wait_ge(*oact.after("y0", j))
                    a.wait_ge(*odve.after("y0", j))
                    a.dma_start(ys_dram[bass.ds(j * SLOTS + NX * SLOTS, SLOTS), :], yr[0]).then_inc(sem("extra_stored"), 16)
                extra(a, body)

            def ovector(v):
                odve.begin(v)
                def body(j):
                    v.wait_ge(sem("extra_x"), j * 16 + 16)
                    expert_vector(v, odve, ope, oact, 0, j, None)
                extra(v, body)

            for e, f in (("sync", osync), ("scalar", oscalar), ("vector", ovector), ("tensor", otensor)):
                programs[e].append(f)

            yg = [arena[:, n * D:(n + 1) * D] for n in range(2 * NT)]
            fdve = Steps(sem("final_dve"), [f"{s}{i}" for i in range(NT) for s in ("a", "b", "s")] + ["ms"] + [f"o{i}" for i in range(NT)])
            fact = Steps(sem("final_act"), ["ln", "rs"])

            def fgpsimd(g):
                g.wait_ge(sem("results_stored"), 1)
                for i in range(NT):
                    for k in range(2):
                        g.indirect_dma_start(out=yg[2 * i + k], out_offset=None, in_=ys_dram,
                                             in_offset=bass.IndirectOffsetOnAxis(ap=idx[:, 2 * i + k:2 * i + k + 1], axis=0)
                                             ).then_inc(sem(f"gathered{i}"), 16)

            def fvector(v):
                for i in range(NT):
                    v.wait_ge(sem(f"gathered{i}"), 32)
                    for k, s in ((0, "a"), (1, "b")):
                        if k:
                            v.wait_ge(*fdve.after(f"a{i}"))
                        v.scalar_tensor_tensor(h[:, i, :], yg[2 * i + k], c_w[k][:, i:i + 1], h[:, i, :], ALU.mult, ALU.add
                                               ).then_inc(*fdve.did(f"{s}{i}"))
                    v.wait_ge(*fdve.after(f"b{i}"))
                    v.tensor_tensor_reduce(scr2, h[:, i, :], h[:, i, :], 1.0, 0.0, ALU.mult, ALU.add,
                                           accum_out=ss2[:, i:i + 1]).then_inc(*fdve.did(f"s{i}"))
                v.wait_ge(*fdve.after(f"s{NT - 1}"))
                v.tensor_scalar(ss2, ss2, 1.0 / D, EPS, ALU.mult, ALU.add).then_inc(*fdve.did("ms"))
                v.wait_ge(*fact.after("rs"))
                for i in range(NT):
                    v.scalar_tensor_tensor(h[:, i, :], h[:, i, :], ss2[:, i:i + 1], nfin, ALU.mult, ALU.mult).then_inc(*fdve.did(f"o{i}"))

            def fscalar(a):
                a.wait_ge(*fdve.after("ms"))
                a.activation(ss2, ss2, ACT.Ln).then_inc(*fact.did("ln"))
                a.wait_ge(*fact.after("ln"))
                a.activation(ss2, ss2, ACT.Exp, scale=-0.5).then_inc(*fact.did("rs"))

            def fsync(sp):
                ov = out[0].rearrange("(i p) d -> p i d", p=P)
                for i in range(NT):
                    sp.wait_ge(*fdve.after(f"o{i}"))
                    sp.dma_start(ov[:, i, :], h[:, i, :]).then_inc(sem("stored"), 16)
                sp.wait_ge(sem("stored"), 16 * NT)

            for e, f in (("sync", fsync), ("scalar", fscalar), ("vector", fvector), ("gpsimd", fgpsimd)):
                programs[e].append(f)

        names = {}
        if stop is None:
            sa = gla("a", 4, 0, 0, [])
            sb_ = delta(4, 4, 8, [sa[2].rounds(4), sa[4].rounds(4)])
            sc = gla("c", 2, 8, 16, [sb_[2].rounds(4), sb_[4].rounds(4)])
            tail(sa, sb_, sc)
        elif stop == "c":
            names["a"] = gla("c", 2, 0, 0, [])
        elif stop == "b":
            names["a"] = delta(4, 0, 0, [])
        else:
            names["a"] = gla("a", 4, 0, 0, [])
        if stop and stop in "abc":
            def dump(sp):
                sp.wait_ge(*names["a"][2].rounds(2 if stop == 'c' else 4))
                sp.wait_ge(*names["a"][4].rounds(2 if stop == 'c' else 4))
                sp.wait_ge(sem("rows_zeroed"), 16 * n_zero)
                sp.wait_ge(*act0.after("ekd"))
                sp.dma_start(dbg["y"], yT[:, 0:4, :]).then_inc(sem("dbg"), 16)
                sp.dma_start(dbg["gates"], gates[:, 0:8, :]).then_inc(sem("dbg"), 16)
                sp.dma_start(dbg["bcol"], bcol[:, :]).then_inc(sem("dbg"), 16)
                sp.wait_ge(sem("dbg"), 48)
            programs["sync"].append(dump)

        @block.sync
        def _(e):
            for f in programs["sync"]:
                f(e)

        @block.scalar
        def _(e):
            for f in programs["scalar"]:
                f(e)

        @block.vector
        def _(e):
            for f in programs["vector"]:
                f(e)

        @block.tensor
        def _(e):
            for f in programs["tensor"]:
                f(e)

        @block.gpsimd
        def _(e):
            for f in programs["gpsimd"]:
                f(e)


_INS = ["x", "meta_tokens", "norm_mix", "w_in", "hgrn_lb_logits", "hgrn_norm", "gdn_conv", "gdn_a_log",
        "gdn_dt_bias", "gdn_norm", "gla_gk_w2", "gla_gk_b", "gla_norm", "w_branch", "w_out", "norm_ffn",
        "router_group_w", "router_group_b", "router_expert_w", "router_expert_b",
        "expert_w_gate", "expert_w_up", "expert_w_down", "norm_final"]


def kernel(**inputs):
    import concourse.bacc as bacc
    from concourse.bass_utils import run_bass_kernel_spmd

    nc = bacc.Bacc("TRN2", target_bir_lowering=False, num_devices=1)
    arrays = {f"in_{n}": np.ascontiguousarray(inputs[n]) for n in _INS}
    arrays["in_consts"] = constants()
    args = [nc.dram_tensor(n, a.shape, mybir.dt.from_np(a.dtype), kind="ExternalInput").ap() for n, a in arrays.items()]
    args.append(nc.dram_tensor("out", (1, SEQ, D), F32, kind="ExternalOutput").ap())
    hybrid_trunk(nc, *args)
    got = run_bass_kernel_spmd(nc, [arrays], core_ids=[0])
    return got.results[0]["out"]
```

```python
import numpy as np
import concourse.bass as bass
from concourse import mybir
from contextlib import ExitStack

F32 = mybir.dt.float32
I32 = mybir.dt.int32
ALU = mybir.AluOpType
ACT = mybir.ActivationFunctionType
AX = mybir.AxisListType

P = 128
D = 1024
KD = D // P
SEQ, META = 512, 16
TOK = META + SEQ
NT = SEQ // P
LEVELS = 7
PADTOK = P + SEQ
NTP = NT + 1
NB, BW = 3, 512
NG, NE, HID = 4, 8, 256
NX = NG * NE
SLOTS = 64
EXTRA = 2 * SEQ // SLOTS
ROWS = (NX + EXTRA) * SLOTS
EPS = 1e-6
LN2 = float(np.log(2.0))

A_Q, A_F, A_I, A_G = 0, 512, 1024, 1536
B_QKV, B_BETA, B_DECAY, B_G = 2048, 3584, 3588, 3592
C_Q, C_K, C_V, C_GK, C_G = 4104, 4360, 4616, 5128, 5144
GATES = 5656

R_NORM, R_LB, R_AN, R_BN, R_CN, R_CONV, R_GKB = 0, 8, 12, 13, 14, 15, 63
NROWS = 65

K_ID, K_INC, K_STR, K_UP, K_LOW = 0, P, 2 * P, 3 * P, (3 + LEVELS) * P
K_RESET = (3 + 2 * LEVELS) * P
K_E64 = K_RESET + TOK
K_DESC = K_E64 + NX
K_J = K_DESC + NE
KCOLS = K_J + 16


def constants():
    c = np.zeros((P, KCOLS), np.float32)
    s, t = np.arange(P)[:, None], np.arange(P)[None, :]
    c[:, K_ID:K_ID + P] = s == t
    c[:, K_INC:K_INC + P] = s <= t
    c[:, K_STR:K_STR + P] = s < t
    for l in range(LEVELS):
        up = ((s ^ t) >> l == 1) & (s < t)
        c[:, K_UP + l * P:K_UP + (l + 1) * P] = up
        c[:, K_LOW + l * P:K_LOW + (l + 1) * P] = up.T
    n = np.arange(TOK)
    c[:, K_RESET:K_RESET + TOK] = ~((n == 0) | ((n >= META) & ((n - META) % P == 0)))
    c[:, K_E64:K_E64 + NX] = np.arange(NX) * SLOTS
    c[:, K_DESC:K_DESC + NE] = NE - np.arange(NE)
    c[:, K_J:K_J + 16] = np.arange(16)
    return c


class Steps:

    def __init__(self, sem, names, base=0):
        self.sem, self.names, self.at, self.base = sem, names, 0, base
        self.index = {n: k + 1 for k, n in enumerate(names)}
        assert len(self.index) == len(names)

    def after(self, name, i=0):
        return self.sem, i * len(self.names) + (self.base + self.index[name])

    def rounds(self, i):
        return self.sem, i * len(self.names) + self.base

    def begin(self, engine):
        engine.nop().then_inc(self.sem, self.base)

    def did(self, name):
        assert self.names[self.at % len(self.names)] == name, (name, self.names[self.at % len(self.names)])
        self.at += 1
        return self.sem, 1


def gla_names(kind):
    nh = 1 if kind == "a" else 2
    sub = range(nh)
    lv = range(LEVELS)
    if kind == "a":
        pe = ["f", "q", "g0", "v"]
        act = ["sgk", "sgq", "sgg0", "v0", "vm", "ab", "e", "l", "ad", "e2", "l2"]
        dve = ["f", "k", "q", "g0", "ls", "dif", "mx", "lf", "b"]
    else:
        pe = ["k", "f", "q", "g0", "g1", "v"]
        act = ["sgg0", "sgg1", "v0", "v1", "vm", "ab", "e", "l"]
        dve = ["k", "f", "q", "g0", "g1", "ls", "lf", "b"]
    ngate = 2 * nh
    pe += [f"gd{s}" for s in sub]
    gate_at = {}
    for l in lv:
        pe += [f"gr{l}_{s}" for s in sub]
        if l == 0:
            pe += ["keT"]
        if l == 1:
            pe += ["kv"]
    pe += [f"o{s}" for s in sub] + [f"ss{s}" for s in sub]
    act += ["eb", "dec", "eke", "keTm", "keTr"]
    for l in lv:
        act += [f"xa{l}", f"xb{l}"]
    act += [f"sq{s}" for s in sub] + [x for s in sub for x in (f"ln{s}", f"ri{s}")]
    dve += ["dbm", "dbr", "d0", "qe", "ke"] + [f"Pd{s}" for s in sub]
    for l in lv:
        if l + 1 < LEVELS:
            dve += [f"d{l + 1}"]
        dve += [f"za{l}", f"zb{l}"]
        if l == 2:
            dve += ["S0", "S1", "S2", "S3"]
        if l:
            dve += [f"P{l - 1}_{s}" for s in sub]
    dve += [f"P{LEVELS - 1}_{s}" for s in sub]
    dve += [x for s in sub for x in (f"y1{s}", f"y{s}")]
    return nh, pe, act, dve


def hybrid_trunk(nc, x, meta_tokens, norm_mix, w_in, hgrn_lb_logits, hgrn_norm, gdn_conv, gdn_a_log,
                 gdn_dt_bias, gdn_norm, gla_gk_w2, gla_gk_b, gla_norm, w_branch, w_out, norm_ffn,
                 router_group_w, router_group_b, router_expert_w, router_expert_b,
                 expert_w_gate, expert_w_up, expert_w_down, norm_final, consts, out):
    ctx = ExitStack()
    with ctx:
        def sb(name, shape, dt=F32):
            return ctx.enter_context(nc.sbuf_tensor(name, shape, dt))

        sems = {}

        def sem(name):
            if name not in sems:
                sems[name] = ctx.enter_context(nc.semaphore(name))
            return sems[name]

        C = sb("C", [P, KCOLS])
        ident, inc, strict = C[:, K_ID:K_ID + P], C[:, K_INC:K_INC + P], C[:, K_STR:K_STR + P]
        reset = C[:, K_RESET:K_RESET + TOK]

        def up(l):
            return C[:, K_UP + l * P:K_UP + (l + 1) * P]

        def low(l):
            return C[:, K_LOW + l * P:K_LOW + (l + 1) * P]

        ones = sb("ones", [P, P])
        spare = sb("spare", [P, 24])
        spare_at = [0]

        def next_spare():
            spare_at[0] = (spare_at[0] + 1) % 24
            return spare[:, spare_at[0]:spare_at[0] + 1]
        col = sb("col", [P, 16])
        one_c, eps_c, zero_c = col[:, 0:1], col[:, 1:2], col[:, 2:3]
        rowsT = sb("rowsT", [P, NROWS])
        gates = sb("gates", [P, NB * KD, SEQ])
        yT = sb("yT", [P, NB * BW // P, SEQ])
        ARENA = 29500
        arena = sb("arena", [P, ARENA])
        uT = arena[:, 0:KD * TOK].rearrange("p (k t) -> p k t", k=KD)
        o = KD * TOK
        wseg = arena[:, o:o + 6 * KD * P].rearrange("p (s k c) -> p s k c", s=6, k=KD)
        o += 6 * KD * P
        wgt = arena[:, o:o + 4 * KD * P].rearrange("p (s k c) -> p s k c", s=4, k=KD)
        o += 4 * KD * P
        WORK = o

        class Area:

            def __init__(self, at, end=ARENA):
                self.at, self.end = at, end

            def take(self, n):
                self.at += n
                assert self.at <= self.end, (self.at, self.end)
                return arena[:, self.at - n:self.at]

        ps = ctx.enter_context(nc.psum_tensor("ps", [P, 8 * 512], F32))

        def bank(n, w=512):
            return ps[:, n * 512:n * 512 + w]

        def slot(n):
            return ps[:, n * 1024 + 496:n * 1024 + 1024]

        def over(ap, n):
            return ap.unsqueeze(1).broadcast_to([ap.shape[0], n, ap.shape[1]])

        def tiles(ap, n=NT):
            return ap.rearrange("p (n t) -> p n t", n=n)

        xs_dram = nc.dram_tensor("sorted_tokens", [ROWS, D], F32).ap()
        ys_dram = nc.dram_tensor("sorted_results", [ROWS, D], F32).ap()

        block = ctx.enter_context(nc.Block())
        programs = {e: [] for e in ("sync", "scalar", "vector", "tensor", "gpsimd")}

        w0 = Area(WORK)
        xt = gates[:, 0:2 * NT, :].rearrange("p (i a) t -> p i (a t)", a=2)
        xm = gates[0:META, 8:10, :].rearrange("p a t -> p (a t)")
        rowsb = gates[0:NROWS, 10, 0:P]
        scr = gates[:, 12:14, :].rearrange("p a t -> p (a t)")
        zeros = gates[:, 14:22, :].rearrange("p a t -> p (a t)")
        ssq = col[:, 3:8]
        small_w = w0.take(KD * 24).rearrange("p (k c) -> p k c", k=KD)
        gkw2 = sb("gkw2", [16, 2 * P])
        lbc = sb("lbc", [P, 16])
        bcol = sb("bcol", [P, 10 * 4 * NTP])
        gkT = sb("gkT", [16, TOK])

        pe0 = Steps(sem("setup_pe"), ["rows", "alb"] + [f"u{k}" for k in range(KD)] + ["small", "gkT", "gcol"])
        act0 = Steps(sem("setup_act"), ["ln", "rs", "lb1", "lb2", "am", "sgm", "ab", "e", "l", "ea", "gk", "eg", "egl", "ekd"])
        dve0 = Steps(sem("setup_dve"), ["ones", "c1", "c2", "c3", "zero", "rows"] +
                     [f"sq{i}" for i in range(5)] + ["ms"] + [f"ut{i}" for i in range(5)] +
                     [f"u{k}" for k in range(KD)] +
                     ["lbm", "lbs", "lb", "om", "lbf", "lnf", "pad", "sm", "smm", "dt", "beta", "sp", "nea", "la0", "gkm", "g", "gl", "bg", "dk"])

        def setup_sync(sp):
            sp.dma_start(xt, x[0].rearrange("(i p) d -> p i d", p=P)).then_inc(sem("x_loaded"), 16)
            sp.dma_start(xm, meta_tokens).then_inc(sem("x_loaded"), 16)
            sp.dma_start(C[:, :], consts).then_inc(sem("consts_loaded"), 16)
            for at, src in ((R_NORM, norm_mix[0].rearrange("(a b) -> a b", b=P)),
                            (R_LB, hgrn_lb_logits[0].rearrange("(a b) -> a b", b=P)),
                            (R_AN, hgrn_norm), (R_BN, gdn_norm), (R_CN, gla_norm),
                            (R_CONV, gdn_conv[0].rearrange("j (c b) -> (j c) b", b=P)),
                            (R_GKB, gla_gk_b[0].rearrange("(a b) -> a b", b=P))):
                sp.dma_start(rowsb[at:at + src.shape[0], :], src).then_inc(sem("rows_loaded"), 16)
            wv = w_in[0].rearrange("(k p) c -> p k c", p=P)
            sp.dma_start(small_w[:, :, 0:8], wv[:, :, B_BETA:B_BETA + 8]).then_inc(sem("small_loaded"), 16)
            sp.dma_start(small_w[:, :, 8:24], wv[:, :, C_GK:C_GK + 16]).then_inc(sem("small_loaded"), 16)
            sp.dma_start(gkw2[:, :], gla_gk_w2[0]).then_inc(sem("small_loaded"), 16)
            sp.dma_start(bcol[:, 0:4], gdn_a_log[0:1, :].broadcast_to([P, 4])).then_inc(sem("small_loaded"), 16)
            sp.dma_start(bcol[:, 4:8], gdn_dt_bias[0:1, :].broadcast_to([P, 4])).then_inc(sem("small_loaded"), 16)

        def bq(n):
            return bcol[:, 8 + n * 20:8 + (n + 1) * 20]
        q_dec, q_beta, q_la, q_g, q_gl, q_eg, q_bg, q_egl = (bq(n) for n in range(8))
        q_kd = bq(8)

        def setup_vector(v):
            v.memset(ones[:, :], 1.0).then_inc(*dve0.did("ones"))
            v.memset(one_c, 1.0).then_inc(*dve0.did("c1"))
            v.memset(eps_c, EPS).then_inc(*dve0.did("c2"))
            v.memset(ssq, 1.0).then_inc(*dve0.did("c3"))
            v.memset(zeros, 0.0).then_inc(*dve0.did("zero"))
            v.wait_ge(*pe0.after("rows"))
            v.tensor_copy(rowsT[:, :], bank(0, NROWS)).then_inc(*dve0.did("rows"))
            v.wait_ge(sem("x_loaded"), 32)
            v.wait_ge(*dve0.after("zero"))
            for i in range(5):
                src = xt[:, i, :] if i < NT else xm
                r = src.shape[0]
                if i:
                    v.wait_ge(*dve0.after(f"sq{i - 1}"))
                v.tensor_tensor_reduce(scr[0:r], src, src, 1.0, 0.0, ALU.mult, ALU.add,
                                       accum_out=ssq[0:r, i:i + 1]).then_inc(*dve0.did(f"sq{i}"))
            v.wait_ge(*dve0.after("sq4"))
            v.tensor_scalar(ssq, ssq, 1.0 / D, EPS, ALU.mult, ALU.add).then_inc(*dve0.did("ms"))
            v.wait_ge(*act0.after("rs"))
            for i in range(5):
                src = xt[:, i, :] if i < NT else xm
                r = src.shape[0]
                v.tensor_scalar(src, src, ssq[0:r, i:i + 1], None, ALU.mult).then_inc(*dve0.did(f"ut{i}"))
            v.wait_ge(*dve0.after("rows"))
            for k in range(KD):
                v.wait_ge(*pe0.after(f"u{k}"))
                v.tensor_scalar(uT[:, k, :], slot(k % 2), rowsT[:, R_NORM + k:R_NORM + k + 1], None,
                                ALU.mult).then_inc(*dve0.did(f"u{k}"))
            lg = rowsT[:, R_LB:R_LB + 4]
            v.tensor_tensor(lbc[:, 0:4], lg, lg, ALU.subtract).then_inc(*dve0.did("lbm"))
            v.wait_ge(*act0.after("lb1"))
            v.reciprocal(lbc[:, 8:12], lbc[:, 4:8]).then_inc(*dve0.did("lbs"))
            v.wait_ge(*dve0.after("lbs"))
            v.tensor_tensor(lbc[:, 4:8], lbc[:, 4:8], lbc[:, 8:12], ALU.mult).then_inc(*dve0.did("lb"))
            v.wait_ge(*dve0.after("lb"))
            v.tensor_tensor(lbc[:, 8:12], lbc[:, 4:8], lbc[:, 4:8], ALU.subtract).then_inc(*dve0.did("om"))
            v.wait_ge(*dve0.after("om"))
            v.tensor_scalar(lbc[:, 0:4], lbc[:, 8:12], -1.0, 1.0, ALU.mult, ALU.add).then_inc(*dve0.did("lbf"))
            v.tensor_scalar(lbc[:, 8:12], lbc[:, 8:12], 1e-30, 2.0 ** 50, ALU.max, ALU.mult).then_inc(*dve0.did("lnf"))
            v.memset(bcol[:, 8:], 0.0).then_inc(*dve0.did("pad"))
            v.wait_ge(*pe0.after("small"))
            v.wait_ge(*dve0.after("pad"))
            v.wait_ge(sem("valid_set"), 4)
            bt = bank(4, NT * 24).rearrange("p (t c) -> p t c", t=NT)
            bm = bank(5, 24)[0:META]
            v.tensor_copy(small_t[:, 1:, :], bt).then_inc(*dve0.did("sm"))
            v.tensor_copy(small_t[0:META, 0, :], bm).then_inc(*dve0.did("smm"))
            v.wait_ge(sem("small_loaded"), 80)
            v.wait_ge(*dve0.after("smm"))
            dec5 = q_dec.rearrange("p (t h) -> p t h", t=NTP)
            v.tensor_tensor(dec5, small_t[:, :, 4:8], over(bcol[:, 4:8], NTP), ALU.add).then_inc(*dve0.did("dt"))
            v.wait_ge(*act0.after("sgm"))
            v.wait_ge(*dve0.after("pad"))
            b5 = q_beta.rearrange("p (t h) -> p t h", t=NTP)
            sg5 = q_eg.rearrange("p (t h) -> p t h", t=NTP)
            v.tensor_copy(b5, sg5).then_inc(*dve0.did("beta"))
            v.wait_ge(*act0.after("l"))
            v.scalar_tensor_tensor(q_dec, q_dec, 0.0, q_la, ALU.max, ALU.add).then_inc(*dve0.did("sp"))
            v.wait_ge(*act0.after("ea"))
            v.wait_ge(*dve0.after("sp"))
            v.scalar_tensor_tensor(dec5, dec5, -1.0, over(bcol[:, 0:4], NTP), ALU.mult, ALU.mult).then_inc(*dve0.did("nea"))
            v.wait_ge(*dve0.after("nea"))
            v.tensor_tensor(q_la, q_dec, valid[:, :], ALU.mult).then_inc(*dve0.did("la0"))
            v.wait_ge(*dve0.after("beta"))
            v.tensor_tensor(q_beta, q_beta, valid[:, :], ALU.mult).then_inc(*dve0.did("gkm"))

        small_t = sb("small_t", [P, NTP, 24])
        valid = sb("valid", [P, 20])

        def setup_gpsimd(g):
            g.memset(valid[:, :], 1.0).then_inc(sem("valid_set"), 1)
            g.memset(small_t[:, 0, :], 0.0).then_inc(sem("valid_set"), 1)
            g.wait_ge(sem("valid_set"), 1)
            g.memset(valid[:, 0:4], 0.0).then_inc(sem("valid_set"), 1)
            g.wait_ge(sem("valid_set"), 3)
            g.memset(valid[0:META, 0:4], 1.0).then_inc(sem("valid_set"), 1)
            g.wait_ge(*dve0.after("zero"))
            g.wait_ge(*pe0.after("gkT"))
            n = ROWS * D // P // 4096
            xz = xs_dram.rearrange("(p r) d -> p (r d)", p=P)
            for c in range(0, ROWS * D // P, 4096):
                w = min(4096, ROWS * D // P - c)
                g.dma_start(xz[:, c:c + w], zeros[:, 0:w]).then_inc(sem("rows_zeroed"), 16)
            yz = ys_dram[NX * SLOTS:, :].rearrange("(p r) d -> p (r d)", p=P)
            for c in range(0, EXTRA * SLOTS * D // P, 4096):
                g.dma_start(yz[:, c:c + 4096], zeros[:, 0:4096]).then_inc(sem("rows_zeroed"), 16)
        n_zero = -(-(ROWS * D // P) // 4096) + EXTRA * SLOTS * D // P // 4096

        def setup_scalar(a):
            a.wait_ge(*dve0.after("ms"))
            a.activation(ssq, ssq, ACT.Ln).then_inc(*act0.did("ln"))
            a.wait_ge(*act0.after("ln"))
            a.activation(ssq, ssq, ACT.Exp, scale=-0.5).then_inc(*act0.did("rs"))
            a.wait_ge(*dve0.after("lbm"))
            a.activation(lbc[:, 4:8], lbc[:, 0:4], ACT.Exp).then_inc(*act0.did("lb1"))
            a.wait_ge(*dve0.after("lnf"))
            a.activation(lbc[:, 8:12], lbc[:, 8:12], ACT.Ln).then_inc(*act0.did("lb2"))
            a.activation(lbc[:, 4:8], lbc[:, 0:4], ACT.Ln).then_inc(*act0.did("am"))
            a.wait_ge(*dve0.after("smm"))
            a.wait_ge(sem("valid_set"), 4)
            a.activation(q_eg.rearrange("p (t h) -> p t h", t=NTP), small_t[:, :, 0:4], ACT.Sigmoid).then_inc(*act0.did("sgm"))
            a.wait_ge(*dve0.after("dt"))
            a.activation(q_la, q_dec, ACT.Abs).then_inc(*act0.did("ab"))
            a.wait_ge(*act0.after("ab"))
            a.activation(q_la, q_la, ACT.Exp, scale=-1.0).then_inc(*act0.did("e"))
            a.wait_ge(*act0.after("e"))
            a.activation(q_la, q_la, ACT.Ln, bias=one_c).then_inc(*act0.did("l"))
            a.activation(bcol[:, 0:4], bcol[:, 0:4], ACT.Exp).then_inc(*act0.did("ea"))
            a.wait_ge(*pe0.after("gkT"))
            a.activation(gkT[:, :], slot(1)[0:16], ACT.Copy).then_inc(*act0.did("gk"))

        def setup_tensor(t):
            t.wait_ge(sem("consts_loaded"), 16)
            t.wait_ge(sem("rows_loaded"), 16 * 7)
            t.transpose(bank(0, NROWS), rowsb, ident[0:NROWS, 0:NROWS]).then_inc(*pe0.did("rows"))
            t.wait_ge(*dve0.after("ut4"))
            t.wait_ge(*dve0.after("rows"))
            t.nop().then_inc(*pe0.did("alb"))
            for k in range(KD):
                if k >= 2:
                    t.wait_ge(*dve0.after(f"u{k - 2}"))
                s = slot(k % 2)
                t.transpose(s[:, 0:META], xm[:, k * P:(k + 1) * P], ident[0:META, 0:META])
                for i in range(NT):
                    mm = t.transpose(s[:, META + i * P:META + (i + 1) * P], xt[:, i, k * P:(k + 1) * P], ident)
                mm.then_inc(*pe0.did(f"u{k}"))
            t.wait_ge(*dve0.after(f"u{KD - 1}"))
            t.wait_ge(sem("small_loaded"), 80)
            for i in range(NTP):
                dst = bank(5, 24)[0:META] if i == 0 else ps[:, 4 * 512 + (i - 1) * 24:4 * 512 + i * 24]
                lo = 0 if i == 0 else META + (i - 1) * P
                w = META if i == 0 else P
                for k in range(KD):
                    mm = t.matmul(dst, uT[:, k, lo:lo + w], small_w[:, k, :], start=(k == 0), stop=(k == KD - 1))
            mm.then_inc(*pe0.did("small"))
            t.wait_ge(*dve0.after("smm"))
            s = slot(1)
            t.transpose(s[0:16, 0:META], small_t[0:META, 0, 8:24], ident[0:META, 0:META])
            for i in range(NT):
                mm = t.transpose(s[0:16, META + i * P:META + (i + 1) * P], small_t[:, i + 1, 8:24], ident)
            mm.then_inc(*pe0.did("gkT"))
            t.wait_ge(*act0.after("gk"))

        for e, f in (("sync", setup_sync), ("scalar", setup_scalar), ("vector", setup_vector),
                     ("tensor", setup_tensor), ("gpsimd", setup_gpsimd)):
            programs[e].append(f)

        def decays(banks_read):
            def tensor(t):
                t.wait_ge(*banks_read)
                t.wait_ge(*dve0.after("gkm"))
                t.wait_ge(*dve0.after("ones"))
                t.matmul(bank(6, 20), inc, q_la, start=True, stop=True)
                t.matmul(bank(7, 20), ones[:, :], q_la, start=True, stop=True).then_inc(*pe0.did("gcol"))
                t.wait_ge(*dve0.after("gl"))

            def vector(v):
                v.wait_ge(*pe0.after("gcol"))
                v.tensor_copy(q_g, bank(6, 20)).then_inc(*dve0.did("g"))
                v.tensor_copy(q_gl, bank(7, 20)).then_inc(*dve0.did("gl"))
                v.wait_ge(*act0.after("egl"))
                v.wait_ge(*dve0.after("gl"))
                v.tensor_tensor(q_bg, q_beta, q_eg, ALU.mult).then_inc(*dve0.did("bg"))
                v.tensor_tensor(q_kd, q_gl, q_g, ALU.subtract).then_inc(*dve0.did("dk"))

            def scalar(a):
                a.wait_ge(*dve0.after("gl"))
                a.activation(q_eg, q_g, ACT.Exp).then_inc(*act0.did("eg"))
                a.activation(q_egl, q_gl, ACT.Exp).then_inc(*act0.did("egl"))
                a.wait_ge(*dve0.after("dk"))
                a.activation(q_kd, q_kd, ACT.Exp).then_inc(*act0.did("ekd"))

            for e, f in (("scalar", scalar), ("vector", vector), ("tensor", tensor)):
                programs[e].append(f)

        wv = w_in[0].rearrange("(k p) c -> p k c", p=P)

        def gla(kind, rounds, first_y, first_gate, earlier):
            nh, pe_n, act_n, dve_n = gla_names(kind)
            pe, act, dve = (Steps(sem(f"{kind}_{e}"), n, 1) for e, n in (("pe", pe_n), ("act", act_n), ("dve", dve_n)))
            segs = ["f", "q", "g0", "v"] if kind == "a" else ["k", "q", "g0", "g1", "v"]
            ngate = 2 * nh
            gate_pe = Steps(sem(f"{kind}_gate_pe"), [f"t{n}" for n in range(ngate)], 1)
            gate_ev = Steps(sem(f"{kind}_gate_evac"), [f"t{n}" for n in range(ngate)], 1)
            w = Area(WORK)
            fb, k_, b_, lf, tmp, eke = (w.take(TOK) for _ in range(6))
            q_, eb, qe = (w.take(SEQ) for _ in range(3))
            g_ = [w.take(SEQ) for _ in range(nh)]
            db = w.take(TOK)
            sg = w.take(SEQ)
            dd = [w.take(SEQ) for _ in range(2)]
            ee = [w.take(SEQ) for _ in range(2)]
            zz = [w.take(SEQ) for _ in range(2)]
            pm = [w.take(SEQ) for _ in range(nh)]
            vt = [w.take(SEQ) for _ in range(nh)]
            vm = w.take(nh * P)[0:META]
            kt = tiles(w.take(NT * P))
            st = tiles(w.take(NT * P))
            dec = w.take(NT)
            sq, ri = eb, sg
            offs = {"a": {"f": (A_F, P), "q": (A_Q, P), "g0": (A_G, P), "v": (A_I, P)},
                    "c": {"k": (C_K, P), "q": (C_Q, P), "g0": (C_G, 2 * P), "g1": (C_G + P, 2 * P),
                          "v": (C_V, 2 * P)}}[kind]
            wi = {s: n for n, s in enumerate(segs)}
            KH = P // nh

            def sync(sp):
                def load(seg, i):
                    at, step = offs[seg]
                    n = nh if seg == "v" else 1
                    for c in range(n):
                        sp.dma_start(wseg[:, wi[seg] + c, :, :], wv[:, :, bass.ds(i * step + at + c * P, P)]
                                     if not isinstance(i, int) else wv[:, :, i * step + at + c * P:i * step + at + (c + 1) * P]
                                     ).then_inc(sem(f"{kind}_w_{seg}"), 16)

                def load_gate(n, i):
                    at = i * (ngate * P) + GATES + (first_gate + n) * P
                    src = wv[:, :, at:at + P] if isinstance(at, int) else wv[:, :, bass.ds(at, P)]
                    sp.dma_start(wgt[:, n, :, :], src).then_inc(sem(f"{kind}_wgate{n}"), 16)
                for q in earlier:
                    sp.wait_ge(*q)
                for s in segs:
                    load(s, 0)
                for n in range(ngate):
                    load_gate(n, 0)
                with sp.Fori(1, rounds, 1) as i:
                    for s in (["q", "f", "g0", "v"] if kind == "a" else segs):
                        sp.wait_ge(*pe.after(s, i - 1))
                        load(s, i)
                    for n in range(ngate):
                        sp.wait_ge(*gate_pe.after(f"t{n}", i - 1))
                        load_gate(n, i)

            def tensor(t):
                pe.begin(t)
                gate_pe.begin(t)
                gates_left = []

                def project(seg, i, n):
                    t.wait_ge(sem(f"{kind}_w_{seg}"), i * 16 + 16)
                    s = slot(n)
                    for k in range(KD):
                        t.matmul(s[:, META:], wseg[:, wi[seg], k, :], uT[:, k, META:], start=(k == 0), stop=(k == KD - 1))
                        mm = t.matmul(s[:, 0:META], wseg[:, wi[seg], k, :], uT[:, k, 0:META], start=(k == 0), stop=(k == KD - 1))
                    mm.then_inc(*pe.did(seg))

                def gate_part(i, steps):
                    for _ in range(steps):
                        if not gates_left:
                            return
                        n, k = gates_left.pop(0)
                        if k == 0:
                            t.wait_ge(sem(f"{kind}_wgate{n}"), i * 16 + 16)
                            if n >= 2:
                                t.wait_ge(*gate_ev.after(f"t{n - 2}", i))
                            elif n == 0:
                                t.wait_ge(*dve.after(f"g{nh - 1}", i))
                        mm = t.matmul(bank(1 + 2 * (n % 2)), wgt[:, n, k, :], uT[:, k, META:],
                                      start=(k == 0), stop=(k == KD - 1))
                        if k == KD - 1:
                            mm.then_inc(*gate_pe.did(f"t{n}"))

                for q in earlier:
                    t.wait_ge(*q)
                with t.Fori(0, rounds, 1) as i:
                    gates_left.extend((n, k) for n in range(ngate) for k in range(KD))
                    if kind == "a":
                        t.wait_ge(*gate_ev.rounds(i))
                        project("f", i, 0)
                        project("q", i, 1)
                        t.wait_ge(*dve.after("f", i))
                        project("g0", i, 0)
                    else:
                        t.wait_ge(*gate_ev.rounds(i))
                        project("k", i, 0)
                        t.wait_ge(sem("c_w2"), i + 1)
                        s = slot(1)
                        for lo, n in ((META, SEQ), (0, META)):
                            mm = t.matmul(s[:, lo:lo + n], w2pad(i), gkT[:, lo:lo + n], start=True, stop=True)
                        mm.then_inc(*pe.did("f"))
                        t.wait_ge(*dve.after("k", i))
                        project("q", i, 0)
                        t.wait_ge(*dve.after("f", i))
                        project("g0", i, 1)
                        t.wait_ge(*dve.after("q", i))
                        project("g1", i, 0)
                    t.wait_ge(sem(f"{kind}_w_v"), i * 16 * nh + 16 * nh)
                    t.wait_ge(*dve.rounds(i))
                    for s in range(nh):
                        for c in range(NTP):
                            lo, n = (0, META) if c == 0 else (META + (c - 1) * P, P)
                            dst = bank(6)[0:META, s * P:(s + 1) * P] if c == 0 else bank(4 + s)[:, (c - 1) * P:c * P]
                            for k in range(KD):
                                mm = t.matmul(dst, uT[:, k, lo:lo + n], wseg[:, wi["v"] + s, k, :],
                                              start=(k == 0), stop=(k == KD - 1))
                    mm.then_inc(*pe.did("v"))
                    gate_part(i, 4 * nh)
                    gb = 0

                    def gram(name, lhs, rhs, free):
                        nonlocal gb
                        t.wait_ge(*free)
                        for c in range(NT):
                            mm = t.matmul(bank(4 + gb % 2)[:, c * P:(c + 1) * P], lhs[:, c * P:(c + 1) * P],
                                          rhs[:, c * P:(c + 1) * P], start=True, stop=True)
                        mm.then_inc(*pe.did(name))
                        gb += 1
                    order = [f"Pd{s}" for s in range(nh)] + [f"P{l}_{s}" for l in range(LEVELS) for s in range(nh)]

                    def free():
                        return act.after("vm", i) if gb < 2 else dve.after(order[gb - 2], i)
                    t.wait_ge(*dve.after("k" if kind == "a" else "f", i))
                    t.wait_ge(*dve.after("q", i))
                    for s in range(nh):
                        gram(f"gd{s}", k_[s * KH:(s + 1) * KH, META:], q_[s * KH:(s + 1) * KH], free())
                    for l in range(LEVELS):
                        gate_part(i, 2 * nh)
                        t.wait_ge(*dve.after(f"zb{l}", i))
                        for s in range(nh):
                            z = zz[l % 2][s * KH:(s + 1) * KH]
                            gram(f"gr{l}_{s}", z, z, free())
                        if l == 0:
                            t.wait_ge(*dve.after("ke", i))
                            t.transpose(bank(6)[0:META, 0:P], eke[:, 0:META], ident)
                            for c in range(1, NT):
                                lo = META + (c - 1) * P
                                mm = t.transpose(bank(6)[:, c * P:(c + 1) * P], eke[:, lo:lo + P], ident)
                            mm.then_inc(*pe.did("keT"))
                        if l == 1:
                            t.wait_ge(*act.after("keTr", i))
                            for c in range(NT):
                                for s in range(nh):
                                    lhs = kt[0:META, 0, s * KH:(s + 1) * KH] if c == 0 else kt[:, c, s * KH:(s + 1) * KH]
                                    rhs = vm[:, s * P:(s + 1) * P] if c == 0 else vt[s][:, (c - 1) * P:c * P]
                                    mm = t.matmul(bank(7)[s * KH:(s + 1) * KH, c * P:(c + 1) * P], lhs, rhs,
                                                  start=True, stop=True)
                            mm.then_inc(*pe.did("kv"))
                    gate_part(i, 100)
                    t.wait_ge(*dve.after(f"P{LEVELS - 1}_{nh - 1}", i))
                    for s in range(nh):
                        for c in range(NT):
                            cs = slice(c * P, (c + 1) * P)
                            ks = slice(s * KH, (s + 1) * KH)
                            t.matmul(bank(6 + s)[:, cs], st[ks, c, :], qe[ks, cs], start=True, stop=False)
                            mm = t.matmul(bank(6 + s)[:, cs], vt[s][:, cs], pm[s][:, cs], start=False, stop=True)
                        mm.then_inc(*pe.did(f"o{s}"))
                    for s in range(nh):
                        t.wait_ge(*act.after(f"sq{s}", i))
                        t.matmul(bank(4 + s), ones[:, :], sqs[s], start=True, stop=True).then_inc(*pe.did(f"ss{s}"))

            def w2pad(i):
                return gkw2s[:, :]

            def scalar(a):
                act.begin(a)
                gate_ev.begin(a)
                for q in earlier:
                    a.wait_ge(*q)
                with a.Fori(0, rounds, 1) as i:
                    a.wait_ge(*dve.rounds(i))
                    if kind == "a":
                        a.wait_ge(*dve.after("f", i))
                        a.activation(tmp, fb, ACT.Sigmoid, scale=-1.0).then_inc(*act.did("sgk"))
                        a.wait_ge(*pe.after("q", i))
                        a.activation(sg, slot(1)[:, META:], ACT.Sigmoid).then_inc(*act.did("sgq"))
                        a.wait_ge(*pe.after("g0", i))
                        a.activation(eb, slot(0)[:, META:], ACT.Sigmoid).then_inc(*act.did("sgg0"))
                    else:
                        a.wait_ge(*pe.after("g0", i))
                        a.activation(sg, slot(1)[:, META:], ACT.Sigmoid).then_inc(*act.did("sgg0"))
                        a.wait_ge(*pe.after("g1", i))
                        a.activation(eb, slot(0)[:, META:], ACT.Sigmoid).then_inc(*act.did("sgg1"))
                    a.wait_ge(*pe.after("v", i))
                    for s in range(nh):
                        a.activation(vt[s], bank(4 + s), ACT.Copy).then_inc(*act.did(f"v{s}"))
                    a.activation(vm, bank(6, nh * P)[0:META], ACT.Copy).then_inc(*act.did("vm"))
                    a.preload_act_table_set("natural_log_exp_and_others")
                    if kind == "a":
                        a.wait_ge(*dve.after("k", i))
                    else:
                        a.wait_ge(*dve.after("f", i))
                    a.activation(tmp, fb, ACT.Abs).then_inc(*act.did("ab"))
                    a.wait_ge(*act.after("ab", i))
                    a.activation(tmp, tmp, ACT.Exp, scale=-1.0).then_inc(*act.did("e"))
                    a.wait_ge(*act.after("e", i))
                    a.activation(tmp, tmp, ACT.Ln, bias=one_c).then_inc(*act.did("l"))
                    if kind == "a":
                        a.wait_ge(*dve.after("dif", i))
                        a.activation(tmp, lf, ACT.Abs).then_inc(*act.did("ad"))
                        a.wait_ge(*act.after("ad", i))
                        a.activation(tmp, tmp, ACT.Exp, scale=-1.0).then_inc(*act.did("e2"))
                        a.wait_ge(*act.after("e2", i))
                        a.activation(tmp, tmp, ACT.Ln, bias=one_c).then_inc(*act.did("l2"))
                    a.wait_ge(*dve.after("b", i))
                    a.activation(eb, b_[:, META:], ACT.Exp).then_inc(*act.did("eb"))
                    a.activation(dec, b_[:, META + P - 1::P], ACT.Exp).then_inc(*act.did("dec"))
                    a.wait_ge(*dve.after("dbr", i))
                    a.activation(eke[:, 0:TOK - P], db[:, 0:TOK - P], ACT.Exp, scale=-1.0).then_inc(*act.did("eke"))

                    def level(l):
                        h = 1 << l
                        d5 = dd[l % 2].rearrange("p (n a h) -> p n a h", a=2, h=h)
                        e5 = ee[l % 2].rearrange("p (n a h) -> p n a h", a=2, h=h)
                        a.wait_ge(*dve.after(f"d{l}", i))
                        if l >= 2:
                            a.wait_ge(*dve.after(f"zb{l - 2}", i))
                        a.activation(e5[:, :, 0, :], d5[:, :, 0, :], ACT.Exp, scale=-1.0).then_inc(*act.did(f"xa{l}"))
                        a.activation(e5[:, :, 1, :], d5[:, :, 1, :], ACT.Exp).then_inc(*act.did(f"xb{l}"))
                    for l in range(LEVELS):
                        if l == ACT_KET:
                            a.wait_ge(*pe.after("keT", i))
                            a.activation(kt[0:META, 0, :], bank(6)[0:META, 0:P], ACT.Copy).then_inc(*act.did("keTm"))
                            a.activation(kt[:, 1:, :], tiles(bank(6))[:, 1:, :], ACT.Copy).then_inc(*act.did("keTr"))
                        level(l)
                        if l >= 3:
                            for n in range((l - 3) * ngate // 4, (l - 2) * ngate // 4):
                                a.wait_ge(*gate_pe.after(f"t{n}", i))
                                a.activation(gates[:, i * ngate + (first_gate + n), :], bank(1 + 2 * (n % 2)),
                                             ACT.Copy).then_inc(*gate_ev.did(f"t{n}"))
                    for s in range(nh):
                        a.wait_ge(*pe.after(f"o{s}", i))
                        a.activation(sqs[s], bank(6 + s), ACT.Square).then_inc(*act.did(f"sq{s}"))
                    for s in range(nh):
                        a.wait_ge(*pe.after(f"ss{s}", i))
                        a.activation(ris[s], bank(4 + s), ACT.Ln, bias=eps_c, scale=1.0 / P).then_inc(*act.did(f"ln{s}"))
                        a.wait_ge(*act.after(f"ln{s}", i))
                        a.activation(ris[s], ris[s], ACT.Exp, scale=-0.5).then_inc(*act.did(f"ri{s}"))

            sqs = [dd[0], dd[1]]
            ris = [ee[0], ee[1]]
            ACT_KET = 2
            fixed = [n for n in act_n if n not in ("keTm", "keTr")]
            at = fixed.index(f"xa{ACT_KET}")
            act.names = fixed[:at] + ["keTm", "keTr"] + fixed[at:]
            act.index = {n: k + 1 for k, n in enumerate(act.names)}
            gkw2s = sb("gkw2s", [16, P]) if kind == "c" else None

            def vector(v):
                dve.begin(v)
                def tt(name, out_, a_, b2, op):
                    v.tensor_tensor(out_, a_, b2, op).then_inc(*dve.did(name))

                with v.Fori(0, rounds, 1) as i:
                    if kind == "a":
                        v.wait_ge(*pe.after("f", i))
                        v.tensor_copy(fb, slot(0)).then_inc(*dve.did("f"))
                        v.wait_ge(*act.after("sgk", i))
                        v.tensor_scalar(k_, tmp, lbc[:, bass.ds(i, 1)], None, ALU.mult).then_inc(*dve.did("k"))
                        v.wait_ge(*act.after("sgq", i))
                        v.scalar_tensor_tensor(q_, slot(1)[:, META:], P ** -0.5, sg, ALU.mult, ALU.mult).then_inc(*dve.did("q"))
                        v.wait_ge(*act.after("sgg0", i))
                        v.tensor_tensor(g_[0], slot(0)[:, META:], eb, ALU.mult).then_inc(*dve.did("g0"))
                        v.wait_ge(*act.after("l", i))
                        v.scalar_tensor_tensor(fb, fb, 0.0, tmp, ALU.min, ALU.subtract).then_inc(*dve.did("ls"))
                        v.wait_ge(*dve.after("ls", i))
                        v.tensor_scalar(lf, fb, lbc[:, bass.ds(i + 4, 1)], lbc[:, bass.ds(i + 8, 1)],
                                        ALU.add, ALU.subtract).then_inc(*dve.did("dif"))
                        v.tensor_scalar(fb, fb, lbc[:, bass.ds(i + 4, 1)], lbc[:, bass.ds(i + 8, 1)],
                                        ALU.add, ALU.max).then_inc(*dve.did("mx"))
                        v.wait_ge(*act.after("l2", i))
                        v.wait_ge(*dve.after("mx", i))
                        tt("lf", lf, fb, tmp, ALU.add)
                    else:
                        v.wait_ge(*pe.after("k", i))
                        v.tensor_copy(k_, slot(0)).then_inc(*dve.did("k"))
                        v.wait_ge(*pe.after("f", i))
                        v.tensor_scalar(fb, slot(1), rowsT[:, bass.ds(i + R_GKB, 1)], None, ALU.add).then_inc(*dve.did("f"))
                        v.wait_ge(*pe.after("q", i))
                        v.tensor_scalar(q_, slot(0)[:, META:], KH ** -0.5, None, ALU.mult).then_inc(*dve.did("q"))
                        v.wait_ge(*act.after("sgg0", i))
                        tt("g0", g_[0], slot(1)[:, META:], sg, ALU.mult)
                        v.wait_ge(*act.after("sgg1", i))
                        tt("g1", g_[1], slot(0)[:, META:], eb, ALU.mult)
                        v.wait_ge(*act.after("l", i))
                        v.scalar_tensor_tensor(fb, fb, 0.0, tmp, ALU.min, ALU.subtract).then_inc(*dve.did("ls"))
                        v.wait_ge(*dve.after("ls", i))
                        v.tensor_scalar(lf, fb, 1.0 / 16.0, None, ALU.mult).then_inc(*dve.did("lf"))
                    v.wait_ge(*dve.after("lf", i))
                    v.tensor_tensor_scan(b_, reset, lf, 0.0, ALU.mult, ALU.add).then_inc(*dve.did("b"))
                    v.wait_ge(*dve.after("b", i))
                    tt("dbm", db[:, 0:META], b_[:, 0:META], b_[:, META - 1:META].broadcast_to([P, META]), ALU.subtract)
                    br = tiles(b_[:, META:])
                    tt("dbr", tiles(db[:, META:])[:, 0:NT - 1], br[:, 0:NT - 1],
                       br[:, 0:NT - 1, P - 1:P].broadcast_to([P, NT - 1, P]), ALU.subtract)

                    def diff(l):
                        h = 1 << l
                        n = SEQ // (2 * h)
                        bb = b_[:, META:].rearrange("p (n t) -> p n t", t=2 * h)
                        if l >= 2:
                            v.wait_ge(*act.after(f"xb{l - 2}", i))
                        tt(f"d{l}", dd[l % 2].rearrange("p (n t) -> p n t", t=2 * h), bb,
                           bb[:, :, h - 1:h].broadcast_to([P, n, 2 * h]), ALU.subtract)
                    diff(0)
                    v.wait_ge(*act.after("eb", i))
                    tt("qe", qe, q_, eb, ALU.mult)
                    v.wait_ge(*act.after("eke", i))
                    tt("ke", eke[:, 0:TOK - P], eke[:, 0:TOK - P], k_[:, 0:TOK - P], ALU.mult)
                    for s in range(nh):
                        v.wait_ge(*pe.after(f"gd{s}", i))
                        tt(f"Pd{s}", tiles(pm[s]), tiles(bank(4 + s % 2)), over(ident, NT), ALU.mult)
                    gb = nh

                    def pick(l):
                        nonlocal gb
                        for s in range(nh):
                            v.wait_ge(*pe.after(f"gr{l}_{s}", i))
                            v.wait_ge(*dve.after(f"Pd{s}" if l == 0 else f"P{l - 1}_{s}", i))
                            v.tensor_copy(next_spare(), one_c)
                            v.copy_predicated(tiles(pm[s]), over(up(l).bitcast(I32), NT), tiles(bank(4 + gb % 2))
                                              ).then_inc(*dve.did(f"P{l}_{s}"))
                            gb += 1
                    for l in range(LEVELS):
                        if l + 1 < LEVELS:
                            diff(l + 1)
                        h = 1 << l
                        view = "p (n a h) -> p n a h"
                        e5, z5 = (m[l % 2].rearrange(view, a=2, h=h) for m in (ee, zz))
                        k5, q5 = (m.rearrange(view, a=2, h=h) for m in (k_[:, META:], q_))
                        v.wait_ge(*act.after(f"xb{l}", i))
                        if l >= 2:
                            v.wait_ge(*pe.after(f"gr{l - 2}_{nh - 1}", i))
                        tt(f"za{l}", z5[:, :, 0, :], k5[:, :, 0, :], e5[:, :, 0, :], ALU.mult)
                        tt(f"zb{l}", z5[:, :, 1, :], q5[:, :, 1, :], e5[:, :, 1, :], ALU.mult)
                        if l == 2:
                            v.wait_ge(*pe.after("kv", i))
                            v.tensor_copy(st[:, 0, :], bank(7)[:, 0:P]).then_inc(*dve.did("S0"))
                            for c in range(1, NT):
                                v.wait_ge(*dve.after(f"S{c - 1}", i))
                                v.scalar_tensor_tensor(st[:, c, :], st[:, c - 1, :], dec[:, c - 1:c],
                                                       bank(7)[:, c * P:(c + 1) * P], ALU.mult, ALU.add
                                                       ).then_inc(*dve.did(f"S{c}"))
                        if l:
                            pick(l - 1)
                    pick(LEVELS - 1)
                    nw = {"a": R_AN, "c": R_CN}[kind]
                    for s in range(nh):
                        v.wait_ge(*act.after(f"ri{s}", i))
                        v.scalar_tensor_tensor(zz[s], bank(6 + s), rowsT[:, nw:nw + 1], ris[s], ALU.mult, ALU.mult
                                               ).then_inc(*dve.did(f"y1{s}"))
                        v.wait_ge(*dve.after(f"y1{s}", i))
                        tt(f"y{s}", yT[:, i * nh + (first_y + s), :], zz[s], g_[s], ALU.mult)

            def gpsimd(g):
                if kind == "c":
                    with g.Fori(0, rounds, 1) as i:
                        g.wait_ge(*pe.rounds(i))
                        g.wait_ge(sem("small_loaded"), 80)
                        g.tensor_copy(gkw2s[:, :], gkw2[:, bass.ds(i * P, P)]).then_inc(sem("c_w2"), 1)

            if kind == "c":
                plain = tensor

                def w2pad(i):
                    return gkw2s[:, :]
            for e, f in (("sync", sync), ("scalar", scalar), ("vector", vector), ("tensor", tensor), ("gpsimd", gpsimd)):
                programs[e].append(f)
            return pe, act, dve, gate_pe, gate_ev

        def delta(rounds, first_y, first_gate, earlier):
            LV = range(1, LEVELS)
            pe = Steps(sem("b_pe"), ["q", "k", "v", "g", "ssq", "ssk", "G", "B", "KK", "QK", "N", "kT", "vT"] +
                       [x for l in LV for x in ((f"Z{l}", f"EZ{l}", f"ZD{l}") if l < LEVELS - 1 else (f"Z{l}", f"EZ{l}"))] +
                       ["nw"] + [x for c in range(NTP) for x in ([f"V{c}"] + ([f"S{c}"] if c < NT else []))] + ["o", "ss"], 1)
            act = Steps(sem("b_act"), ["sq", "sk", "sv", "sg", "qq", "kk", "lq", "rq", "lk", "rk", "eg", "E", "N"] +
                        [f"Z{l}" for l in LV] + ["nw", "oo", "ln", "ri"], 1)
            dve = Steps(sem("b_dve"), [f"{s}{j}" for s in "qkv" for j in range(4)] +
                        [x for s in "qkv" for x in (f"{s}m", f"{s}r")] + ["g", "pad"] +
                        ["qn", "kn", "dif", "min", "kb", "Ei", "qg", "Es", "U", "QK", "Ua", "Ub", "kbg", "kd", "vb", "Da", "Db"] +
                        [x for l in LV for x in ((f"E{l}", f"D{l}") if l < LEVELS - 1 else (f"E{l}",))] +
                        [x for c in range(NTP) for x in ([f"V{c}"] + ([f"S{c}"] if c < NT else []))] + ["y1", "y"], 1)
            pool = Steps(sem("b_pool"), ["la", "be"], 1)
            gate_pe = Steps(sem("b_gate_pe"), ["t0", "t1"], 1)
            gate_ev = Steps(sem("b_gate_evac"), ["t0", "t1"], 1)
            w = Area(WORK)
            z_, kbg, kd, vb, vn, nwT, s_, n_, qf, kf, vf, kb, em, es, u_, d_, e_ = (w.take(PADTOK) for _ in range(17))
            g_, eg, qg, qk = (w.take(SEQ) for _ in range(4))
            conv = {"q": z_[:, 0:TOK], "k": kbg[:, 0:TOK], "v": kd[:, 0:TOK]}
            sig = vb[:, 0:TOK]
            feat = {"q": qf, "k": kf, "v": vf}
            sqb, rr, labc, bebc = vn, nwT, s_, n_
            segs = ["q", "k", "v", "g"]
            offs = {"q": B_QKV, "k": B_QKV + BW, "v": B_QKV + 2 * BW, "g": B_G}
            slots = {"q": 0, "k": 1, "v": 0, "g": 1}

            def t5(ap):
                return tiles(ap, NTP)

            def pair(n):
                return ps[:, n * 512:n * 512 + PADTOK]

            def head_col(q, i):
                return q.rearrange("p (t h) -> p t h", t=NTP)[:, :, bass.ds(i, 1)].broadcast_to([P, NTP, P])

            def sync(sp):
                def load(s, i):
                    at = i * P + offs[s]
                    src = wv[:, :, at:at + P] if isinstance(at, int) else wv[:, :, bass.ds(at, P)]
                    sp.dma_start(wseg[:, segs.index(s), :, :], src).then_inc(sem(f"b_w_{s}"), 16)

                def load_gate(n, i):
                    at = i * (2 * P) + GATES + (first_gate + n) * P
                    src = wv[:, :, at:at + P] if isinstance(at, int) else wv[:, :, bass.ds(at, P)]
                    sp.dma_start(wgt[:, n, :, :], src).then_inc(sem(f"b_wgate{n}"), 16)
                for q in earlier:
                    sp.wait_ge(*q)
                for s in segs:
                    load(s, 0)
                for n in range(2):
                    load_gate(n, 0)
                with sp.Fori(1, rounds, 1) as i:
                    for s in segs:
                        sp.wait_ge(*pe.after(s, i - 1))
                        load(s, i)
                    for n in range(2):
                        sp.wait_ge(*gate_pe.after(f"t{n}", i - 1))
                        load_gate(n, i)

            def gpsimd(g):
                pool.begin(g)
                for q in earlier:
                    g.wait_ge(*q)
                with g.Fori(0, rounds, 1) as i:
                    g.wait_ge(*dve.rounds(i))
                    g.wait_ge(*dve0.after("dk"))
                    g.tensor_copy(t5(labc), head_col(q_la, i)).then_inc(*pool.did("la"))
                    g.tensor_copy(t5(bebc), head_col(q_beta, i)).then_inc(*pool.did("be"))

            def tensor(t):
                pe.begin(t)
                gate_pe.begin(t)
                left = []

                def gate_part(i, steps):
                    for _ in range(steps):
                        if not left:
                            return
                        n, k = left.pop(0)
                        if k == 0:
                            t.wait_ge(sem(f"b_wgate{n}"), i * 16 + 16)
                            t.wait_ge(*dve.after("g", i))
                        mm = t.matmul(bank(1 + 2 * n), wgt[:, n, k, :], uT[:, k, META:], start=(k == 0), stop=(k == KD - 1))
                        if k == KD - 1:
                            mm.then_inc(*gate_pe.did(f"t{n}"))

                def each(name, dst, lhs, rhs, n=NTP, transpose=False):
                    for c in range(n):
                        cs = slice(c * P, (c + 1) * P)
                        if transpose:
                            mm = t.transpose(dst[:, cs], lhs[:, cs], ident)
                        else:
                            mm = t.matmul(dst[:, cs], lhs[:, cs], rhs[:, cs], start=True, stop=True)
                    mm.then_inc(*pe.did(name))

                for q in earlier:
                    t.wait_ge(*q)
                with t.Fori(0, rounds, 1) as i:
                    left.extend((n, k) for n in range(2) for k in range(KD))
                    t.wait_ge(*gate_ev.rounds(i))
                    for seg, free in (("q", None), ("k", dve.rounds(i)), ("v", dve.after("q3", i)), ("g", dve.after("k3", i))):
                        t.wait_ge(sem(f"b_w_{seg}"), i * 16 + 16)
                        if free:
                            t.wait_ge(*free)
                        s = slot(slots[seg])
                        for k in range(KD):
                            wt = wseg[:, segs.index(seg), k, :]
                            t.matmul(s[:, META:], wt, uT[:, k, META:], start=(k == 0), stop=(k == KD - 1))
                            mm = t.matmul(s[:, 0:META], wt, uT[:, k, 0:META], start=(k == 0), stop=(k == KD - 1))
                        mm.then_inc(*pe.did(seg))
                    for s, b in (("q", 4), ("k", 6)):
                        t.wait_ge(*act.after(s * 2, i))
                        src = sqb if s == "q" else kb
                        t.matmul(pair(b)[:, 0:512], ones[:, :], src[:, 0:512], start=True, stop=True)
                        t.matmul(pair(b)[:, 512:], ones[:, :], src[:, 512:], start=True, stop=True).then_inc(*pe.did("ss" + s))
                    t.wait_ge(*pool.after("la", i))
                    t.wait_ge(*act.after("lq", i))
                    for c in range(NTP):
                        mm = t.matmul(pair(4)[:, c * P:(c + 1) * P], labc[:, c * P:(c + 1) * P], inc, start=True, stop=True)
                    mm.then_inc(*pe.did("G"))
                    t.wait_ge(*pool.after("be", i))
                    t.wait_ge(*act.after("lk", i))
                    for c in range(NTP):
                        mm = t.matmul(pair(6)[:, c * P:(c + 1) * P], bebc[:, c * P:(c + 1) * P], ident, start=True, stop=True)
                    mm.then_inc(*pe.did("B"))
                    gate_part(i, 4)
                    t.wait_ge(*dve.after("kb", i))
                    t.wait_ge(*act.after("eg", i))
                    each("KK", pair(4), kf, kb)
                    each("QK", bank(6), kf[:, P:], qf[:, P:], NT)
                    gate_part(i, 1)
                    t.wait_ge(*dve.after("U", i))
                    each("N", pair(4), u_, None, transpose=True)
                    t.wait_ge(*dve.after("QK", i))
                    each("kT", pair(6), kf, None, transpose=True)
                    t.wait_ge(*dve.after("kd", i))
                    each("vT", pair(6), vf, None, transpose=True)
                    gate_part(i, 1)
                    for l in LV:
                        t.wait_ge(*dve.after("Db" if l == 1 else f"D{l - 1}", i))
                        each(f"Z{l}", pair(4), n_, e_)
                        gate_part(i, 1)
                        t.wait_ge(*act.after(f"Z{l}", i))
                        t.wait_ge(*dve.after("vb" if l == 1 else f"E{l - 1}", i))
                        each(f"EZ{l}", pair(6), d_, z_)
                        if l < LEVELS - 1:
                            each(f"ZD{l}", pair(4), z_, d_)
                        gate_part(i, 1)
                    gate_part(i, 100)
                    t.wait_ge(*dve.after(f"E{LEVELS - 1}", i))
                    each("nw", pair(4), kbg, e_)
                    t.wait_ge(*act.after("nw", i))
                    for c in range(NTP):
                        cs = slice(c * P, (c + 1) * P)
                        if c:
                            t.wait_ge(*dve.after(f"S{c - 1}", i))
                        vd = bank(4 + c % 2, P)
                        mm = t.matmul(vd, e_[:, cs], vb[:, cs], start=True, stop=(c == 0))
                        if c:
                            mm = t.matmul(vd, nwT[:, cs], s_[:, (c - 1) * P:c * P], start=False, stop=True)
                        mm.then_inc(*pe.did(f"V{c}"))
                        t.wait_ge(*dve.after(f"V{c}", i))
                        if c < NT:
                            t.matmul(bank(6 + c % 2, P), kd[:, cs], vn[:, cs], start=True, stop=True).then_inc(*pe.did(f"S{c}"))
                        if c:
                            os = slice((c - 1) * P, c * P)
                            t.matmul(bank(2)[:, os], s_[:, os], qg[:, os], start=True, stop=False)
                            mm = t.matmul(bank(2)[:, os], vn[:, cs], qk[:, os], start=False, stop=True)
                    mm.then_inc(*pe.did("o"))
                    t.wait_ge(*act.after("oo", i))
                    t.matmul(bank(4), ones[:, :], d_[:, 0:SEQ], start=True, stop=True).then_inc(*pe.did("ss"))

            def scalar(a):
                act.begin(a)
                gate_ev.begin(a)
                a.wait_ge(sem("rows_zeroed"), 16 * n_zero)
                a.wait_ge(*act0.after("ekd"))
                with a.Fori(0, rounds, 1) as i:
                    a.wait_ge(*dve.rounds(i))
                    for s in "qkv":
                        a.wait_ge(*dve.after(f"{s}3", i))
                        if s != "q":
                            a.wait_ge(*dve.after({"k": "qr", "v": "kr"}[s], i))
                        a.activation(sig, conv[s], ACT.Sigmoid).then_inc(*act.did(f"s{s}"))
                    a.wait_ge(*pe.after("g", i))
                    a.activation(eg, slot(1)[:, META:], ACT.Sigmoid).then_inc(*act.did("sg"))
                    a.wait_ge(*dve.after("pad", i))
                    a.activation(sqb, qf, ACT.Square).then_inc(*act.did("qq"))
                    a.activation(kb, kf, ACT.Square).then_inc(*act.did("kk"))
                    a.preload_act_table_set("natural_log_exp_and_others")
                    for s, b, dst in (("q", 4, rr), ("k", 6, em)):
                        a.wait_ge(*pe.after("ss" + s, i))
                        a.activation(dst, pair(b), ACT.Ln, bias=eps_c).then_inc(*act.did("l" + s))
                        a.wait_ge(*act.after("l" + s, i))
                        a.activation(dst, dst, ACT.Exp, scale=-0.5).then_inc(*act.did("r" + s))
                    a.wait_ge(*dve.after("min", i))
                    a.activation(eg, pair(4)[:, P:], ACT.Exp).then_inc(*act.did("eg"))
                    a.activation(es, es, ACT.Exp).then_inc(*act.did("E"))
                    a.wait_ge(*pe.after("N", i))
                    a.activation(n_, pair(4), ACT.Copy).then_inc(*act.did("N"))
                    for l in LV:
                        a.wait_ge(*pe.after(f"Z{l}", i))
                        a.activation(z_, pair(4), ACT.Copy).then_inc(*act.did(f"Z{l}"))
                        if l >= 4 and l < 6:
                            n = l - 4
                            a.wait_ge(*gate_pe.after(f"t{n}", i))
                            a.activation(gates[:, i * 2 + (first_gate + n), :], bank(1 + 2 * n), ACT.Copy).then_inc(*gate_ev.did(f"t{n}"))
                    a.wait_ge(*pe.after("nw", i))
                    a.activation(nwT, pair(4), ACT.Copy, scale=-1.0).then_inc(*act.did("nw"))
                    a.wait_ge(*pe.after("o", i))
                    a.activation(d_[:, 0:SEQ], bank(2), ACT.Square).then_inc(*act.did("oo"))
                    a.wait_ge(*pe.after("ss", i))
                    a.activation(u_[:, 0:SEQ], bank(4), ACT.Ln, bias=eps_c, scale=1.0 / P).then_inc(*act.did("ln"))
                    a.wait_ge(*act.after("ln", i))
                    a.activation(u_[:, 0:SEQ], u_[:, 0:SEQ], ACT.Exp, scale=-0.5).then_inc(*act.did("ri"))

            def vector(v):
                dve.begin(v)
                def tt(name, out_, a_, b2, op=ALU.mult):
                    v.tensor_tensor(out_, a_, b2, op).then_inc(*dve.did(name))
                v.wait_ge(*act0.after("ekd"))
                with v.Fori(0, rounds, 1) as i:
                    for n, s in enumerate("qkv"):
                        v.wait_ge(*pe.after(s, i))
                        src, c = slot(slots[s]), conv[s]
                        for j in range(4):
                            wc = rowsT[:, bass.ds(i + (R_CONV + (3 - j) * 12 + n * 4), 1)]
                            if j == 0:
                                v.tensor_scalar(c, src, wc, None, ALU.mult).then_inc(*dve.did(f"{s}0"))
                            else:
                                v.wait_ge(*dve.after(f"{s}{j - 1}", i))
                                v.scalar_tensor_tensor(c[:, j:], src[:, 0:TOK - j], wc, c[:, j:], ALU.mult, ALU.add
                                                       ).then_inc(*dve.did(f"{s}{j}"))
                    for s in "qkv":
                        v.wait_ge(*act.after(f"s{s}", i))
                        tt(f"{s}m", feat[s][:, 0:META], conv[s][:, 0:META], sig[:, 0:META])
                        tt(f"{s}r", feat[s][:, P:], conv[s][:, META:], sig[:, META:])
                    v.wait_ge(*act.after("sg", i))
                    tt("g", g_, slot(1)[:, META:], eg)
                    v.memset(arena3(qf, META, P), 0.0).then_inc(*dve.did("pad"))
                    v.wait_ge(*act.after("rq", i))
                    v.scalar_tensor_tensor(qf, qf, P ** -0.5, rr, ALU.mult, ALU.mult).then_inc(*dve.did("qn"))
                    v.wait_ge(*act.after("rk", i))
                    tt("kn", kf, kf, em)
                    v.wait_ge(*pe.after("G", i))
                    tt("dif", t5(es), t5(pair(4)), head_col(q_g, i), ALU.subtract)
                    v.wait_ge(*dve.after("dif", i))
                    v.tensor_scalar(es, es, 0.0, None, ALU.min).then_inc(*dve.did("min"))
                    v.wait_ge(*pe.after("B", i))
                    v.wait_ge(*dve.after("kn", i))
                    v.scalar_tensor_tensor(kb, pair(6), -1.0, kf, ALU.mult, ALU.mult).then_inc(*dve.did("kb"))
                    v.wait_ge(*act.after("E", i))
                    tt("Ei", t5(em), t5(es), over(inc, NTP))
                    tt("qg", qg, qf[:, P:], eg)
                    v.wait_ge(*dve.after("Ei", i))
                    tt("Es", t5(es), t5(es), over(strict, NTP))
                    v.wait_ge(*dve.after("Es", i))
                    v.wait_ge(*pe.after("KK", i))
                    tt("U", u_, pair(4), es)
                    v.wait_ge(*pe.after("QK", i))
                    tt("QK", qk, bank(6), em[:, P:])
                    v.wait_ge(*dve.after("U", i))
                    tt("Ua", t5(e_), t5(u_), over(up(0), NTP))
                    v.wait_ge(*dve.after("Ua", i))
                    tt("Ub", t5(e_), t5(e_), over(ident, NTP), ALU.add)
                    v.wait_ge(*pe.after("kT", i))
                    tt("kbg", t5(kbg), t5(pair(6)), head_col(q_bg, i))
                    tt("kd", t5(kd), t5(pair(6)), head_col(q_kd, i))
                    v.wait_ge(*pe.after("vT", i))
                    tt("vb", t5(vb), t5(pair(6)), head_col(q_beta, i))
                    v.wait_ge(*act.after("N", i))
                    tt("Da", t5(d_), t5(n_), over(low(0), NTP))
                    v.wait_ge(*dve.after("Da", i))
                    tt("Db", t5(d_), t5(d_), over(ident, NTP), ALU.add)
                    for l in LV:
                        v.wait_ge(*pe.after(f"EZ{l}", i))
                        v.tensor_copy(next_spare(), one_c)
                        v.copy_predicated(t5(e_), over(up(l).bitcast(I32), NTP), t5(pair(6))).then_inc(*dve.did(f"E{l}"))
                        if l < LEVELS - 1:
                            v.wait_ge(*pe.after(f"ZD{l}", i))
                            v.tensor_copy(next_spare(), one_c)
                            v.copy_predicated(t5(d_), over(low(l).bitcast(I32), NTP), t5(pair(4))).then_inc(*dve.did(f"D{l}"))
                    for c in range(NTP):
                        cs = slice(c * P, (c + 1) * P)
                        v.wait_ge(*pe.after(f"V{c}", i))
                        v.tensor_copy(vn[:, cs], bank(4 + c % 2, P)).then_inc(*dve.did(f"V{c}"))
                        if c < NT:
                            v.wait_ge(*pe.after(f"S{c}", i))
                            if c == 0:
                                v.tensor_copy(s_[:, cs], bank(6, P)).then_inc(*dve.did("S0"))
                            else:
                                v.wait_ge(*dve.after(f"S{c - 1}", i))
                                v.scalar_tensor_tensor(s_[:, cs], s_[:, (c - 1) * P:c * P],
                                                       q_egl[:, bass.ds(i + c * 4, 1)], bank(6 + c % 2, P),
                                                       ALU.mult, ALU.add).then_inc(*dve.did(f"S{c}"))
                    v.wait_ge(*act.after("ri", i))
                    v.scalar_tensor_tensor(es[:, 0:SEQ], bank(2), rowsT[:, R_BN:R_BN + 1], u_[:, 0:SEQ], ALU.mult, ALU.mult
                                           ).then_inc(*dve.did("y1"))
                    v.wait_ge(*dve.after("y1", i))
                    tt("y", yT[:, bass.ds(i + first_y, 1), :].rearrange("p a t -> p (a t)"), es[:, 0:SEQ], g_)

            def arena3(first, lo, hi):
                at = WORK + 8 * PADTOK
                return arena[:, at:at + 3 * PADTOK].rearrange("p (a t) -> p a t", a=3)[:, :, lo:hi]

            for e, f in (("sync", sync), ("scalar", scalar), ("vector", vector), ("tensor", tensor), ("gpsimd", gpsimd)):
                programs[e].append(f)
            return pe, act, dve, gate_pe, gate_ev

        def tail(a_steps, b_steps, c_steps):
            pe_c, act_c, dve_c, _, gate_c = c_steps
            mixers_done = [dve_c.rounds(2), gate_c.rounds(2), pe_c.rounds(2)]
            W = 4
            WBR = KD * TOK
            wbr = [arena[:, WBR + n * 12 * P:WBR + (n + 1) * 12 * P].rearrange("p (k c) -> p k c", k=12) for n in range(W)]
            wo = arena[:, ARENA - KD * D:].rearrange("p (k c) -> p k c", k=KD)
            gb = gates[:, :, :].rearrange("p (b n) t -> p b n t", b=NB)
            h = yT[:, 0:2 * NT, :].rearrange("p (i a) t -> p i (a t)", a=2)
            u2 = gates[:, 8:16, :].rearrange("p (i a) t -> p i (a t)", a=2)
            u2T = gates[:, 0:KD, :]
            wr = gates[:, 16, 0:288].rearrange("p (k c) -> p k c", k=KD)
            rb = gates[:, 16, 288:324]
            scr2 = gates[:, 18:20, :].rearrange("p a t -> p (a t)")
            nf = gates[:, 20:22, :].rearrange("p a t -> p (a t)")
            nfin = gates[:, 22:24, :].rearrange("p a t -> p (a t)")
            pe = Steps(sem("merge_pe"), [f"p{n}" for n in range(W)], 1)
            act = Steps(sem("merge_act"), [f"s{n}" for n in range(W)], 1)
            dve = Steps(sem("merge_dve"), [f"{s}{n}" for n in range(W) for s in ("m", "a", "b")], 3 * W + 1)
            pe2 = Steps(sem("router_pe"), ["o0", "o1", "o2", "o3", "T0", "o4", "o5", "T1", "o6", "o7", "T2", "T3", "lg", "rk"])
            rt = ["lb", "gm", "lt", "ge", "gd", "gx", "og", "el", "es", "m1", "e1", "q1", "x1", "o1",
                  "n2", "m2", "e2", "q2", "x2", "o2", "dm", "O1", "O2", "M", "rank", "cnt",
                  "j64", "xa", "xb", "xc", "xd", "ci", "ob", "A1", "A2", "r1", "r2", "r3", "R1", "R1s", "R2", "R2s",
                  "idx", "ja", "jb", "jc", "jd", "ji", "ni", "gs", "gv", "w1a", "w1", "w2", "c1", "c2"]
            rows_order = [step_ for i in range(NT) for step_ in ([f"h{2 * i}", f"h{2 * i + 1}", f"s{i}", f"ms{i}"] +
                                                         ([f"T{i - 1}"] if i == NT - 1 else []) + [f"u{i}"] +
                                                         ([f"T{i - 1}"] if 0 < i < NT - 1 else []))] + [f"T{NT - 1}"]
            dve2 = Steps(sem("router_dve"), rows_order + rt)
            act2 = Steps(sem("router_act"), [f"{s}{i}" for i in range(NT) for s in ("ln", "rs")] + ["eg", "e2"])
            rw = sb("rw", [P, 900])
            idx = sb("idx", [P, 2 * NT], I32)
            tile_of = sb("tile_of", [1, EXTRA + 1], I32)
            at = [0]

            def small(*shape):
                n = int(np.prod(shape))
                at[0] += n
                assert at[0] <= 900
                ap = rw[:, at[0] - n:at[0]]
                if len(shape) == 2:
                    return ap.rearrange("p (a b) -> p a b", a=shape[0])
                return ap
            ss2 = small(NT)
            lg = small(NT, NG + NX)
            c_w = [small(NT), small(NT)]

            def sync(sp):
                bv = w_branch[0].rearrange("b (k p) d -> p (b k) d", p=P)
                sp.wait_ge(*pe_c.after("v", 1))
                for n in range(W):
                    sp.dma_start(wbr[n], bv[:, :, n * P:(n + 1) * P]).then_inc(sem(f"branch_w{n}"), 16)
                for q in mixers_done:
                    sp.wait_ge(*q)
                sp.dma_start(wo, w_out[0].rearrange("(k p) d -> p k d", p=P)).then_inc(sem("out_w"), 16)
                load_weights(sp, 0, 0)
                for n in range(W):
                    sp.wait_ge(*pe.after(f"p{n}", 0))
                    sp.dma_start(wbr[n], bv[:, :, (W + n) * P:(W + n + 1) * P]).then_inc(sem(f"branch_w{n}"), 16)
                for q in (pe.rounds(KD // W), dve.rounds(KD // W)):
                    sp.wait_ge(*q)
                sp.dma_start(h, x[0].rearrange("(i p) d -> p i d", p=P)).then_inc(sem("x_again"), 16)
                sp.dma_start(nf, norm_ffn[0:1, :].broadcast_to([P, D])).then_inc(sem("tail_small"), 16)
                sp.dma_start(nfin, norm_final.unsqueeze(0).broadcast_to([P, D])).then_inc(sem("tail_small"), 16)
                sp.dma_start(wr[:, :, 0:NG], router_group_w[0].rearrange("(k p) c -> p k c", p=P)).then_inc(sem("tail_small"), 16)
                sp.dma_start(wr[:, :, NG:], router_expert_w[0].rearrange("(k p) c -> p k c", p=P)).then_inc(sem("tail_small"), 16)
                sp.dma_start(rb[:, 0:NG], router_group_b[0:1, :].broadcast_to([P, NG])).then_inc(sem("tail_small"), 16)
                sp.dma_start(rb[:, NG:], router_expert_b[0:1, :].broadcast_to([P, NX])).then_inc(sem("tail_small"), 16)

            def scalar(a):
                act.begin(a)
                a.wait_ge(*gate_c.rounds(2))
                with a.Fori(0, KD // W, 1) as i:
                    for n in range(W):
                        g = gb[:, :, bass.ds(i * W + n, 1), :].rearrange("p b a t -> p b (a t)")
                        a.activation(g, g, ACT.Sigmoid).then_inc(*act.did(f"s{n}"))
                a.preload_act_table_set("natural_log_exp_and_others")
                for i in range(NT):
                    r = ss2[:, i:i + 1]
                    a.wait_ge(*dve2.after(f"ms{i}"))
                    a.activation(r, r, ACT.Ln).then_inc(*act2.did(f"ln{i}"))
                    a.wait_ge(*act2.after(f"ln{i}"))
                    a.activation(r, r, ACT.Exp, scale=-0.5).then_inc(*act2.did(f"rs{i}"))
                a.wait_ge(*dve2.after("lt"))
                a.activation(gx, lt, ACT.Exp).then_inc(*act2.did("eg"))
                a.wait_ge(*dve2.after("dm"))
                a.activation(e2, dm, ACT.Exp).then_inc(*act2.did("e2"))

            def tensor(t):
                pe.begin(t)
                t.wait_ge(*gate_c.rounds(2))
                with t.Fori(0, KD // W, 1) as i:
                    for n in range(W):
                        t.wait_ge(sem(f"branch_w{n}"), i * 16 + 16)
                        t.wait_ge(*(dve.after(f"m{n - 2}", i) if n >= 2 else dve.after(f"m{n + W - 2}", i - 1)))
                        for b in range(NB):
                            if n == 0 and b == NB - 1:
                                t.wait_ge(*dve_c.rounds(2))
                            for k in range(4):
                                mm = t.matmul(bank(4 * (n % 2) + b), wbr[n][:, 4 * b + k, :], yT[:, 4 * b + k, :],
                                              start=(k == 0), stop=(k == 3))
                        mm.then_inc(*pe.did(f"p{n}"))
                t.wait_ge(*dve.rounds(KD // W))
                t.wait_ge(sem("out_w"), 16)

                def turn_tokens(i):
                    t.wait_ge(*dve2.after(f"u{i}"))
                    for k in range(KD):
                        mm = t.transpose(bank(2 * i + k // 4)[:, k % 4 * P:(k % 4 + 1) * P], u2[:, i, k * P:(k + 1) * P], ident)
                    mm.then_inc(*pe2.did(f"T{i}"))

                def logits(i):
                    if i == 0:
                        t.wait_ge(sem("tail_small"), 96)
                    t.wait_ge(*dve2.after(f"T{i}"))
                    for k in range(KD):
                        mm = t.matmul(bank(0)[:, i * 36:(i + 1) * 36], u2T[:, k, i * P:(i + 1) * P], wr[:, k, :],
                                      start=(k == 0), stop=(k == KD - 1))
                    return mm

                for i in range(NT):
                    for n in (2 * i, 2 * i + 1):
                        for k in range(KD):
                            mm = t.matmul(bank(n), gates[:, k, i * P:(i + 1) * P], wo[:, k, n % 2 * 512:(n % 2 + 1) * 512],
                                          start=(k == 0), stop=(k == KD - 1))
                        mm.then_inc(*pe2.did(f"o{n}"))
                    if i >= 2:
                        logits(i - 2)
                    if i >= 1:
                        turn_tokens(i - 1)
                turn_tokens(NT - 1)
                logits(NT - 2)
                logits(NT - 1).then_inc(*pe2.did("lg"))
                t.wait_ge(*dve2.after("M"))
                for i in range(NT):
                    dst = bank(3)[:, i * NX:(i + 1) * NX]
                    t.matmul(dst, strict, mm_[:, i, :], start=True, stop=(i == 0))
                    for j in range(i):
                        t.matmul(dst, ones[:, :], mm_[:, j, :], start=False, stop=(j == i - 1))
                for j in range(NT):
                    mm = t.matmul(bank(3)[:, NT * NX:(NT + 1) * NX], ones[:, :], mm_[:, j, :], start=(j == 0), stop=(j == NT - 1))
                mm.then_inc(*pe2.did("rk"))

            lt, gx, og = small(NT, NG), small(NT, NG), small(NT, NG)
            t4 = small(NT, NG)
            gm, gv, m1, m2, dm, e2, mx = (small(NT) for _ in range(7))
            el, o1, o2, t8 = small(NT, NE), small(NT, NE), small(NT, NE), small(NT, NE)
            O1, O2, mm_, rk = (gates[:, 17, n * 128:(n + 1) * 128].rearrange("p (i e) -> p i e", i=NT) for n in range(4))
            sel = gates[:, 16, 324:324 + 128].rearrange("p (i g e) -> p i g e", i=NT, g=NG)
            cnt, ci, ex, ob, aa = (small(NX) for _ in range(5))
            j64 = small(16)
            rows2 = small(NT, 2)
            ej = small(17)
            big = gates[:, 18, :].rearrange("p (e j) -> p e j", j=16)
            u2out = u2
            J = C[:, K_J:K_J + 16]
            DESC = C[:, K_DESC:K_DESC + NE]
            E64 = C[:, K_E64:K_E64 + NX]

            def vector(v):
                dve.begin(v)
                with v.Fori(0, KD // W, 1) as i:
                    for n in range(W):
                        g = gb[:, :, bass.ds(i * W + n, 1), :].rearrange("p b a t -> p b (a t)")
                        v.wait_ge(*pe.after(f"p{n}", i))
                        v.wait_ge(*act.after(f"s{n}", i))
                        v.tensor_tensor(g, ps[:, 4 * (n % 2) * 512:(4 * (n % 2) + 3) * 512].rearrange("p (b t) -> p b t", b=NB), g,
                                        ALU.mult).then_inc(*dve.did(f"m{n}"))
                        for b, s in ((1, "a"), (2, "b")):
                            v.wait_ge(*dve.after(f"m{n}" if s == "a" else f"a{n}", i))
                            v.tensor_tensor(g[:, 0, :], g[:, 0, :], g[:, b, :], ALU.add).then_inc(*dve.did(f"{s}{n}"))
                v.wait_ge(sem("x_again"), 16)

                def turned(i):
                    v.wait_ge(*pe2.after(f"T{i}"))
                    v.tensor_copy(u2T[:, :, i * P:(i + 1) * P],
                                  ps[:, 2 * i * 512:(2 * i + 2) * 512].rearrange("p (k t) -> p k t", k=KD)).then_inc(*dve2.did(f"T{i}"))
                for i in range(NT):
                    for j in range(2):
                        hs = h[:, i, j * 512:(j + 1) * 512]
                        v.wait_ge(*pe2.after(f"o{2 * i + j}"))
                        v.tensor_tensor(hs, bank(2 * i + j), hs, ALU.add).then_inc(*dve2.did(f"h{2 * i + j}"))
                    v.wait_ge(*dve2.after(f"h{2 * i + 1}"))
                    r = ss2[:, i:i + 1]
                    v.tensor_tensor_reduce(scr2, h[:, i, :], h[:, i, :], 1.0, 0.0, ALU.mult, ALU.add, accum_out=r).then_inc(*dve2.did(f"s{i}"))
                    v.wait_ge(*dve2.after(f"s{i}"))
                    v.tensor_scalar(r, r, 1.0 / D, EPS, ALU.mult, ALU.add).then_inc(*dve2.did(f"ms{i}"))
                    if i == NT - 1:
                        turned(i - 1)
                    v.wait_ge(*act2.after(f"rs{i}"))
                    if i == 0:
                        v.wait_ge(sem("tail_small"), 96)
                    v.scalar_tensor_tensor(u2[:, i, :], h[:, i, :], r, nf, ALU.mult, ALU.mult).then_inc(*dve2.did(f"u{i}"))
                    if 0 < i < NT - 1:
                        turned(i - 1)
                turned(NT - 1)

                def step(name, ins):
                    ins.then_inc(*dve2.did(name))
                    v.wait_ge(*dve2.after(name))

                def tt(name, out_, a_, b_, op):
                    step(name, v.tensor_tensor(out_, a_, b_, op))

                def ts(name, out_, a_, s1, op0, s2=None, op1=None):
                    step(name, v.tensor_scalar(out_, a_, s1, s2, op0, op1) if op1 else v.tensor_scalar(out_, a_, s1, None, op0))

                def red(name, out_, a_, op):
                    step(name, v.tensor_reduce(out_, a_, axis=AX.X, op=op))

                def wide(ap, n):
                    return ap.unsqueeze(2).broadcast_to([P, NT, n])
                v.wait_ge(*pe2.after("lg"))
                tt("lb", lg, bank(0, NT * 36).rearrange("p (i c) -> p i c", i=NT), over(rb, NT), ALU.add)
                g4, g32 = lg[:, :, 0:NG], lg[:, :, NG:].rearrange("p i (g e) -> p i g e", g=NG)
                red("gm", gm, g4, ALU.max)
                tt("lt", lt, g4, wide(gm, NG), ALU.subtract)
                ts("ge", t4, lt, 0.0, ALU.is_ge)
                tt("gd", t4, t4, over(DESC[:, 0:NG], NT), ALU.mult)
                red("gx", mx, t4, ALU.max)
                tt("og", og, t4, wide(mx, NG), ALU.is_equal)
                tt("el", sel, g32, og.unsqueeze(3).broadcast_to([P, NT, NG, NE]), ALU.mult)
                red("es", el, sel.rearrange("p i g e -> p i e g"), ALU.add)
                for n, o_, m_ in (("1", o1, m1), ("2", o2, m2)):
                    if n == "2":
                        step("n2", v.scalar_tensor_tensor(el, o1, -1e30, el, ALU.mult, ALU.add))
                    red("m" + n, m_, el, ALU.max)
                    tt("e" + n, t8, el, wide(m_, NE), ALU.is_ge)
                    tt("q" + n, t8, t8, over(DESC, NT), ALU.mult)
                    red("x" + n, mx, t8, ALU.max)
                    tt("o" + n, o_, t8, wide(mx, NE), ALU.is_equal)
                tt("dm", dm, m2, m1, ALU.subtract)
                for n, o_, O_ in (("1", o1, O1), ("2", o2, O2)):
                    tt("O" + n, O_.rearrange("p i (g e) -> p i g e", g=NG), og.unsqueeze(3).broadcast_to([P, NT, NG, NE]),
                       o_.unsqueeze(2).broadcast_to([P, NT, NG, NE]), ALU.mult)
                tt("M", mm_, O1, O2, ALU.add)
                v.wait_ge(*pe2.after("rk"))
                step("rank", v.tensor_copy(rk, bank(3, NT * NX).rearrange("p (i e) -> p i e", i=NT)))
                step("cnt", v.tensor_copy(cnt, bank(3)[:, NT * NX:(NT + 1) * NX]))
                ts("j64", j64, J, float(SLOTS), ALU.mult)
                tt("xa", big, cnt.unsqueeze(2).broadcast_to([P, NX, 16]), over(j64, NX), ALU.subtract)
                ts("xb", big, big, 0.0, ALU.is_gt)
                red("xc", ex, big, ALU.add)
                ts("xd", ex, ex, 1.0, ALU.max, -1.0, ALU.add)
                step("ci", v.tensor_tensor_scan(ci, ones[:, 0:NX], ex, 0.0, ALU.mult, ALU.add))
                tt("ob", ob, ci, ex, ALU.subtract)
                ts("A1", aa, ob, float(SLOTS), ALU.mult, float((NX - 1) * SLOTS), ALU.add)
                tt("A2", aa, aa, E64, ALU.subtract)
                ts("r1", sel.rearrange("p i g e -> p i (g e)"), rk, float(SLOTS), ALU.is_ge)
                selr = sel.rearrange("p i g e -> p i (g e)")
                tt("r2", selr, selr, over(aa, NT), ALU.mult)
                tt("r3", rk, rk, over(E64, NT), ALU.add)
                tt("R1", rk, rk, selr, ALU.add)
                tt("R1s", O1, O1, rk, ALU.mult)
                tt("R2", O2, O2, rk, ALU.mult)
                red("R2s", rows2[:, :, 0], O1, ALU.add)
                red("idx", rows2[:, :, 1], O2, ALU.add)
                step("ja", v.tensor_copy(idx[:, :], rows2.rearrange("p i k -> p (i k)")))
                tt("jb", big, J.unsqueeze(1).broadcast_to([P, NX, 16]), ci.unsqueeze(2).broadcast_to([P, NX, 16]), ALU.is_ge)
                red("jc", ej[:, 0:16], big.rearrange("p e j -> p j e"), ALU.add)
                ts("jd", ej[:, 0:16], ej[:, 0:16], float(NX - 1), ALU.min)
                step("ji", v.tensor_copy(tile_of[:, 0:16], ej[0:1, 0:16]))
                step("ni", v.tensor_copy(tile_of[:, 16:17], ci[0:1, NX - 1:NX]))
                v.wait_ge(*act2.after("eg"))
                red("gs", gv, gx, ALU.add)
                step("gv", v.reciprocal(gv, gv))
                v.wait_ge(*act2.after("e2"))
                ts("w1a", m1, e2, 1.0, ALU.add)
                step("w1", v.reciprocal(m1, m1))
                tt("w2", m2, e2, m1, ALU.mult)
                tt("c1", c_w[0], m1, gv, ALU.mult)
                tt("c2", c_w[1], m2, gv, ALU.mult)

            def gpsimd(g):
                g.wait_ge(*dve2.after("ja"))
                g.wait_ge(sem("rows_zeroed"), 16 * n_zero)
                for i in range(NT):
                    for k in range(2):
                        g.indirect_dma_start(out=xs_dram, out_offset=bass.IndirectOffsetOnAxis(ap=idx[:, 2 * i + k:2 * i + k + 1], axis=0),
                                             in_=u2[:, i, :], in_offset=None).then_inc(sem("scattered"), 16)

            for e, f in (("sync", sync), ("scalar", scalar), ("vector", vector), ("tensor", tensor), ("gpsimd", gpsimd)):
                programs[e].append(f)

            xr = [gates[0:SLOTS, 2 * n:2 * n + 2, :].rearrange("p a t -> p (a t)") for n in range(4)]
            yr = [gates[0:SLOTS, 8 + 2 * n:10 + 2 * n, :].rearrange("p a t -> p (a t)") for n in range(2)]
            xT = [gates[:, 12 + n, :].rearrange("p (k t) -> p k t", k=KD) for n in range(2)]
            hd = [gates[:, 14 + n, 0:256] for n in range(2)]
            wgv = expert_w_gate[0].rearrange("g e (p k) h -> (g e) p (k h)", p=P)
            wuv = expert_w_up[0].rearrange("g e (p k) h -> (g e) p (k h)", p=P)
            wdv = expert_w_down[0].rearrange("g e (p k) h -> (g e) p (k h)", p=P)
            U = 4
            LOOPED = NX // U - 1
            WX = 3 * 2 * D
            ring4 = [arena[:, at:at + WX] for at in (ARENA - KD * D - WX, 0, WX, ARENA - KD * D)]

            class Each:

                def __init__(self, name):
                    self.sem = sem(name)

                def begin(self, engine):
                    engine.nop().then_inc(self.sem, 1)

                def of(self, e):
                    return self.sem, e + 2

            rows_turned, x_read, gate_made, up_made, made = (Each(f"expert_{n}") for n in ("turned", "x_read", "gate", "up", "out"))
            sig_made, act_hidden, hidden_made, left_read, right_read = (
                Each(f"expert_{n}") for n in ("sigmoid", "gated", "hidden", "left_read", "right_read"))

            def parts(n):
                r = ring4[n]
                return (r[:, 0:2048].rearrange("p (k h) -> p k h", k=KD), r[:, 2048:4096].rearrange("p (k h) -> p k h", k=KD),
                        r[:, 4096:6144].rearrange("p (j d) -> p j d", j=2))

            def load_weights(sp, n, e):
                one = (lambda vw: vw[e]) if isinstance(e, int) else (lambda vw: vw[bass.ds(e, 1)].rearrange("a p m -> p (a m)"))
                for vw, lo in ((wgv, 0), (wuv, 2048), (wdv, 4096)):
                    sp.dma_start(ring4[n][:, lo:lo + 2048], one(vw)).then_inc(sem(f"expert_w{n}"), 16)

            def load_rows(sp, n, e):
                sp.dma_start(xr[n], xs_dram[e * SLOTS:(e + 1) * SLOTS, :] if isinstance(e, int)
                             else xs_dram[bass.ds(e * SLOTS, SLOTS), :]).then_inc(sem(f"expert_x{n}"), 16)

            def esync(sp):
                for n in (1, 2):
                    load_weights(sp, n, n)
                sp.wait_ge(*pe2.after("o7"))
                load_weights(sp, 3, 3)
                sp.wait_ge(sem("scattered"), 16 * 2 * NT)
                sp.wait_ge(*pe2.after("lg"))
                for n in range(U):
                    load_rows(sp, n, n)
                with sp.Fori(0, LOOPED, 1) as i:
                    for n in range(U):
                        sp.wait_ge(*rows_turned.of(i * U + n))
                        load_rows(sp, n, i * U + (n + U))
                        sp.wait_ge(*made.of(i * U + n))
                        load_weights(sp, n, i * U + (n + U))

            def turn_rows(t, e, n, i, xw):
                t.wait_ge(*xw)
                if not (isinstance(e, int) and e < 2):
                    t.wait_ge(*x_read.of(e - 2))
                for k in range(KD):
                    dst, rows = bank(n % 2)[:, k * SLOTS:(k + 1) * SLOTS], xr[n][:, k::KD]
                    if k == 0:
                        t.matmul(dst, rows, ident[0:SLOTS, 0:SLOTS], start=True, stop=True)
                    else:
                        mm = t.transpose(dst, rows, ident[0:SLOTS, 0:SLOTS])
                return mm

            def up_products(t, n, which):
                wm, b = parts(n)[which], (2, 4)[which]
                for j in range(2):
                    for k in range(KD):
                        mm = t.matmul(bank(b + n % 2)[:, j * SLOTS:(j + 1) * SLOTS], wm[:, k, j::2], xT[n % 2][:, k, :],
                                      start=(k == 0), stop=(k == KD - 1))
                return mm

            def down_products(t, n):
                wd = parts(n)[2]
                for half in range(2):
                    for j in range(2):
                        mm = t.matmul(bank(6 + half)[0:SLOTS, :], hd[n % 2][:, j * SLOTS:(j + 1) * SLOTS],
                                      wd[:, j, half * 512:(half + 1) * 512], start=(j == 0), stop=(j == 1))
                return mm

            def etensor(t):
                for q in (rows_turned, gate_made, up_made, made):
                    q.begin(t)

                def turn(e, n, i):
                    turn_rows(t, e, n, i, (sem(f"expert_x{n}"), i * 16 + 16)).then_inc(rows_turned.sem, 1)

                def up(e, n, i):
                    t.wait_ge(sem(f"expert_w{n}"), i * 48 + 48)
                    t.wait_ge(*x_read.of(e))
                    up_products(t, n, 0).then_inc(gate_made.sem, 1)
                    up_products(t, n, 1).then_inc(up_made.sem, 1)

                def down(e, n, first=False):
                    t.wait_ge(*hidden_made.of(e))
                    if not first:
                        t.wait_ge(*left_read.of(e - 1))
                        t.wait_ge(*right_read.of(e - 1))
                    down_products(t, n).then_inc(made.sem, 1)

                turn(0, 0, 0)
                turn(1, 1, 0)
                up(0, 0, 0)
                with t.Fori(0, LOOPED, 1) as i:
                    for m in range(U):
                        e, n, n2 = i * U + (m + 1), (m + 1) % U, (m + 2) % U
                        turn(e + 1, n2, i + (m + 2) // U)
                        up(e, n, i + (m + 1) // U)
                        down(e - 1, m)
                for e in range(LOOPED * U + 1, NX):
                    if e + 1 < NX:
                        turn(e + 1, (e + 1) % U, (e + 1) // U)
                    up(e, e % U, e // U)
                    down(e - 1, (e - 1) % U)
                down(NX - 1, (NX - 1) % U)

            def escalar(a):
                for q in (sig_made, left_read):
                    q.begin(a)
                for n in range(2):
                    a.nop().then_inc(sem(f"expert_stored{n}"), 1)

                def sigmoid(e, n, first=False):
                    a.wait_ge(*gate_made.of(e))
                    if not first:
                        a.wait_ge(*hidden_made.of(e - 2))
                    a.activation(hd[n % 2][:, 128:256], bank(2 + n % 2, 2 * SLOTS), ACT.Sigmoid).then_inc(sig_made.sem, 1)

                def result(e, n, turns, row):
                    a.wait_ge(*made.of(e))
                    a.wait_ge(sem(f"expert_stored{n % 2}"), turns * 16 + 1)
                    a.activation(yr[n % 2][:, 0:512], bank(6)[0:SLOTS, :], ACT.Copy).then_inc(left_read.sem, 1)
                    a.wait_ge(*left_read.of(e))
                    a.wait_ge(*right_read.of(e))
                    a.dma_start(ys_dram[bass.ds(row, SLOTS), :] if not isinstance(row, int) else ys_dram[row:row + SLOTS, :],
                                yr[n % 2]).then_inc(sem(f"expert_stored{n % 2}"), 16)

                sigmoid(0, 0, True)
                sigmoid(1, 1, True)
                with a.Fori(0, LOOPED, 1) as i:
                    for m in range(U):
                        e = i * U + m
                        result(e, m, i * 2 + m // 2, i * (U * SLOTS) + m * SLOTS)
                        sigmoid(e + 2, m)
                for e in range(LOOPED * U, NX):
                    result(e, e % U, e // 2, e * SLOTS)
                    if e + 2 < NX:
                        sigmoid(e + 2, e % 2)

            def evector(v):
                for q in (x_read, act_hidden, hidden_made, right_read):
                    q.begin(v)
                v.wait_ge(sem("scattered"), 16 * 2 * NT)

                def read_rows(e, n):
                    v.wait_ge(*rows_turned.of(e))
                    if not (isinstance(e, int) and e < 2):
                        v.wait_ge(*up_made.of(e - 2))
                    v.tensor_copy(xT[n % 2], bank(n % 2).rearrange("p (k t) -> p k t", k=KD)).then_inc(x_read.sem, 1)

                def hidden(e, n):
                    v.wait_ge(*sig_made.of(e))
                    v.tensor_tensor(hd[n % 2][:, 128:256], hd[n % 2][:, 128:256], bank(2 + n % 2, 2 * SLOTS), ALU.mult
                                    ).then_inc(act_hidden.sem, 1)
                    v.wait_ge(*act_hidden.of(e))
                    v.wait_ge(*up_made.of(e))
                    if not (isinstance(e, int) and e < 2):
                        v.wait_ge(*made.of(e - 2))
                    v.tensor_tensor(hd[n % 2][:, 0:128], hd[n % 2][:, 128:256], bank(4 + n % 2, 2 * SLOTS), ALU.mult
                                    ).then_inc(hidden_made.sem, 1)

                def result(e, n, turns):
                    v.wait_ge(*made.of(e))
                    v.wait_ge(sem(f"expert_stored{n % 2}"), turns * 16 + 1)
                    v.tensor_copy(yr[n % 2][:, 512:], bank(7)[0:SLOTS, :]).then_inc(right_read.sem, 1)

                read_rows(0, 0)
                read_rows(1, 1)
                hidden(0, 0)
                with v.Fori(0, LOOPED, 1) as i:
                    for m in range(U):
                        e = i * U + (m + 1)
                        read_rows(e + 1, m)
                        hidden(e, m + 1)
                        result(e - 1, m, i * 2 + m // 2)
                for e in range(LOOPED * U + 1, NX):
                    if e + 1 < NX:
                        read_rows(e + 1, e + 1)
                    hidden(e, e)
                    result(e - 1, e - 1, (e - 1) // 2)
                result(NX - 1, NX - 1, (NX - 1) // 2)

            for e, f in (("sync", esync), ("scalar", escalar), ("vector", evector), ("tensor", etensor)):
                programs[e].append(f)

            ope = Steps(sem("extra_pe"), ["T0", "g0", "u0", "y0"], 1)
            oact = Steps(sem("extra_act"), ["s0", "y0"], 1)
            odve = Steps(sem("extra_dve"), ["T0", "a0", "h0", "y0"], 1)

            def extra(eng, body):
                eng.wait_ge(*dve2.after("ni"))
                count = eng.value_load(tile_of[0:1, EXTRA:EXTRA + 1], min_val=0, max_val=EXTRA)
                with eng.If(count > 0):
                    with eng.Fori(0, EXTRA, 1) as j:
                        with eng.If(count > j):
                            body(j)
                return count

            def osync(sp):
                sp.wait_ge(*made.of(NX - 1))
                sp.wait_ge(sem("expert_stored0"), 16 * NX // 2 + 1)
                sp.wait_ge(sem("expert_stored1"), 16 * NX // 2 + 1)

                def body(j):
                    sp.wait_ge(sem("extra_stored"), j * 16 + 1)
                    e = sp.value_load(tile_of[0:1, bass.ds(j, 1)], min_val=0, max_val=NX - 1)
                    sp.dma_start(xr[0], xs_dram[bass.ds(j * SLOTS + NX * SLOTS, SLOTS), :]).then_inc(sem("extra_x"), 16)
                    for vw, lo in ((wgv, 0), (wuv, 2048), (wdv, 4096)):
                        sp.dma_start(ring4[0][:, lo:lo + 2048], vw[bass.ds(e, 1)].rearrange("a p m -> p (a m)")).then_inc(sem("extra_w"), 16)
                count = extra(sp, body)
                sp.wait_ge(sem("extra_stored"), count * 16 + 1)
                sp.nop().then_inc(sem("results_stored"), 1)

            def otensor(t):
                ope.begin(t)
                def body(j):
                    t.wait_ge(*oact.rounds(j))
                    t.wait_ge(*odve.rounds(j))
                    t.wait_ge(*left_read.of(NX - 1))
                    t.wait_ge(*right_read.of(NX - 1))
                    turn_rows(t, 0, 0, j, (sem("extra_x"), j * 16 + 16)).then_inc(*ope.did("T0"))
                    t.wait_ge(sem("extra_w"), j * 48 + 48)
                    t.wait_ge(*odve.after("T0", j))
                    up_products(t, 0, 0).then_inc(*ope.did("g0"))
                    up_products(t, 0, 1).then_inc(*ope.did("u0"))
                    t.wait_ge(*odve.after("h0", j))
                    down_products(t, 0).then_inc(*ope.did("y0"))
                extra(t, body)

            def oscalar(a):
                oact.begin(a)
                a.nop().then_inc(sem("extra_stored"), 1)
                def body(j):
                    a.wait_ge(sem("extra_x"), j * 16 + 16)
                    a.wait_ge(*ope.after("g0", j))
                    a.activation(hd[0][:, 128:256], bank(2, 2 * SLOTS), ACT.Sigmoid).then_inc(*oact.did("s0"))
                    a.wait_ge(*ope.after("y0", j))
                    a.activation(yr[0][:, 0:512], bank(6)[0:SLOTS, :], ACT.Copy).then_inc(*oact.did("y0"))
                    a.wait_ge(*oact.after("y0", j))
                    a.wait_ge(*odve.after("y0", j))
                    a.dma_start(ys_dram[bass.ds(j * SLOTS + NX * SLOTS, SLOTS), :], yr[0]).then_inc(sem("extra_stored"), 16)
                extra(a, body)

            def ovector(v):
                odve.begin(v)
                def body(j):
                    v.wait_ge(sem("extra_x"), j * 16 + 16)
                    v.wait_ge(*ope.after("T0", j))
                    v.tensor_copy(xT[0], bank(0).rearrange("p (k t) -> p k t", k=KD)).then_inc(*odve.did("T0"))
                    v.wait_ge(*oact.after("s0", j))
                    v.tensor_tensor(hd[0][:, 128:256], hd[0][:, 128:256], bank(2, 2 * SLOTS), ALU.mult).then_inc(*odve.did("a0"))
                    v.wait_ge(*odve.after("a0", j))
                    v.wait_ge(*ope.after("u0", j))
                    v.tensor_tensor(hd[0][:, 0:128], hd[0][:, 128:256], bank(4, 2 * SLOTS), ALU.mult).then_inc(*odve.did("h0"))
                    v.wait_ge(*ope.after("y0", j))
                    v.tensor_copy(yr[0][:, 512:], bank(7)[0:SLOTS, :]).then_inc(*odve.did("y0"))
                extra(v, body)

            for e, f in (("sync", osync), ("scalar", oscalar), ("vector", ovector), ("tensor", otensor)):
                programs[e].append(f)

            yg = [arena[:, n * D:(n + 1) * D] for n in range(2 * NT)]
            fdve = Steps(sem("final_dve"), ["a0", "b0", "a1", "b1", "o0", "a2", "b2", "o1", "a3", "b3", "o2", "o3"])
            fact = Steps(sem("final_act"), [f"{s}{i}" for i in range(NT) for s in ("s", "ln", "rs")])

            def fgpsimd(g):
                g.wait_ge(sem("results_stored"), 1)
                for i in range(NT):
                    for k in range(2):
                        g.indirect_dma_start(out=yg[2 * i + k], out_offset=None, in_=ys_dram,
                                             in_offset=bass.IndirectOffsetOnAxis(ap=idx[:, 2 * i + k:2 * i + k + 1], axis=0)
                                             ).then_inc(sem(f"gathered{i}"), 16)

            def fvector(v):
                def normed(i):
                    v.wait_ge(*fact.after(f"rs{i}"))
                    v.scalar_tensor_tensor(h[:, i, :], h[:, i, :], ss2[:, i:i + 1], nfin, ALU.mult, ALU.mult).then_inc(*fdve.did(f"o{i}"))

                for i in range(NT):
                    v.wait_ge(sem(f"gathered{i}"), 32)
                    for k, s in ((0, "a"), (1, "b")):
                        if k:
                            v.wait_ge(*fdve.after(f"a{i}"))
                        v.scalar_tensor_tensor(h[:, i, :], yg[2 * i + k], c_w[k][:, i:i + 1], h[:, i, :], ALU.mult, ALU.add
                                               ).then_inc(*fdve.did(f"{s}{i}"))
                    if i:
                        normed(i - 1)
                normed(NT - 1)

            def fscalar(a):
                a.preload_act_table_set("natural_log_exp_and_others")
                for i in range(NT):
                    r = ss2[:, i:i + 1]
                    a.wait_ge(*fdve.after(f"b{i}"))
                    if i:
                        a.wait_ge(*fact.after(f"s{i - 1}"))
                    a.activation(scr2, h[:, i, :], ACT.Square, accum_out=r).then_inc(*fact.did(f"s{i}"))
                    a.wait_ge(*fact.after(f"s{i}"))
                    a.activation(r, r, ACT.Ln, bias=eps_c, scale=1.0 / D).then_inc(*fact.did(f"ln{i}"))
                    a.wait_ge(*fact.after(f"ln{i}"))
                    a.activation(r, r, ACT.Exp, scale=-0.5).then_inc(*fact.did(f"rs{i}"))

            def fsync(sp):
                ov = out[0].rearrange("(i p) d -> p i d", p=P)
                for i in range(NT):
                    sp.wait_ge(*fdve.after(f"o{i}"))
                    sp.dma_start(ov[:, i, :], h[:, i, :]).then_inc(sem("stored"), 16)
                sp.wait_ge(sem("stored"), 16 * NT)

            for e, f in (("sync", fsync), ("scalar", fscalar), ("vector", fvector), ("gpsimd", fgpsimd)):
                programs[e].append(f)

        gla_a = gla("a", 4, 0, 0, [])
        decays(gla_a[2].rounds(4))
        delta_b = delta(4, 4, 8, [gla_a[2].rounds(4), gla_a[4].rounds(4)])
        gla_c = gla("c", 2, 8, 16, [delta_b[2].rounds(4), delta_b[4].rounds(4)])
        tail(gla_a, delta_b, gla_c)

        @block.sync
        def _(e):
            for f in programs["sync"]:
                f(e)

        @block.scalar
        def _(e):
            for f in programs["scalar"]:
                f(e)

        @block.vector
        def _(e):
            for f in programs["vector"]:
                f(e)

        @block.tensor
        def _(e):
            for f in programs["tensor"]:
                f(e)

        @block.gpsimd
        def _(e):
            for f in programs["gpsimd"]:
                f(e)


_INS = ["x", "meta_tokens", "norm_mix", "w_in", "hgrn_lb_logits", "hgrn_norm", "gdn_conv", "gdn_a_log",
        "gdn_dt_bias", "gdn_norm", "gla_gk_w2", "gla_gk_b", "gla_norm", "w_branch", "w_out", "norm_ffn",
        "router_group_w", "router_group_b", "router_expert_w", "router_expert_b",
        "expert_w_gate", "expert_w_up", "expert_w_down", "norm_final"]


def kernel(**inputs):
    import concourse.bacc as bacc
    from concourse.bass_utils import run_bass_kernel_spmd

    nc = bacc.Bacc("TRN2", target_bir_lowering=False, num_devices=1)
    arrays = {f"in_{n}": np.ascontiguousarray(inputs[n]) for n in _INS}
    arrays["in_consts"] = constants()
    args = [nc.dram_tensor(n, a.shape, mybir.dt.from_np(a.dtype), kind="ExternalInput").ap() for n, a in arrays.items()]
    args.append(nc.dram_tensor("out", (1, SEQ, D), F32, kind="ExternalOutput").ap())
    hybrid_trunk(nc, *args)
    got = run_bass_kernel_spmd(nc, [arrays], core_ids=[0])
    return got.results[0]["out"]
```
